# Optimizing a Trainium2 kernel written in Bass

```python
import math
import jax, jax.numpy as jnp
from jax import lax
import numpy as np

D_MODEL = 1024
BATCH = 1
SEQ = 256
DEPTH = 2

N_MIXERS = 2
D_FF = 4 * D_MODEL
RMS_EPS = 1e-6
NEG_INF = -1e30

GDN_HEADS = D_MODEL // 128
GDN_DK = 128
GDN_DV = 128
GDN_CONV = 5
GDN_CHUNK = 64
GDN_QKV = GDN_HEADS * (2 * GDN_DK + GDN_DV)
GDN_IN = GDN_QKV + GDN_HEADS * GDN_DV + 4 * GDN_HEADS

DSWA_CONFIGS = ((128, 1), (512, 4), (2048, 16))
DSWA_HEADS_PER_GROUP = 6
DSWA_HEAD_DIM = 64
DSWA_HEADS = len(DSWA_CONFIGS) * DSWA_HEADS_PER_GROUP
DSWA_WIDTH = DSWA_HEADS * DSWA_HEAD_DIM

REL_BUCKETS = 32
REL_MAX_DIST = 1024

N_LAYERS_A = (DEPTH + 1) // 2
N_LAYERS_B = DEPTH // 2


def rmsnorm(x, g):
    xf = x.astype(jnp.float32)
    y = xf * lax.rsqrt(jnp.mean(xf * xf, axis=-1, keepdims=True) + RMS_EPS)
    return (y * g.astype(jnp.float32)).astype(x.dtype)

def l2norm(t):
    return t * lax.rsqrt(jnp.sum(t * t, axis=-1, keepdims=True) + 1e-6)

def rel_bucket(rel):
    nb = REL_BUCKETS // 2
    max_exact = nb // 2
    ret = jnp.where(rel > 0, nb, 0)
    n = jnp.abs(rel)
    nf = jnp.maximum(n, 1).astype(jnp.float32)
    large = max_exact + (jnp.log(nf / max_exact) / math.log(REL_MAX_DIST / max_exact)
                         * (nb - max_exact)).astype(jnp.int32)
    large = jnp.minimum(large, nb - 1)
    return ret + jnp.where(n < max_exact, n, large)

def gated_delta_chunked(q, k, v, g, beta):
    B, H, S, DK = q.shape
    DV = v.shape[-1]
    C = GDN_CHUNK
    nc = S // C
    q = q.reshape(B, H, nc, C, DK)
    k = k.reshape(B, H, nc, C, DK)
    v = v.reshape(B, H, nc, C, DV)
    g = g.reshape(B, H, nc, C)
    beta = beta.reshape(B, H, nc, C)
    G = jnp.cumsum(g, axis=-1)
    incl = jnp.tril(jnp.ones((C, C), bool))
    strict = jnp.tril(jnp.ones((C, C), bool), -1)
    diff = jnp.where(incl, G[..., :, None] - G[..., None, :], 0.0)
    decay = jnp.where(incl, jnp.exp(diff), 0.0)
    kb = k * beta[..., None]
    a = jnp.where(strict, jnp.einsum('bhnid,bhnjd->bhnij', kb, k) * decay, 0.0)
    rhs = jnp.concatenate([v * beta[..., None], kb * jnp.exp(G)[..., None]], axis=-1)
    sol = lax.linalg.triangular_solve(a, rhs, left_side=True, lower=True, unit_diagonal=True)
    u, w = sol[..., :DV], sol[..., DV:]
    intra = jnp.einsum('bhnid,bhnjd->bhnij', q, k) * decay
    g_last = G[..., -1]
    q_dec = q * jnp.exp(G)[..., None]
    k_dec = k * jnp.exp(g_last[..., None] - G)[..., None]
    xs = tuple(jnp.moveaxis(t, 2, 0) for t in (u, w, intra, q_dec, k_dec, g_last))

    def step(state, inp):
        u_c, w_c, intra_c, qd_c, kd_c, gl_c = inp
        v_new = u_c - jnp.einsum('bhck,bhkv->bhcv', w_c, state)
        o_c = (jnp.einsum('bhck,bhkv->bhcv', qd_c, state)
               + jnp.einsum('bhij,bhjv->bhiv', intra_c, v_new))
        state = (state * jnp.exp(gl_c)[..., None, None]
                 + jnp.einsum('bhck,bhcv->bhkv', kd_c, v_new))
        return state, o_c

    s0 = jnp.zeros((B, H, DK, DV), jnp.float32)
    _, o = lax.scan(step, s0, xs)
    return jnp.moveaxis(o, 0, 2).reshape(B, H, S, DV)

def gated_deltanet_bidir(h, w_in, conv_w, a_log, dt_bias, norm_w, w_out):
    B, S, _ = h.shape
    H, DK, DV = GDN_HEADS, GDN_DK, GDN_DV
    f32 = jnp.float32
    proj = h @ w_in
    qkv = proj[..., :GDN_QKV]
    z = proj[..., GDN_QKV:GDN_QKV + H * DV].reshape(B, S, H, DV)
    ab = proj[..., GDN_QKV + H * DV:]
    pad = GDN_CONV // 2
    qkv = jax.nn.silu(lax.conv_general_dilated(
        qkv, conv_w, window_strides=(1,), padding=[(pad, pad)],
        dimension_numbers=('NWC', 'WIO', 'NWC'), feature_group_count=GDN_QKV))
    qkv = qkv.astype(f32)
    q = qkv[..., :H * DK].reshape(B, S, H, DK)
    k = qkv[..., H * DK:2 * H * DK].reshape(B, S, H, DK)
    v = qkv[..., 2 * H * DK:].reshape(B, S, H, DV)
    q = l2norm(q) * (DK ** -0.5)
    k = l2norm(k)
    a = ab[..., :2 * H].reshape(B, S, 2, H).astype(f32)
    b = ab[..., 2 * H:].reshape(B, S, 2, H).astype(f32)
    g = -jnp.exp(a_log.astype(f32)) * jax.nn.softplus(a + dt_bias.astype(f32))
    beta = jax.nn.sigmoid(b)
    qh, kh, vh = (jnp.transpose(t, (0, 2, 1, 3)) for t in (q, k, v))
    gh = jnp.transpose(g, (2, 0, 3, 1))
    bh = jnp.transpose(beta, (2, 0, 3, 1))
    o_fwd = gated_delta_chunked(qh, kh, vh, gh[0], bh[0])
    flip = lambda t: jnp.flip(t, axis=2)
    o_bwd = flip(gated_delta_chunked(flip(qh), flip(kh), flip(vh), flip(gh[1]), flip(bh[1])))
    o = jnp.transpose(o_fwd + o_bwd, (0, 2, 1, 3))
    o = o * lax.rsqrt(jnp.mean(o * o, axis=-1, keepdims=True) + RMS_EPS)
    o = o * norm_w.astype(f32) * jax.nn.silu(z.astype(f32))
    return o.reshape(B, S, H * DV).astype(h.dtype) @ w_out

def banded_attention(q, k, v, bias, half):
    N, L, H, E = q.shape
    blk = half
    nb = -(-L // blk)
    lp = nb * blk
    qb = jnp.pad(q, ((0, 0), (0, lp - L), (0, 0), (0, 0))).reshape(N, nb, blk, H, E)

    def windows(t):
        tb = jnp.pad(t, ((0, 0), (blk, lp - L + blk), (0, 0), (0, 0))).reshape(N, nb + 2, blk, H, E)
        return jnp.concatenate([tb[:, :-2], tb[:, 1:-1], tb[:, 2:]], axis=2)

    kw, vw = windows(k), windows(v)
    s = jnp.einsum('nbqhe,nbkhe->nbhqk', qb, kw).astype(jnp.float32) * (E ** -0.5)
    s = s + bias[None, None]
    q_idx = jnp.arange(lp).reshape(nb, blk)
    k_idx = jnp.arange(nb)[:, None] * blk - blk + jnp.arange(3 * blk)[None, :]
    off = k_idx[:, None, :] - q_idx[:, :, None]
    valid = (jnp.abs(off) <= half) & (k_idx[:, None, :] >= 0) & (k_idx[:, None, :] < L)
    s = jnp.where(valid[None, :, None], s, NEG_INF)
    m = jnp.max(s, axis=-1, keepdims=True)
    lse = m + jnp.log(jnp.sum(jnp.exp(s - m), axis=-1, keepdims=True))
    p = jnp.exp(s - lse)
    o = jnp.einsum('nbhqk,nbkhe->nbqhe', p.astype(v.dtype), vw).reshape(N, lp, H, E)[:, :L]
    lse = jnp.transpose(lse[..., 0], (0, 1, 3, 2)).reshape(N, lp, H)[:, :L]
    return o, lse

def to_sub(t, d):
    B, S, Hh, E = t.shape
    return jnp.swapaxes(t.reshape(B, S // d, d, Hh, E), 1, 2).reshape(B * d, S // d, Hh, E)

def from_sub(t, d, B):
    L = t.shape[1]
    rest = t.shape[2:]
    return jnp.swapaxes(t.reshape(B, d, L, *rest), 1, 2).reshape(B, L * d, *rest)

def dilated_window_attention(h, w_in, w_out, rel_table):
    B, S, _ = h.shape
    Hg, E = DSWA_HEADS_PER_GROUP, DSWA_HEAD_DIM
    qkv = (h @ w_in).reshape(B, S, 3, DSWA_HEADS, E)
    q, k, v = qkv[:, :, 0], qkv[:, :, 1], qkv[:, :, 2]
    outs, lses = [], []
    for gi, (window, dil) in enumerate(DSWA_CONFIGS):
        half = window // (2 * dil)
        hs = slice(gi * Hg, (gi + 1) * Hg)
        rel = (jnp.arange(3 * half)[None, :] - half - jnp.arange(half)[:, None]) * dil
        bias = jnp.take(rel_table, rel_bucket(rel), axis=0)[..., hs]
        bias = jnp.transpose(bias, (2, 0, 1)).astype(jnp.float32)
        o, lse = banded_attention(to_sub(q[:, :, hs], dil), to_sub(k[:, :, hs], dil),
                                  to_sub(v[:, :, hs], dil), bias, half)
        outs.append(from_sub(o, dil, B))
        lses.append(from_sub(lse, dil, B))
    o = jnp.stack(outs, axis=2)
    alpha = jax.nn.softmax(jnp.stack(lses, axis=2), axis=2)
    o = (o * alpha[..., None].astype(o.dtype)).reshape(B, S, DSWA_WIDTH)
    return o @ w_out

def squared_relu_mlp(h, w1, w2):
    return jnp.square(jax.nn.relu(h @ w1)) @ w2

def first_inputs(seed: int = 0) -> dict:
    key = jax.random.key(seed)
    ks = jax.random.split(key, 16)
    f32 = jnp.float32
    nrm = lambda kk, shape, scale: jax.random.normal(kk, shape, f32) * scale
    x = nrm(ks[0], (BATCH, SEQ, D_MODEL), 1.0)
    norm_mix = 1.0 + nrm(ks[1], (DEPTH, D_MODEL), 0.02)
    norm_mlp = 1.0 + nrm(ks[2], (DEPTH, D_MODEL), 0.02)
    norm_final = 1.0 + nrm(ks[3], (D_MODEL,), 0.02)
    rel_bias = nrm(ks[4], (REL_BUCKETS, DSWA_HEADS), 0.2)
    gdn_w_in = nrm(ks[5], (N_LAYERS_A, D_MODEL, GDN_IN), D_MODEL ** -0.5)
    gdn_conv_w = nrm(ks[6], (N_LAYERS_A, GDN_CONV, 1, GDN_QKV), GDN_CONV ** -0.5)
    gdn_a_log = jnp.log(jax.random.uniform(ks[7], (N_LAYERS_A, 2, GDN_HEADS), f32, 1.0, 16.0))
    dt = jnp.exp(jax.random.uniform(ks[8], (N_LAYERS_A, 2, GDN_HEADS), f32,
                                    math.log(1e-3), math.log(1e-1)))
    gdn_dt_bias = dt + jnp.log(-jnp.expm1(-dt))
    gdn_norm_w = 1.0 + nrm(ks[9], (N_LAYERS_A, GDN_DV), 0.02)
    gdn_w_out = nrm(ks[10], (N_LAYERS_A, GDN_HEADS * GDN_DV, D_MODEL), (GDN_HEADS * GDN_DV) ** -0.5)
    dswa_w_in = nrm(ks[11], (N_LAYERS_B, D_MODEL, 3 * DSWA_WIDTH), D_MODEL ** -0.5)
    dswa_w_out = nrm(ks[12], (N_LAYERS_B, DSWA_WIDTH, D_MODEL), DSWA_WIDTH ** -0.5)
    mlp_w1 = nrm(ks[13], (DEPTH, D_MODEL, D_FF), D_MODEL ** -0.5)
    mlp_w2 = nrm(ks[14], (DEPTH, D_FF, D_MODEL), D_FF ** -0.5)
    return {'x': x, 'norm_mix': norm_mix, 'norm_mlp': norm_mlp, 'norm_final': norm_final,
            'rel_bias': rel_bias, 'gdn_w_in': gdn_w_in, 'gdn_conv_w': gdn_conv_w,
            'gdn_a_log': gdn_a_log, 'gdn_dt_bias': gdn_dt_bias, 'gdn_norm_w': gdn_norm_w,
            'gdn_w_out': gdn_w_out, 'dswa_w_in': dswa_w_in, 'dswa_w_out': dswa_w_out,
            'mlp_w1': mlp_w1, 'mlp_w2': mlp_w2}

def first_block(x, norm_mix, norm_mlp, norm_final, rel_bias, gdn_w_in, gdn_conv_w,
              gdn_a_log, gdn_dt_bias, gdn_norm_w, gdn_w_out, dswa_w_in, dswa_w_out,
              mlp_w1, mlp_w2):
    for i in range(DEPTH):
        h = rmsnorm(x, norm_mix[i])
        j = i // N_MIXERS
        if i % N_MIXERS == 0:
            y = gated_deltanet_bidir(h, gdn_w_in[j], gdn_conv_w[j], gdn_a_log[j],
                                     gdn_dt_bias[j], gdn_norm_w[j], gdn_w_out[j])
        else:
            y = dilated_window_attention(h, dswa_w_in[j], dswa_w_out[j], rel_bias)
        x = x + y
        h = rmsnorm(x, norm_mlp[i])
        x = x + squared_relu_mlp(h, mlp_w1[i], mlp_w2[i])
    return rmsnorm(x, norm_final)


N_HEADS_MLA = 8
QK_NOPE = 64
QK_ROPE = 32
V_HEAD = 64
Q_RANK = 384
KV_RANK = 256
ROPE_THETA = 10000.0
Q_BLOCK = 128
MLA_WIDTH = N_HEADS_MLA * V_HEAD
POOL_WINDOWS = (2, 4, 8, 16)
POOL_GROUPS = 4
POOL_GROUP = 128
POOL_WIDTH = POOL_GROUPS * POOL_GROUP
POOL_OUT_GROUP = D_MODEL // POOL_GROUPS
CONV_HEADS = 8
CONV_HEAD_DIM = 64
CONV_WIDTH = CONV_HEADS * CONV_HEAD_DIM
CONV_K = 3
N_BRANCH = 3
N_EXPERTS = 16
EXPERT_FF = 1024
EC_FACTOR = 2
EPS = 1e-6

IN_SPLITS = (Q_RANK, KV_RANK, QK_ROPE, POOL_WIDTH, CONV_WIDTH, CONV_WIDTH, CONV_WIDTH, N_BRANCH * D_MODEL)
IN_COLS = sum(IN_SPLITS)
IN_OFFSETS = tuple(int(v) for v in np.cumsum(IN_SPLITS)[:-1])


def rmsnorm_2(x, g):
    xf = x.astype(jnp.float32)
    y = xf * lax.rsqrt(jnp.mean(xf * xf, axis=-1, keepdims=True) + EPS)
    return (y * g.astype(jnp.float32)).astype(x.dtype)

def rope_tables(positions, dim):
    freqs = ROPE_THETA ** (-jnp.arange(0, dim, 2, dtype=jnp.float32) / dim)
    ang = positions.astype(jnp.float32)[..., None] * freqs
    return jnp.cos(ang), jnp.sin(ang)

def apply_rope(x, cos, sin):
    half = x.shape[-1] // 2
    xf = x.astype(jnp.float32)
    x1, x2 = xf[..., :half], xf[..., half:]
    return jnp.concatenate([x1 * cos - x2 * sin, x1 * sin + x2 * cos], axis=-1).astype(x.dtype)

def mla_branch(cq, ckv, kr, cos, sin, q_norm_g, w_uq, kv_norm_g, w_ukv, w_oa):
    B, S, _ = cq.shape
    H, DQK = N_HEADS_MLA, QK_NOPE + QK_ROPE
    q = (rmsnorm_2(cq, q_norm_g) @ w_uq).reshape(B, S, H, DQK)
    q_rope = apply_rope(q[..., QK_NOPE:], cos[:, :, None], sin[:, :, None])
    kv = (rmsnorm_2(ckv, kv_norm_g) @ w_ukv).reshape(B, S, H, QK_NOPE + V_HEAD)
    k_nope, v = kv[..., :QK_NOPE], kv[..., QK_NOPE:]
    k_rope = apply_rope(kr, cos, sin)
    q = jnp.concatenate([q[..., :QK_NOPE], q_rope], axis=-1) * (DQK ** -0.5)
    k = jnp.concatenate([k_nope, jnp.broadcast_to(k_rope[:, :, None], (B, S, H, QK_ROPE))], axis=-1)
    nb = S // Q_BLOCK
    qb = q.reshape(B, nb, Q_BLOCK, H, DQK).transpose(1, 0, 2, 3, 4)

    def attend(q_blk):
        s = jnp.einsum('bqhd,bkhd->bhqk', q_blk, k).astype(jnp.float32)
        p = jax.nn.softmax(s, axis=-1).astype(v.dtype)
        return jnp.einsum('bhqk,bkhd->bqhd', p, v)

    o = lax.map(attend, qb)
    o = o.transpose(1, 0, 2, 3, 4).reshape(B, S, MLA_WIDTH)
    return o @ w_oa

def pool_branch(u, w_pool, pool_scale):
    B, S, _ = u.shape
    ug = u.reshape(B, S, POOL_GROUPS, POOL_GROUP).astype(jnp.float32)
    cs = jnp.concatenate([jnp.zeros((B, 1, POOL_GROUPS, POOL_GROUP), jnp.float32),
                          jnp.cumsum(ug, axis=1)], axis=1)
    t = jnp.arange(S)
    outs = []
    for gi, w in enumerate(POOL_WINDOWS):
        lo = jnp.clip(t - w // 2, 0, S - 1)
        hi = jnp.clip(t + w // 2 - 1, 0, S - 1)
        cnt = (hi - lo + 1).astype(jnp.float32)[:, None]
        csg = cs[:, :, gi]
        mean = (csg[:, hi + 1] - csg[:, lo]) / cnt
        outs.append(mean - ug[:, :, gi])
    mixed = jnp.stack(outs, axis=2).astype(u.dtype)
    y = jnp.einsum('bsgc,gcd->bsgd', mixed, w_pool).reshape(B, S, D_MODEL)
    return y * pool_scale

def conv_branch(xin, b_gate, c_gate, conv_w, w_oc):
    S = xin.shape[1]
    z = c_gate * xin
    pad = CONV_K // 2
    zp = jnp.pad(z, ((0, 0), (pad, pad), (0, 0)))
    y = sum(conv_w[k] * zp[:, k:k + S] for k in range(CONV_K))
    return (b_gate * y) @ w_oc

def ec_moe(h, w_router, w_gate, w_up, w_down):
    B, S, D = h.shape
    cap = EC_FACTOR * S // N_EXPERTS
    logits = jnp.einsum('bsd,de->bse', h, w_router).astype(jnp.float32)
    aff = jax.nn.softmax(logits, axis=-1)
    top_val, top_idx = lax.top_k(aff.transpose(0, 2, 1), cap)
    xg = jax.vmap(lambda hb, ib: hb[ib])(h, top_idx)
    g = jnp.einsum('becd,edf->becf', xg, w_gate)
    u = jnp.einsum('becd,edf->becf', xg, w_up)
    y = jnp.einsum('becf,efd->becd', jax.nn.silu(g) * u, w_down) * top_val[..., None].astype(h.dtype)
    return jax.vmap(lambda yb, ib: jnp.zeros((S, D), yb.dtype).at[ib.reshape(-1)].add(yb.reshape(-1, D)))(y, top_idx)

def second_inputs(seed: int = 0) -> dict:
    key = jax.random.key(seed)
    ks = jax.random.split(key, 24)
    f32 = jnp.float32
    D, L = D_MODEL, DEPTH

    def nrm(k, shape, scale):
        return jax.random.normal(k, shape, f32) * scale

    steps = jax.random.randint(ks[2], (BATCH, SEQ), 1, 3)
    positions = (jnp.cumsum(steps, axis=1) - steps[:, :1]).astype(jnp.int32)
    return {
        "x": nrm(ks[0], (BATCH, SEQ, D), 1.0),
        "c": nrm(ks[1], (BATCH, D), 1.0),
        "positions": positions,
        "w_mod": nrm(ks[3], (L, D, 6 * D), 0.5 * D ** -0.5),
        "b_mod": nrm(ks[4], (L, 6 * D), 0.01),
        "norm1_g": 1.0 + nrm(ks[5], (L, D), 0.05),
        "w_in": nrm(ks[6], (L, D, IN_COLS), D ** -0.5),
        "b_gate": nrm(ks[7], (L, N_BRANCH * D), 0.01),
        "q_norm_g": 1.0 + nrm(ks[8], (L, Q_RANK), 0.05),
        "w_uq": nrm(ks[9], (L, Q_RANK, N_HEADS_MLA * (QK_NOPE + QK_ROPE)), Q_RANK ** -0.5),
        "kv_norm_g": 1.0 + nrm(ks[10], (L, KV_RANK), 0.05),
        "w_ukv": nrm(ks[11], (L, KV_RANK, N_HEADS_MLA * (QK_NOPE + V_HEAD)), KV_RANK ** -0.5),
        "w_oa": nrm(ks[12], (L, MLA_WIDTH, D), MLA_WIDTH ** -0.5),
        "w_pool": nrm(ks[13], (L, POOL_GROUPS, POOL_GROUP, POOL_OUT_GROUP), POOL_GROUP ** -0.5),
        "pool_scale": 1.0 + nrm(ks[14], (L, D), 0.05),
        "conv_w": nrm(ks[15], (L, CONV_K, CONV_WIDTH), CONV_K ** -0.5),
        "w_oc": nrm(ks[16], (L, CONV_WIDTH, D), CONV_WIDTH ** -0.5),
        "w_out": nrm(ks[17], (L, D, D), D ** -0.5),
        "norm2_g": 1.0 + nrm(ks[18], (L, D), 0.05),
        "w_router": nrm(ks[19], (L, D, N_EXPERTS), D ** -0.5),
        "w_gate": nrm(ks[20], (L, N_EXPERTS, D, EXPERT_FF), D ** -0.5),
        "w_up": nrm(ks[21], (L, N_EXPERTS, D, EXPERT_FF), D ** -0.5),
        "w_down": nrm(ks[22], (L, N_EXPERTS, EXPERT_FF, D), EXPERT_FF ** -0.5),
        "final_g": 1.0 + nrm(ks[23], (D,), 0.05),
    }

def second_block(x, c, positions, w_mod, b_mod, norm1_g, w_in, b_gate, q_norm_g, w_uq, kv_norm_g, w_ukv, w_oa,
              w_pool, pool_scale, conv_w, w_oc, w_out, norm2_g, w_router, w_gate, w_up, w_down, final_g):
    B, S, D = x.shape
    cos, sin = rope_tables(positions, QK_ROPE)
    c_act = jax.nn.silu(c)
    for l in range(DEPTH):
        mod = (c_act @ w_mod[l] + b_mod[l])[:, None, :]
        sh1, sc1, g1, sh2, sc2, g2 = jnp.split(mod, 6, axis=-1)
        h = rmsnorm_2(x, norm1_g[l]) * (1.0 + sc1) + sh1
        proj = h @ w_in[l]
        cq, ckv, kr, pu, cx, cb, cc, gl = jnp.split(proj, IN_OFFSETS, axis=-1)
        ya = mla_branch(cq, ckv, kr, cos, sin, q_norm_g[l], w_uq[l], kv_norm_g[l], w_ukv[l], w_oa[l])
        yb = pool_branch(pu, w_pool[l], pool_scale[l])
        yc = conv_branch(cx, cb, cc, conv_w[l], w_oc[l])
        gates = jax.nn.sigmoid((gl + b_gate[l]).astype(jnp.float32)).astype(x.dtype).reshape(B, S, N_BRANCH, D)
        merged = gates[:, :, 0] * ya + gates[:, :, 1] * yb + gates[:, :, 2] * yc
        x = x + g1 * (merged @ w_out[l])
        h2 = rmsnorm_2(x, norm2_g[l]) * (1.0 + sc2) + sh2
        x = x + g2 * ec_moe(h2, w_router[l], w_gate[l], w_up[l], w_down[l])
    return rmsnorm_2(x, final_g)


def setup_inputs(seed=0):
    out = dict(first_inputs(seed))
    for name, value in second_inputs(seed + 1).items():
        if name != "x":
            out[name + "_2"] = value
    return out


def reference(
    x, norm_mix, norm_mlp, norm_final, rel_bias, gdn_w_in, gdn_conv_w, gdn_a_log, gdn_dt_bias,
    gdn_norm_w, gdn_w_out, dswa_w_in, dswa_w_out, mlp_w1, mlp_w2, c_2, positions_2, w_mod_2,
    b_mod_2, norm1_g_2, w_in_2, b_gate_2, q_norm_g_2, w_uq_2, kv_norm_g_2, w_ukv_2, w_oa_2,
    w_pool_2, pool_scale_2, conv_w_2, w_oc_2, w_out_2, norm2_g_2, w_router_2, w_gate_2, w_up_2,
    w_down_2, final_g_2,
):
    x = first_block(
        x, norm_mix, norm_mlp, norm_final, rel_bias, gdn_w_in, gdn_conv_w, gdn_a_log,
        gdn_dt_bias, gdn_norm_w, gdn_w_out, dswa_w_in, dswa_w_out, mlp_w1, mlp_w2,
    )
    return second_block(
        x, c_2, positions_2, w_mod_2, b_mod_2, norm1_g_2, w_in_2, b_gate_2, q_norm_g_2, w_uq_2,
        kv_norm_g_2, w_ukv_2, w_oa_2, w_pool_2, pool_scale_2, conv_w_2, w_oc_2, w_out_2,
        norm2_g_2, w_router_2, w_gate_2, w_up_2, w_down_2, final_g_2,
    )


_drawn_inputs = setup_inputs


def setup_inputs(seed=0):
    import zlib

    import numpy as np

    out = dict(_drawn_inputs(seed))
    spreads = {}
    factors = {'rel_bias': 5.699,
     'gdn_norm_w': 3.651,
     'b_mod_2': 3.316,
     'b_gate_2': 8.0,
     'q_norm_g_2': 8.0,
     'w_uq_2': 2.718,
     'kv_norm_g_2': 8.0,
     'pool_scale_2': 5.067,
     'norm2_g_2': 3.663}
    for name, (base, spread) in spreads.items():
        noise = np.random.default_rng([zlib.crc32(name.encode()), seed]).standard_normal(out[name].shape)
        drawn = base * np.exp(spread * noise) if base else spread * noise
        out[name] = __import__('jax').numpy.asarray(drawn.astype(out[name].dtype))
    for name, factor in factors.items():
        out[name] = (out[name] * factor).astype(out[name].dtype)
    return out
```

```python
from contextlib import ExitStack
import math

import numpy as np

import concourse.bass as bass
from concourse import mybir

ALU = mybir.AluOpType
ACT = mybir.ActivationFunctionType
F32 = mybir.dt.float32
I32 = mybir.dt.int32
U32 = mybir.dt.uint32
U8 = mybir.dt.uint8
AX = mybir.AxisListType.X

P = 128
D = 1024
KC = D // P
T = 256
TT = T // P
EPS = 1e-6
GH = 8
LEVELS = (2, 4, 8, 16, 32, 64)
SH, SE, SGRP, SHALF = 18, 64, 6, 64
SDIL = (1, 4, 16)
BUCKETS, MAX_DIST = 32, 1024
TZW = 3 * P
NL = 2
MH, NOPE, ROPE, VH, QR, KVR = 8, 64, 32, 64, 384, 256
DQK = NOPE + ROPE
QKW = QR + KVR
NE, CAP, FF = 16, 32, 1024
C_PU, C_CX, C_CB, C_CC, C_GL = 672, 1184, 1696, 2208, 2720
NEG = -1e30

ROWS = (
    (("norm_mix", 16), ("norm_mlp", 16), ("c_2", 8), ("norm1_g_2", 16), ("norm2_g_2", 16), ("b_gate_2", 48)),
    (("gdn_conv_w", 120),),
    (("b_mod_2", 96), ("pool_scale_2", 16), ("q_norm_g_2", 6), ("kv_norm_g_2", 4)),
    (("conv_w_2", 24),),
)
COL = {}
for _n, _rows in enumerate(ROWS):
    _at = 0
    for _name, _len in _rows:
        COL[_name] = _n * P + _at
        _at += _len

CREDITED = ("mod_mm", "mod_out", "s4_mm", "expert_done", "he_ready", "ys_out")

RING = 6
SLOT = 4096
U_QKV, U_Z, U_AB, U_GOUT = 0, 6, 8, 9
U_MLP = (11, 49)
MLP_TURNS = 2
U_SIN, U_SOUT = 39, 46
U_SEC = 77
SEC_UNITS = 18 + 6 * NE
SEC_TURNS = SEC_UNITS // RING
(V_CQ, V_KV, V_PU, V_CX, V_CC, V_CB, V_UQ, V_UKV, V_OA, V_GL, V_OC, V_OUT, V_MOE) = (
    0, 1, 2, 3, 4, 5, 6, 7, 8, (9, 10, 11, 12, 14, 15), 13, 16, 18)


def rel_buckets():
    rel = np.arange(-(T - 1), T)
    nb = BUCKETS // 2
    me = nb // 2
    n = np.abs(rel)
    nf = np.maximum(n, 1).astype(np.float32)
    large = me + (np.log(nf / np.float32(me)) / np.float32(math.log(MAX_DIST / me)) * np.float32(nb - me)).astype(np.int32)
    large = np.minimum(large, nb - 1)
    return np.where(rel > 0, nb, 0) + np.where(n < me, n, large)


NREL = 2 * T - 1


def constants():
    i = np.arange(P)
    eye = np.eye(P, dtype=np.float32)
    ones = np.ones((P, P), np.float32)
    cum = np.stack([(i[:, None] <= i[None]), (i[:, None] >= i[None])], 1).astype(np.float32)
    neg = np.where(cum > 0, 0.0, NEG).astype(np.float32)
    fr = (10000.0 ** (-np.arange(0, ROPE, 2, dtype=np.float32) / np.float32(ROPE))).astype(np.float32)
    tok = np.stack([i, i + P], 1).astype(np.float32)
    fconst = np.concatenate([eye, ones, np.tile(fr[None], (P, 1)), tok], 1)
    gconst = np.concatenate([cum.reshape(P, -1), neg.reshape(P, -1)], 1)
    low = []
    for s in (1,) + LEVELS:
        same = (i[:, None] // (2 * s)) == (i[None] // (2 * s))
        low.append(same & (i[:, None] % (2 * s) >= s) & (i[None] % (2 * s) < s))
    low = np.stack(low, 1)
    masks = np.stack([low, low.transpose(2, 1, 0)], 1).astype(np.float32)
    t = np.arange(T)
    pm = np.zeros((4, T, T), np.float32)
    for g, w in enumerate((2, 4, 8, 16)):
        lo, hi = np.clip(t - w // 2, 0, T - 1), np.clip(t + w // 2 - 1, 0, T - 1)
        inside = (t[None] >= lo[:, None]) & (t[None] <= hi[:, None])
        pm[g] = inside / (hi - lo + 1).astype(np.float32)[:, None] - np.eye(T, dtype=np.float32)
    pool = pm.transpose(2, 0, 1).reshape(TT, P, 4, T).transpose(1, 0, 2, 3)
    rel = np.arange(-(T - 1), T)
    onehot = (rel_buckets()[None] == np.arange(BUCKETS)[:, None]).astype(np.float32)
    mask = np.zeros((SH, NREL), np.float32)
    for g, d in enumerate(SDIL):
        bad = (rel % d != 0) | (np.abs(rel) > SHALF * d)
        mask[g * SGRP:(g + 1) * SGRP, bad] = NEG
    return {
        "k_base": fconst, "k_gdn": gconst, "k_masks": np.ascontiguousarray(masks.reshape(P, -1)),
        "k_pool": np.ascontiguousarray(pool.reshape(P, -1)).astype(np.float32),
        "k_onehot": onehot, "k_reverse": np.ascontiguousarray(eye[::-1]), "k_winmask": mask,
    }


def program(nc, A, out, stop=None):
    with ExitStack() as ctx:
        sb = lambda n, s, d=F32: ctx.enter_context(nc.sbuf_tensor(n, s, d))
        sems = {}

        def sem(n):
            if n not in sems:
                sems[n] = ctx.enter_context(nc.semaphore(n))
            return sems[n]

        PS = ctx.enter_context(nc.psum_tensor("psum", [P, 8, 512], F32))
        ring = sb("ring", [P, RING, SLOT])
        X = sb("x_resid", [P, TT, D])
        XN = sb("x_normed", [P, TT, D])
        HT = sb("h_featmajor", [P, KC, T])
        base = sb("base", [P, 2 * P + 18])
        COLS = sb("param_cols", [P, 4 * P])
        MODC = sb("mod_cols", [P, NL, 48])
        CACT = sb("c_act", [P, KC])
        ssq = sb("ssq", [P, 2]); var = sb("var", [P, 2]); rstd = sb("rstd", [P, 2])
        nhalf = sb("neg_half", [P, 64])
        ar = sb("arena", [P, 20480])
        marks = sb("block_masks", [P, 2 * 7 * P], U8)
        rel_dram = nc.dram_tensor("rel_scratch", [SH, NREL], F32, kind="Internal").ap()

        ident, ones = base[:, 0:P], base[:, P:2 * P]
        freq, tokid = base[:, 2 * P:2 * P + 16], base[:, 2 * P + 16:2 * P + 18]

        class Carve:
            def __init__(self, at=0):
                self.at = at

            def __call__(self, *shape, parts=P):
                n = int(np.prod(shape))
                v = ar[0:parts, self.at:self.at + n]
                self.at += n
                assert self.at <= 20480, self.at
                if len(shape) == 2:
                    v = v.rearrange("p (a b) -> p a b", b=shape[1])
                if len(shape) == 3:
                    v = v.rearrange("p (a b c) -> p a b c", b=shape[1], c=shape[2])
                if len(shape) == 4:
                    v = v.rearrange("p (a b c d) -> p a b c d", b=shape[1], c=shape[2], d=shape[3])
                return v

        def bank(b, n=512):
            return PS[:, b, 0:n]

        def pair(b, w):
            return PS[:, b, :].rearrange("p (a w) -> p a w", w=w)

        c = Carve()
        KQT = c(GH, 2, T)
        KN = c(GH, TT, P)
        V = c(GH, TT, P)
        Z = c(TT, D)
        CUM = c(2, P)
        NEGM = c(2, P)
        NW = c(P)
        GS = c(2, 16)
        BT = c(2, 16)
        GC = c(2, 2, 8)
        EG = c(2, 2, 8)
        KD_S = c(2, 2, 8)
        TOT = c(2, 2, 8)
        RQK = c(TT, 16)
        RQV = c(TT, 16)
        DTB = c(16); ALOG = c(16)
        SPT = c(6, 32)
        top = c.at
        CP = c(3, 260)
        CV = c(3, T)
        OA = Carve(top)
        O_ACC = OA(TT, GH, P)
        GJ = OA.at
        lanes = []
        for _ in range(2):
            lanes.append(dict(DT=OA(4, P), KD=OA(4, 2, P), Tm=OA(4, P), U=OA(4, P)))
        SST = OA(4, P)
        VN = OA(4, P)
        R1 = OA(4, P)
        c = Carve(0)
        RL = c(TT, 512)
        MT = c(4, T)
        MA = [c(512), c(512)]
        c = Carve(0)
        SQKT = c(18, T)
        SV = c(TT, SH * SE)
        TZ = c(2, TZW)
        SP_ = c(4, T)
        SPT2 = c(2, 2, T)
        SO = c(TT, SH * SE)
        SOT = c(9, T)
        NMX = c(TT, SH); MX = c(TT, SH); SM = c(TT, SH); SC = c(TT, SH)
        MM = c(TT, SGRP); SS = c(TT, SH); DEN = c(TT, SGRP)
        RV = c(NREL + 1); RMK = c(NREL + 1); ROH = c(NREL + 1); RTB = c(SH)
        FGR = c(D)
        RJ = c(P)
        c = Carve(0)
        POOLM = c(TT, 4, T)
        WPOOL = c(4, T)
        WR = c(KC, NE)
        COS = c(TT, 16); SIN = c(TT, 16); ANG = c(TT, 16); KRD = c(TT, 16); POSF = c(TT)
        GR = c(D)
        TMP = c(512)
        sec_top = c.at
        CQ = c(TT, QKW)
        KR = c(TT, ROPE)
        KRR = c(TT, ROPE)
        CQT = c(5, T)
        MQ = c(TT, MH, DQK)
        MK = c(TT, MH, DQK)
        MV = c(TT, MH, VH)
        RT = c(4, P)
        PU = c(TT, 512)
        MIXT = c(4, T)
        BCT = c(4, T)
        OT = c(4, T)
        MSM = c(MH, 2); MNM = c(MH, 2); SS2 = c(4); VAR2 = c(4); RS2 = c(4)
        q_at = c.at
        QT = c(MH, T)
        KT = c(MH, T)
        c = Carve(sec_top)
        MP = c(2, T); MP2 = c(2, T)
        c2 = Carve(c.at)
        MPT = [CQT[:, 0:2, :], CQT[:, 2:4, :]]
        c = Carve(q_at)
        CX = c(4, T)
        CZ = c(4, 258)
        c = Carve(q_at)
        MG = c(KC, T)
        SG = c(2, T)
        MT2 = c(2, T)
        c = Carve(sec_top)
        XG = c(KC, NE * CAP)
        ST = c(TT, NE * CAP)
        STV = c(TT, NE * CAP)
        AFF = c(TT, NE)
        RM = c(TT); RSM = c(TT); RIN = c(TT)
        AT = c(T); AT2 = c(T)
        VALS = c(CAP); IDXF = c(CAP)
        BD = c(2, NE * CAP)
        XGE = c(KC, CAP)
        SREP = c(TT, 4, CAP)
        S4 = c(T)
        SILG = c(T)
        HE = c(T)
        HTE = c(2, P)
        YS = c(2, 512)
        zero1 = sb("zero", [P, 1])[:]
        GCOL = sb("gate_cols", [P, 16])[:]
        SCL = sb("norm_scale", [P, KC])[:]
        BIA = sb("norm_shift", [P, KC])[:]
        LC = sb("layer_cols", [P, 49])[:]
        PSC, BG, CW, QKG = LC[:, 0:8], LC[:, 8:32], LC[:, 32:44], LC[:, 44:49]
        IDXU = sb("topk_index", [16, CAP], U32)
        POSI = sb("pos_i", [P, TT], I32)
        rows = ring

        nlev_ = len(LEVELS)
        ajunk = sb("act_junk", [P, 1])
        JUNK = lanes[0]["DT"][:, 0]
        GJUNK = ar[:, GJ:GJ + 2048]
        MSTAGE = ar[:, GJ + 512:GJ + 512 + 2 * 7 * P]
        w_full = [sem(f"w_full{i}") for i in range(RING)]
        w_free = [sem(f"w_free{i}") for i in range(RING)]

        def full(eng, n, turns=0):
            eng.wait_ge(w_full[n % RING], (turns + (n // RING + 1)) * 16)

        def colof(name, i):
            return COLS[:, COL[name] + i:COL[name] + i + 1]

        block = ctx.enter_context(nc.Block())

        FGR2 = GR

        @block.sync
        def _(sp):
            def load(n, src, turns=0, parts=P):
                if n >= RING:
                    sp.wait_ge(w_free[n % RING], turns + n // RING)
                a, b = src.shape[1], src.shape[2]
                dst = ring[0:parts, n % RING, 0:a * b].rearrange("p (a b) -> p a b", b=b)
                sp.dma_start(dst, src).then_inc(w_full[n % RING], 16)

            def dump(n):
                sp.wait_ge(sem("x_ready"), n)
                sp.dma_start(out[0].rearrange("(t p) d -> p t d", p=P), X[:]).then_inc(sem("out_stored"), 16)
                sp.wait_ge(sem("out_stored"), 16)

            def cols(w, a, b):
                return w.rearrange("(k p) n -> p k n", p=P)[:, :, a:b]

            sp.dma_start(base[:], A["k_base"]).then_inc(sem("params_in"), 16)
            for n, group in enumerate(ROWS):
                at = 0
                for name, cnt in group:
                    v = A[name]
                    nd = len(v.shape)
                    flat = v.rearrange({1: "a -> a", 2: "a b -> (a b)", 3: "a b c -> (a b c)", 4: "a b c d -> (a b c d)"}[nd])
                    sp.dma_start(XN[at:at + cnt, 1, n * P:(n + 1) * P],
                                 flat.rearrange("(r w) -> r w", w=P)).then_inc(sem("params_in"), 16)
                    at += cnt
            sp.dma_start(X[:], A["x"][0].rearrange("(t p) d -> p t d", p=P)).then_inc(sem("x_in"), 16)
            load(0, cols(A["gdn_w_in"][0], 0, 512))
            sp.dma_start(CUM, A["k_gdn"][:, 0:2 * P].rearrange("p (a b) -> p a b", b=P)).then_inc(sem("gdn_in"), 16)
            sp.dma_start(NEGM, A["k_gdn"][:, 2 * P:4 * P].rearrange("p (a b) -> p a b", b=P)).then_inc(sem("gdn_in"), 16)
            sp.dma_start(MSTAGE, A["k_masks"]).then_inc(sem("gdn_in"), 16)
            sp.dma_start(NW, A["gdn_norm_w"].partition_broadcast(P)[:, 0]).then_inc(sem("gdn_in"), 16)
            sp.dma_start(DTB, A["gdn_dt_bias"].rearrange("a b c -> a (b c)").partition_broadcast(P)[:, 0]).then_inc(sem("gdn_in"), 16)
            sp.dma_start(ALOG, A["gdn_a_log"].rearrange("a b c -> a (b c)").partition_broadcast(P)[:, 0]).then_inc(sem("gdn_in"), 16)
            for t in range(TT):
                sp.dma_start(POSI[:, t:t + 1], A["positions_2"][0, t * P:(t + 1) * P].rearrange("(p a) -> p a", a=1)).then_inc(sem("gdn_in"), 16)
            for u in range(1, 8):
                load(U_QKV + u, cols(A["gdn_w_in"][0], 512 * u, 512 * (u + 1)))
            load(U_AB, cols(A["gdn_w_in"][0], 4096, 4128))

            def halves(w, u):
                return w[u * 512:(u + 1) * 512, :].rearrange("(k p) n -> p k n", p=P)

            for u in range(2):
                load(U_GOUT + u, halves(A["gdn_w_out"][0], u))
            if stop == "gdn":
                return dump(1)

            def mlp(l):
                w1, w2, wm = A["mlp_w1"][l], A["mlp_w2"][l], A["w_mod_2"][l]
                w1c = w1.rearrange("(k p) n -> p k n", p=P)
                wmc = wm.rearrange("(k p) n -> p k n", p=P)
                w2r = w2.rearrange("(u k p) n -> u p k n", k=4, p=P)
                n0 = U_MLP[l]
                load(n0, w1c[:, :, 0:512])
                load(n0 + 1, w1c[:, :, 512:1024])
                load(n0 + 2, w2r[0])
                with sp.Fori(0, 2) as i:
                    for j in range(3):
                        n = n0 + 3 + 4 * j
                        turns = i * MLP_TURNS
                        load(n, w1c[:, :, bass.ds((i * 3 + j + 2) * 512, 512)], turns)
                        load(n + 1, w2r[bass.ds(i * 3 + j + 1, 1)][0], turns)
                        load(n + 2, wmc[:, :, bass.ds((i * 3 + j) * 1024, 512)], turns)
                        load(n + 3, wmc[:, :, bass.ds((i * 3 + j) * 1024 + 512, 512)], turns)
                load(n0 + 27, w2r[7])

            mlp(0)
            if stop == "mlp0":
                return dump(2)
            sp.wait_ge(sem("x_ready"), 2)
            sp.dma_start(ROH[0:BUCKETS, 0:NREL], A["k_onehot"]).then_inc(sem("tables_in"), 16)
            sp.dma_start(RMK[0:SH, 0:NREL], A["k_winmask"]).then_inc(sem("tables_in"), 16)
            sp.dma_start(RTB[0:BUCKETS, :], A["rel_bias"]).then_inc(sem("tables_in"), 16)
            sp.dma_start(RJ, A["k_reverse"]).then_inc(sem("tables_in"), 16)
            sp.dma_start(FGR, A["norm_final"].rearrange("(a d) -> a d", a=1).partition_broadcast(P)[:, 0]).then_inc(sem("fgr_in"), 16)
            w = A["dswa_w_in"][0]
            for u in range(7):
                load(U_SIN + u, cols(w, 512 * u, min(512 * (u + 1), 3456)))
            sp.wait_ge(sem("rel_vec"), 1)
            sp.dma_start(rel_dram, RV[0:SH, 0:NREL]).then_inc(sem("rel_out"), 16)
            sp.wait_ge(sem("rel_out"), 16)
            tz = lambda h: bass.AP(rel_dram.tensor, rel_dram.offset + h * NREL, [[1, P], [1, TZW]])
            for h in range(SH):
                if h >= 2:
                    sp.wait_ge(sem("s_biased"), 2 * (h - 1))
                sp.dma_start(TZ[:, h % 2, :], tz(h)).then_inc(sem(f"tz_in{h % 2}"), 16)
            wo = A["dswa_w_out"][0]
            for u in range(2):
                load(U_SOUT + u, halves(wo, u))
            load(U_SOUT + 2, wo[1024:1152, :].rearrange("(k p) n -> p k n", p=P))
            mlp(1)
            if stop == "b1":
                return dump(5)
            sp.wait_ge(sem("x_ready"), 5)
            sp.dma_start(POOLM.rearrange("p a b c -> p (a b c)"), A["k_pool"]).then_inc(sem("tables_in"), 16)
            with sp.Fori(0, NL) as L:
                tu = L * SEC_TURNS
                ld = lambda n, src: load(U_SEC + n, src, tu)
                one = lambda ap: ap[bass.ds(L, 1)][0]
                sp.wait_ge(sem("x_ready"), L * 2 + 5)
                sp.dma_start(WPOOL, one(A["w_pool_2"]).rearrange("g c n -> c g n")).then_inc(sem("side_in"), 16)
                sp.dma_start(WR, one(A["w_router_2"]).rearrange("(k p) n -> p k n", p=P)).then_inc(sem("side_in"), 16)
                wi = one(A["w_in_2"])
                for n, a, b in ((V_CQ, 0, QR), (V_KV, QR, C_PU), (V_PU, C_PU, C_CX), (V_CX, C_CX, C_CB),
                                (V_CC, C_CC, C_GL), (V_CB, C_CB, C_CC)):
                    ld(n, cols(wi, a, b))
                ld(V_UQ, one(A["w_uq_2"]).rearrange("(k p) n -> p k n", p=P))
                ld(V_UKV, one(A["w_ukv_2"]).rearrange("(k p) n -> p k n", p=P))
                ld(V_OA, one(A["w_oa_2"]).rearrange("(k p) n -> p k n", p=P))
                for g in range(6):
                    if g == 4:
                        ld(V_OC, one(A["w_oc_2"]).rearrange("(k p) n -> p k n", p=P))
                    ld(V_GL[g], cols(wi, C_GL + 512 * g, C_GL + 512 * (g + 1)))
                for u in range(2):
                    ld(V_OUT + u, halves(one(A["w_out_2"]), u))
                with sp.Fori(0, NE) as e:
                    two = lambda ap: one(ap)[bass.ds(e, 1)][0]
                    for m, name in enumerate(("w_gate_2", "w_up_2")):
                        for u in range(2):
                            load(U_SEC + V_MOE + 2 * m + u, halves(two(A[name]), u), tu + e)
                    for u in range(2):
                        load(U_SEC + V_MOE + 4 + u, cols(two(A["w_down_2"]), 512 * u, 512 * (u + 1)), tu + e)
            sp.wait_ge(sem("x_ready"), 9)
            sp.dma_start(FGR2, A["final_g_2"].rearrange("(a d) -> a d", a=1).partition_broadcast(P)[:, 0]).then_inc(sem("fgr_in"), 16)
            for t in range(TT):
                sp.wait_ge(sem("x_ready"), t + 1 + 9)
                sp.dma_start(out[0, t * P:(t + 1) * P, :], X[:, t, :]).then_inc(sem("out_stored"), 16)
            sp.wait_ge(sem("out_stored"), 16 * TT)


        def spent(eng, n, turns=0):
            eng.wait_ge(w_free[n % RING], turns + (n // RING + 1))

        def W(n, b, parts=P):
            a = SLOT // b
            return ring[0:parts, n % RING, 0:a * b].rearrange("p (a b) -> p a b", b=b)

        def qkv_piece(eng, ch):
            if ch % 4 == 3:
                spent(eng, U_QKV + ch // 4)
            else:
                eng.wait_ge(sem("chunk_mm"), 3 * (ch // 4) + ch % 4 + 1)

        @block.tensor
        def _(pe):
            mm = nc.tensor.matmul

            def used(ins, n):
                ins.then_inc(w_free[n % RING], 1)

            def norm(k):
                pe.wait_ge(sem("xn0"), k + 1)
                for t in range(TT):
                    if t == 1:
                        pe.wait_ge(sem("xn1"), k + 1)
                    for dc in range(KC):
                        o = pair(4 + dc // 2, P)[:, (dc % 2) * 2 + t]
                        ins = nc.tensor.transpose(o, XN[:, t, dc * P:(dc + 1) * P], ident)
                ins.then_inc(sem("ht_psum"), 1)

            def normed(k):
                pe.wait_ge(sem("ht_ready"), k * 8 + 8)

            pe.wait_ge(sem("params_in"), 16 + 16 * sum(len(g) for g in ROWS))
            for n, group in enumerate(ROWS):
                cnt = sum(x for _, x in group)
                ins = nc.tensor.transpose(PS[:, 3, n * P:n * P + cnt], XN[0:cnt, 1, n * P:(n + 1) * P], ident[0:cnt, 0:cnt])
            ins.then_inc(sem("cols_psum"), 1)

            norm(0)
            normed(0)

            def qkv(ch):
                n = U_QKV + ch // 4
                if ch % 4 == 0:
                    full(pe, n)
                if ch >= 4:
                    pe.wait_ge(sem("chunk_out"), ch - 3)
                for k in range(KC):
                    ins = mm(bank(ch % 4, T), W(n, 512)[:, k, (ch % 4) * P:(ch % 4 + 1) * P], HT[:, k, :],
                             start=k == 0, stop=k == KC - 1)
                if ch % 4 == 3:
                    used(ins, n)
                else:
                    ins.then_inc(sem("chunk_mm"), 1)

            def turn(ch):
                pe.wait_ge(sem("silu"), ch + 1)
                if ch >= 2:
                    if ch - 2 < 16:
                        pe.wait_ge(sem("sq_done"), ch - 1)
                    if ch - 2 >= GH:
                        pe.wait_ge(sem("tok_done"), ch - 1 - GH)
                src = KQT[:, ch, 1, :] if ch < GH else KQT[:, ch - GH, 0, :] if ch < 2 * GH else CV[:, ch % 3, :]
                for t in range(TT):
                    ins = nc.tensor.transpose(PS[:, 4 + ch % 2, t * P:(t + 1) * P], src[:, t * P:(t + 1) * P], ident)
                ins.then_inc(sem("turned"), 1)

            for ch in range(24):
                qkv(ch)
                if ch >= 2:
                    turn(ch - 2)
            turn(22)
            turn(23)
            for u in range(2):
                full(pe, U_Z + u)
                for t in range(TT):
                    b = 2 * u + t
                    pe.wait_ge(sem("chunk_out"), 21 + b)
                    for k in range(KC):
                        ins = mm(bank(b), HT[:, k, t * P:(t + 1) * P], W(U_Z + u, 512)[:, k, :],
                                 start=k == 0, stop=k == KC - 1)
                    if t == 0:
                        ins.then_inc(sem("tok_mm"), 1)
                used(ins, U_Z + u)
            full(pe, U_AB)
            for t in range(TT):
                for k in range(KC):
                    ins = mm(PS[:, 6, t * 32:(t + 1) * 32], HT[:, k, t * P:(t + 1) * P],
                             ring[:, U_AB % RING, k * 32:(k + 1) * 32], start=k == 0, stop=k == KC - 1)
            used(ins, U_AB)
            pe.wait_ge(sem("kn_ready"), 1)
            for g in range(4):
                if g >= 2:
                    pe.wait_ge(sem("knt_done"), g - 1)
                for hh in range(2):
                    for t in range(TT):
                        ins = nc.tensor.transpose(pair(4 + g % 2, P)[:, hh * 2 + t], KN[:, 2 * g + hh, t, :], ident)
                ins.then_inc(sem("knt_mm"), 1)
            pe.wait_ge(sem("gs_ready"), 1)
            for d in range(2):
                rhs = GS[:, :, d * 8:(d + 1) * 8]
                mm(PS[:, 7, d * 16:(d + 1) * 16].rearrange("p (a b) -> p a b", b=8), CUM[:, d, :], rhs, start=True, stop=True)
                ins = mm(PS[:, 7, 32 + d * 16:48 + d * 16].rearrange("p (a b) -> p a b", b=8), ones, rhs, start=True, stop=True)
            ins.then_inc(sem("cum_mm"), 1)
            pe.wait_ge(sem("decay_out"), 1 + 1)
            pe.wait_ge(sem("knt_done"), 4)
            pe.wait_ge(sem("tok_out"), 4)

            nlev = len(LEVELS)
            for it in range(4):
                d, hg = it // 2, (it % 2) * 4
                fst, snd = (0, 1) if d == 0 else (1, 0)
                if it >= 1:
                    pe.wait_ge(sem("core_done"), it)
                for l in range(2):
                    for h in range(4):
                        g = d * 8 + hg + h
                        mm(pair(3 * l, P)[:, h], GS[:, l, g:g + 1].to_broadcast([P, P]), CUM[:, d, :], start=True, stop=True)
                    for h in range(4):
                        g = d * 8 + hg + h
                        mm(pair(3 * l + 1, P)[:, h], BT[:, l, g:g + 1].to_broadcast([P, P]), ident, start=True, stop=True)
                    for h in range(4):
                        b = (3 * l + 2) if h < 2 else 6 + l
                        ins = mm(pair(b, P)[:, (h % 2) * 2:(h % 2) * 2 + 2], KQT[:, hg + h, 0, l * P:(l + 1) * P],
                                 KQT[:, hg + h, :, l * P:(l + 1) * P], start=True, stop=True)
                    ins.then_inc(sem("core_setup"), 1)
                for l in range(2):
                    pe.wait_ge(sem("u_init"), 2 * it + l + 1)
                    for h in range(4):
                        ins = nc.tensor.transpose(pair(3 * l, P)[:, h], lanes[l]["U"][:, h], ident)
                    ins.then_inc(sem("t_init"), 1)
                for q in range(nlev):
                    for l in range(2):
                        if q == 0:
                            pe.wait_ge(sem("t_ready"), 2 * it + l + 1)
                        else:
                            pe.wait_ge(sem("t_grown"), (it * 5 + q - 1) * 2 + l + 1)
                        for h in range(4):
                            ins = mm(pair(3 * l, P)[:, h], lanes[l]["KD"][:, h, 0], lanes[l]["Tm"][:, h], start=True, stop=True)
                        ins.then_inc(sem("p_mm"), 1)
                    for l in range(2):
                        pe.wait_ge(sem("p_out"), (it * nlev + q) * 2 + l + 1)
                        if q >= 1:
                            pe.wait_ge(sem("u_grown"), (it * nlev + q - 1) * 2 + l + 1)
                        if q < nlev - 1:
                            for h in range(4):
                                ins = mm(pair(3 * l + 1, P)[:, h], lanes[l]["U"][:, h], lanes[l]["DT"][:, h], start=True, stop=True)
                            ins.then_inc(sem("q_mm"), 1)
                        for h in range(4):
                            ins = mm(pair(3 * l + 2, P)[:, h], lanes[l]["DT"][:, h], lanes[l]["U"][:, h], start=True, stop=True)
                        ins.then_inc(sem("r_mm"), 1)
                pe.wait_ge(sem("u_grown"), (it + 1) * nlev * 2)
                pe.wait_ge(sem("r1_ready"), 2 * it + 1)
                for h in range(4):
                    ins = mm(pair(6, P)[:, h], lanes[fst]["U"][:, h], R1[:, h], start=True, stop=True)
                ins.then_inc(sem("vn_mm"), 1)
                pe.wait_ge(sem("vn_out"), 2 * it + 1)
                pe.wait_ge(sem("kdec"), it + 1)
                for h in range(4):
                    ins = mm(pair(7, P)[:, h], lanes[fst]["Tm"][:, h], VN[:, h], start=True, stop=True)
                ins.then_inc(sem("s_mm"), 1)
                for h in range(4):
                    ins = mm(pair(2, P)[:, h], lanes[fst]["KD"][:, h, 1], VN[:, h], start=True, stop=True)
                ins.then_inc(sem("o_mm"), 1)
                pe.wait_ge(sem("s_out"), it + 1)
                for h in range(4):
                    mm(pair(0, P)[:, h], KQT[:, hg + h, 0, snd * P:(snd + 1) * P], SST[:, h], start=True, stop=True)
                    ins = mm(pair(1, P)[:, h], KQT[:, hg + h, 1, snd * P:(snd + 1) * P], SST[:, h], start=True, stop=True)
                ins.then_inc(sem("ks_mm"), 1)
                pe.wait_ge(sem("r1_ready"), 2 * it + 2)
                for h in range(4):
                    ins = mm(pair(6, P)[:, h], lanes[snd]["U"][:, h], R1[:, h], start=True, stop=True)
                ins.then_inc(sem("vn_mm"), 1)
                pe.wait_ge(sem("vn_out"), 2 * it + 2)
                for h in range(4):
                    ins = mm(pair(7, P)[:, h], lanes[snd]["KD"][:, h, 1], VN[:, h], start=True, stop=True)
                ins.then_inc(sem("o_mm"), 1)

            for t in range(TT):
                pe.wait_ge(sem("y_ready"), t + 1)
                for dc in range(KC):
                    ins = nc.tensor.transpose(pair(3 + dc // 2, P)[:, (dc % 2) * 2 + t], XN[:, t, dc * P:(dc + 1) * P], ident)
            ins.then_inc(sem("y_turned"), 1)
            pe.wait_ge(sem("y_back"), 4)

            def rows_product(n, turns, lhs, first, last):
                full(pe, n, turns)
                cnt = lhs.shape[1]
                for kk in range(cnt):
                    for b in range(4):
                        t, h = b // 2, b % 2
                        ins = mm(bank(b), lhs[:, kk, t * P:(t + 1) * P], W(n, D)[:, kk, h * 512:(h + 1) * 512],
                                 start=first and kk == 0, stop=last and kk == cnt - 1, skip_group_check=True)
                used(ins, n)

            for u in range(2):
                rows_product(U_GOUT + u, 0, HT[:, 4 * u:4 * u + 4, :], u == 0, u == 1)
            if stop == "gdn":
                return

            def mlp(l):
                n0 = U_MLP[l]

                def up(n, turns, t, relus):
                    full(pe, n, turns)
                    if relus is not None:
                        pe.wait_ge(sem("relu"), relus)
                    for k in range(KC):
                        ins = mm(bank(4 + t), HT[:, k, t * P:(t + 1) * P], W(n, 512)[:, k, :], start=k == 0, stop=k == KC - 1)
                    if t == 1:
                        used(ins, n)
                    else:
                        ins.then_inc(sem("up_mm"), 1)

                def chunk(u, n_up, n_down, turns, mods, first=False, last=False):
                    if n_up is not None:
                        up(n_up, turns, 0, u * 2 + 1)
                    pe.wait_ge(sem("relu"), u * 2 + 2)
                    pe.wait_ge(sem("mod_out"), mods + 1)
                    for t in range(TT):
                        for cc in range(4):
                            ins = nc.tensor.transpose(pair(6 + cc // 2, P)[:, (cc % 2) * 2 + t], RL[:, t, cc * P:(cc + 1) * P], ident)
                    ins.then_inc(sem("rl_turned"), 1)
                    if n_up is not None:
                        up(n_up, turns, 1, u * 2 + 2)
                    pe.wait_ge(sem("mt_ready"), u * 2 + 2)
                    rows_product(n_down, turns, MT, first, last)

                for t in range(TT):
                    up(n0, 0, t, None)
                chunk(8 * l, n0 + 1, n0 + 2, 0, 6 * l, first=True)
                with pe.Fori(0, 2) as i:
                    for j in range(3):
                        n = n0 + 3 + 4 * j
                        chunk(i * 3 + (8 * l + 1 + j), n, n + 1, i * MLP_TURNS, i * 3 + (6 * l + j))
                        spent(pe, n + 2, i * MLP_TURNS)
                        spent(pe, n + 3, i * MLP_TURNS)
                        for cc in range(8):
                            ins = mm(PS[:, 6, cc:cc + 1], MA[cc // 4][:, (cc % 4) * P:(cc % 4 + 1) * P], ones[:, 0:1],
                                     start=True, stop=True)
                        ins.then_inc(sem("mod_mm"), 1)
                chunk(8 * l + 7, None, n0 + 27, 0, 6 * l + 6, last=True)

            norm(1)
            normed(1)
            mlp(0)
            if stop == "mlp0":
                return

            norm(2)
            normed(2)
            pe.wait_ge(sem("tables_in"), 64)
            mm(PS[0:SH, 3, 0:NREL], RTB[0:BUCKETS, :], ROH[0:BUCKETS, 0:NREL], start=True, stop=True).then_inc(sem("rel_mm"), 1)
            for ch in range(18):
                n = U_SIN + ch // 4
                if ch % 4 == 0:
                    full(pe, n)
                if ch == 3:
                    pe.wait_ge(sem("rel_vec"), 1)
                if ch >= 4:
                    pe.wait_ge(sem("chunk_out"), ch - 3 + 24)
                for k in range(KC):
                    ins = mm(bank(ch % 4, T), W(n, 512)[:, k, (ch % 4) * P:(ch % 4 + 1) * P], HT[:, k, :],
                             start=k == 0, stop=k == KC - 1)
                if ch % 4 == 3:
                    used(ins, n)
                else:
                    ins.then_inc(sem("chunk_mm"), 1)
            for i, (n, a, w, tot, b) in enumerate(((4, 256, 256, 512, 4), (5, 0, 512, 512, 6), (6, 0, 384, 384, 4))):
                full(pe, U_SIN + n)
                for t in range(TT):
                    if i == 2:
                        pe.wait_ge(sem("tok_out"), t + 1 + 4)
                    for k in range(KC):
                        ins = mm(bank(b + t, w), HT[:, k, t * P:(t + 1) * P], W(U_SIN + n, tot)[:, k, a:a + w],
                                 start=k == 0, stop=k == KC - 1)
                    if t == 0:
                        ins.then_inc(sem("tok_mm"), 1)
                used(ins, U_SIN + n)
            pe.wait_ge(sem("chunk_out"), 18 + 24)
            pe.wait_ge(sem("tok_out"), 6 + 4)

            for h in range(SH + 2):
                if h < SH:
                    lo = 64 * (h % 2)
                    if h >= 2:
                        pe.wait_ge(sem("s_biased"), 2 * (h - 1))
                    for t in range(TT):
                        ins = mm(pair(h % 2, T)[:, t], SQKT[lo:lo + 64, h // 2, t * P:(t + 1) * P],
                                 SQKT[lo:lo + 64, 9 + h // 2, :], start=True, stop=True)
                    ins.then_inc(sem("scores_mm"), 1)
                if 1 <= h <= SH:
                    g = h - 1
                    pe.wait_ge(sem("exp_done"), 2 * (g + 1))
                    if g >= 2:
                        pe.wait_ge(sem("pt_out"), g - 1)
                    for t in range(TT):
                        for kt in range(TT):
                            ins = nc.tensor.transpose(pair(2 + g % 2, T)[:, kt, t * P:(t + 1) * P],
                                                      SP_[:, (g % 2) * 2 + t, kt * P:(kt + 1) * P], ident)
                    ins.then_inc(sem("p_turned"), 1)
                if h >= 2:
                    g = h - 2
                    pe.wait_ge(sem("pt_out"), g + 1)
                    if g >= 2:
                        pe.wait_ge(sem("s_o_out"), g - 1)
                    for t in range(TT):
                        for kt in range(TT):
                            ins = mm(PS[:, 4 + g % 2, t * SE:(t + 1) * SE], SPT2[:, g % 2, kt, t * P:(t + 1) * P],
                                     SV[:, kt, g * SE:(g + 1) * SE], start=kt == 0, stop=kt == 1)
                    ins.then_inc(sem("s_pv"), 1)
            pe.wait_ge(sem("y_ready"), 2 + 2)
            for cc in range(9):
                for t in range(TT):
                    ins = nc.tensor.transpose(pair(cc // 2, P)[:, (cc % 2) * 2 + t], SO[:, t, cc * P:(cc + 1) * P], RJ)
            ins.then_inc(sem("y_turned"), 1)
            pe.wait_ge(sem("y_back"), 5 + 4)
            for u in range(3):
                rows_product(U_SOUT + u, 0, SOT[:, 4 * u:min(4 * u + 4, 9), :], u == 0, u == 2)
            norm(3)
            normed(3)
            mlp(1)
            if stop == "b1":
                return

            with pe.Fori(0, NL) as L:
                tu = L * SEC_TURNS
                u2 = U_SEC
                norm(L * 2 + 4)
                normed(L * 2 + 4)

                def tok(n, w, b, name, a=0):
                    full(pe, u2 + n, tu)
                    for t in range(TT):
                        for k in range(KC):
                            ins = mm(bank(b + t, w), HT[:, k, t * P:(t + 1) * P], W(u2 + n, w)[:, k, :],
                                     start=k == 0, stop=k == KC - 1)
                        if t == 0:
                            ins.then_inc(sem(name), 1)
                    used(ins, u2 + n)

                def feat(n, b):
                    full(pe, u2 + n, tu)
                    for ch in range(4):
                        for k in range(KC):
                            ins = mm(pair(b + ch // 2, T)[:, ch % 2], W(u2 + n, 512)[:, k, ch * P:(ch + 1) * P], HT[:, k, :],
                                     start=k == 0, stop=k == KC - 1, skip_group_check=True)
                    used(ins, u2 + n)

                tok(V_CQ, QR, 0, "cq_mm")
                tok(V_KV, C_PU - QR, 2, "kv_mm")
                tok(V_PU, 512, 4, "pu_mm")
                feat(V_CX, 6)
                pe.wait_ge(sem("ckv_out"), L + 1)
                pe.wait_ge(sem("sq2"), L + 1)
                feat(V_CC, 0)
                feat(V_CB, 2)
                pe.wait_ge(sem("cqn_ready"), L + 1)
                pe.wait_ge(sem("pu_out"), L + 1)
                pe.wait_ge(sem("cx_out"), L + 1)
                for cc in range(5):
                    for t in range(TT):
                        ins = nc.tensor.transpose(pair(4 + cc // 2, P)[:, (cc % 2) * 2 + t], CQ[:, t, cc * P:(cc + 1) * P], ident)
                ins.then_inc(sem("cqt_mm"), 1)
                pe.wait_ge(sem("tables_in"), 16 + 64)
                for g in range(4):
                    if g == 2:
                        pe.wait_ge(sem("mix_out"), L * 2 + 1)
                    for tt in range(TT):
                        ins = mm(pair(7, T)[:, g % 2], PU[:, tt, g * P:(g + 1) * P], POOLM[:, tt, g, :],
                                 start=tt == 0, stop=tt == 1, skip_group_check=True)
                    if g % 2 == 1:
                        ins.then_inc(sem("mix_mm"), 1)
                pe.wait_ge(sem("cqt_out"), L * 5 + 5)
                pe.wait_ge(sem("mix_out"), L * 2 + 2)
                full(pe, u2 + V_UQ, tu)
                for t in range(TT):
                    for h in range(2):
                        for k in range(3):
                            ins = mm(bank(4 + 2 * t + h, 384), CQT[:, k, t * P:(t + 1) * P], W(u2 + V_UQ, 768)[:, k, h * 384:(h + 1) * 384],
                                     start=k == 0, stop=k == 2)
                used(ins, u2 + V_UQ)
                full(pe, u2 + V_UKV, tu)
                pe.wait_ge(sem("conv_y"), L + 1)
                for t in range(TT):
                    for h in range(2):
                        for k in range(2):
                            ins = mm(bank(2 * t + h), CQT[:, 3 + k, t * P:(t + 1) * P], W(u2 + V_UKV, D)[:, k, h * 512:(h + 1) * 512],
                                     start=k == 0, stop=k == 1)
                used(ins, u2 + V_UKV)
                for j, src in enumerate((MQ, MK)):
                    if j == 0:
                        pe.wait_ge(sem("mq_ready"), L + 1)
                    else:
                        pe.wait_ge(sem("mk_ready"), L * 4 + 4)
                    if j == 1:
                        pe.wait_ge(sem("mv_out"), L + 1)
                    for g in range(4):
                        b = (4 if j == 0 else 0) + g
                        for hh in range(2):
                            for t in range(TT):
                                ins = nc.tensor.transpose(pair(b, P)[0:DQK, hh * 2 + t], src[:, t, 2 * g + hh, :], ident)
                        ins.then_inc(sem("mqk_mm"), 1)
                pe.wait_ge(sem("mqk_out"), L * 8 + 8)
                for h in range(MH + 2):
                    if h < MH:
                        if h >= 2:
                            pe.wait_ge(sem("exp_done"), L * 16 + 2 * (h - 1) + 2 * SH)
                        for t in range(TT):
                            ins = mm(pair(h % 2, T)[:, t], QT[0:DQK, h, t * P:(t + 1) * P], KT[0:DQK, h, :], start=True, stop=True)
                        ins.then_inc(sem("scores_mm"), 1)
                    if 1 <= h <= MH:
                        g = h - 1
                        pe.wait_ge(sem("m_p"), L * 8 + g + 1)
                        if g >= 2:
                            pe.wait_ge(sem("pt_out"), L * 8 + g - 1 + SH)
                        for t in range(TT):
                            for kt in range(TT):
                                ins = nc.tensor.transpose(pair(2 + g % 2, T)[:, kt, t * P:(t + 1) * P],
                                                          (MP, MP2)[g % 2][:, t, kt * P:(kt + 1) * P], ident)
                        ins.then_inc(sem("p_turned"), 1)
                    if h >= 2:
                        g = h - 2
                        pe.wait_ge(sem("pt_out"), L * 8 + g + 1 + SH)
                        lo = 64 * (g % 2)
                        for kt in range(TT):
                            ins = mm(pair(4 + g // 4, T)[lo:lo + 64, (g // 2) % 2], MV[:, kt, g, :], MPT[g % 2][:, kt, :],
                                     start=kt == 0, stop=kt == 1, skip_group_check=True)
                        if g % 4 == 3:
                            ins.then_inc(sem("m_pv"), 1)
                pe.wait_ge(sem("ot_out"), L * 2 + 2)
                full(pe, u2 + V_OA, tu)
                for q in range(24):
                    b, dc = q // 8, q % 8
                    ng = u2 + V_GL[q // 4]
                    if q % 4 == 0:
                        full(pe, ng, tu)
                    if q == 16:
                        full(pe, u2 + V_OC, tu)
                    if q >= 2:
                        pe.wait_ge(sem("gate_out"), L * 24 + q - 1)
                        pe.wait_ge(sem("merge"), L * 24 + q - 1)
                    for k in range(KC):
                        ins = mm(bank(q % 2, T), W(ng, 512)[:, k, (dc % 4) * P:(dc % 4 + 1) * P], HT[:, k, :],
                                 start=k == 0, stop=k == KC - 1)
                    if q % 4 == 3:
                        used(ins, ng)
                    else:
                        ins.then_inc(sem("gate_mm"), 1)
                    o = bank(2 + q % 2, T)
                    if b == 1:
                        pe.wait_ge(sem("side_in"), L * 32 + 32)
                        mm(o, WPOOL[:, dc // 2, (dc % 2) * P:(dc % 2 + 1) * P], MIXT[:, dc // 2, :],
                           start=True, stop=True).then_inc(sem("branch_mm"), 1)
                    else:
                        wu = u2 + (V_OA if b == 0 else V_OC)
                        for k in range(4):
                            ins = mm(o, W(wu, D)[:, k, dc * P:(dc + 1) * P], (OT, BCT)[b // 2][:, k, :], start=k == 0, stop=k == 3)
                        if dc == 7:
                            used(ins, wu)
                        else:
                            ins.then_inc(sem("branch_mm"), 1)

                def spread(ins_col, b, name):
                    for dc in range(KC):
                        ins = mm(pair(b + dc // 4, P)[:, dc % 4], GCOL[:, ins_col + dc:ins_col + dc + 1].to_broadcast([P, P]), ident,
                                 start=True, stop=True, skip_group_check=True)
                    ins.then_inc(sem("spread"), 1)

                pe.wait_ge(sem("gcol"), L + 1)
                spread(0, 4, "g1")
                pe.wait_ge(sem("merge"), L * 24 + 24)
                for u in range(2):
                    rows_product(u2 + V_OUT + u, tu, MG[:, 4 * u:4 * u + 4, :], u == 0, u == 1)

                norm(L * 2 + 5)
                normed(L * 2 + 5)
                for t in range(TT):
                    for k in range(KC):
                        ins = mm(PS[:, 4, t * NE:(t + 1) * NE], HT[:, k, t * P:(t + 1) * P], WR[:, k, :], start=k == 0, stop=k == KC - 1)
                ins.then_inc(sem("router_mm"), 1)
                pe.wait_ge(sem("aff_ready"), L + 1)
                for t in range(TT):
                    ins = nc.tensor.transpose(PS[0:NE, 5, t * P:(t + 1) * P], AFF[:, t, :], ident)
                ins.then_inc(sem("aff_turned"), 1)
                pe.wait_ge(sem("bd_ready"), L + 1)
                for j in range(2):
                    ins = mm(bank(6 + j), ones[0:NE, :], BD[0:NE, j, :], start=True, stop=True)
                ins.then_inc(sem("picks_mm"), 1)
                pe.wait_ge(sem("st_ready"), L + 1)
                for dc in range(KC):
                    if dc >= 4:
                        pe.wait_ge(sem(f"xg_out{dc % 2}"), L * 4 + (dc - 4) // 2 + 1)
                    for t in range(TT):
                        ins = mm(bank(dc % 4), XN[:, t, dc * P:(dc + 1) * P], ST[:, t, :], start=t == 0, stop=t == 1)
                    ins.then_inc(sem("xg_mm"), 1)
                pe.wait_ge(sem("xg_out0"), L * 4 + 4)
                pe.wait_ge(sem("xg_out1"), L * 4 + 4)
                pe.wait_ge(sem("filled"), 1)
                for b in range(4):
                    mm(bank(b), zero1.to_broadcast([P, P]), zero1.to_broadcast([P, 512]), start=True, stop=False, skip_group_check=True)
                with pe.Fori(0, NE) as e:
                    te = tu + e
                    v = u2 + V_MOE
                    ev = L * NE + e
                    pe.wait_ge(sem("xge_ready"), ev + 1)
                    pe.wait_ge(sem("ys_out"), ev * 2 + 1)
                    for m in range(2):
                        if m == 1:
                            pe.wait_ge(sem("he_ready"), ev + 1)
                        for u in range(2):
                            full(pe, v + 2 * m + u, te)
                            for kk in range(4):
                                for j in range(4):
                                    ins = mm(PS[32 * j:32 * j + 32, 4 + m, 0:T], XGE[:, 4 * u + kk, :],
                                             W(v + 2 * m + u, D)[:, kk, j * T:(j + 1) * T],
                                             start=u == 0 and kk == 0, stop=u == 1 and kk == 3, tile_position=(0, 32 * j),
                                             skip_group_check=True)
                            used(ins, v + 2 * m + u)
                    pe.wait_ge(sem("srep_ready"), ev + 1)
                    for t in range(TT):
                        ins = nc.tensor.transpose(PS[:, 6, T + t * P:T + (t + 1) * P], SREP[:, t].rearrange("p a b -> p (a b)"), ident)
                    ins.then_inc(sem("s4_mm"), 1)
                    pe.wait_ge(sem("s4_out"), ev + 1)
                    pe.wait_ge(sem("he_ready"), ev + 1 + 1)
                    for cc in range(2):
                        ins = nc.tensor.transpose(PS[:, 6, cc * P:(cc + 1) * P], HE[:, cc * P:(cc + 1) * P], ident)
                    ins.then_inc(sem("hte_mm"), 1)
                    pe.wait_ge(sem("hte_out"), ev + 1)
                    for u in range(2):
                        full(pe, v + 4 + u, te)
                        yb = (7, 4)[u]
                        for cc in range(2):
                            for j in range(4):
                                ins = mm(PS[32 * j:32 * j + 32, yb, :], HTE[:, cc, 32 * j:32 * j + 32], W(v + 4 + u, 512)[:, 2 * j + cc, :],
                                         start=cc == 0, stop=cc == 1, tile_position=(0, 32 * j), skip_group_check=True)
                        used(ins, v + 4 + u)
                    for u in range(2):
                        pe.wait_ge(sem("ys_out"), ev * 2 + u + 1 + 1)
                        for t in range(TT):
                            ins = mm(bank(2 * t + u), S4[:, t * P:(t + 1) * P], YS[:, u, :], start=False, stop=False, skip_group_check=True)
                    ins.then_inc(sem("expert_done"), 1)
                spread(8, 6, "g2")

        @block.vector
        def _(dve):
            v = nc.vector
            settle = v.drain

            def bc(ap, n):
                return ap.unsqueeze(2).to_broadcast([ap.shape[0], ap.shape[1], n])

            def bm(ap, n):
                return ap.unsqueeze(1).to_broadcast([ap.shape[0], n, ap.shape[1]])

            def mean_square(r):
                v.tensor_tensor_reduce(out=XN[:, 1, :], in0=X[:, 1, :], in1=X[:, 1, :], scale=1.0, scalar=0.0,
                                       op0=ALU.mult, op1=ALU.add, accum_out=ssq[:, 1:2])
                settle()
                dve.wait_ge(sem("ssq_act"), r + 1)
                v.tensor_scalar(var[:], ssq[:], 1.0 / D, EPS, ALU.mult, ALU.add).then_inc(sem("var_ready"), 1)
                dve.wait_ge(sem("rstd_ready"), r + 1)

            def norm(r, j, scale, shift=None):
                mean_square(r)
                v.tensor_scalar(XN[:, 1, :], X[:, 1, :], rstd[:, 1:2], None, ALU.mult).then_inc(sem("xn1"), 1)
                dve.wait_ge(sem("ht_psum"), j + 1)
                for dc in range(4, KC):
                    src = pair(4 + dc // 2, T)[:, dc % 2]
                    if shift is None:
                        ins = v.tensor_scalar(HT[:, dc, :], src, scale(dc), None, ALU.mult)
                    else:
                        ins = v.tensor_scalar(HT[:, dc, :], src, scale(dc), shift(dc), ALU.mult, ALU.add)
                    ins.then_inc(sem("ht_ready"), 1)

            def residual():
                for b in range(4):
                    t, h = b // 2, b % 2
                    xs = X[:, t, h * 512:(h + 1) * 512]
                    ins = v.tensor_tensor(xs, bank(b), xs, ALU.add)
                ins.then_inc(sem("x_ready"), 1)

            dve.wait_ge(sem("x_in"), 16)
            dve.wait_ge(sem("cols_psum"), 1)
            dve.wait_ge(sem("cols_ready"), 4)
            norm(0, 0, lambda dc: colof("norm_mix", dc))
            dve.wait_ge(sem("filled"), 1)

            def conv(ch):
                dve.wait_ge(sem("chunk_out"), ch + 1)
                if ch >= 3:
                    dve.wait_ge(sem("silu"), ch - 2)
                if ch - 3 >= 16:
                    dve.wait_ge(sem("turned"), ch - 2)
                x, y = CP[:, ch % 3, :], CV[:, ch % 3, :]
                tap = lambda k: colof("gdn_conv_w", 24 * k + ch)
                v.tensor_scalar(y, x[:, 0:T], tap(0), None, ALU.mult)
                for k in range(1, 5):
                    settle()
                    ins = v.scalar_tensor_tensor(y, x[:, k:k + T], tap(k), y, ALU.mult, ALU.add)
                ins.then_inc(sem("conv_out"), 1)

            def to_tokens(ch):
                dve.wait_ge(sem("turned"), ch + 1)
                dst = KN[:, ch - GH] if ch < 2 * GH else V[:, ch - 2 * GH]
                v.tensor_copy(dst, pair(4 + ch % 2, P)[:, 0:2]).then_inc(sem("tok_done"), 1)

            for ch in range(24):
                conv(ch)
                if ch - 3 >= GH:
                    to_tokens(ch - 3)
            for ch in (21, 22, 23):
                to_tokens(ch)
            dve.wait_ge(sem("gdn_in"), 16 * 8)
            v.tensor_copy(marks[:], MSTAGE)
            spent(dve, U_AB)
            ab = PS[:, 6, 0:64].rearrange("p (t c) -> p t c", c=32)
            s2 = [SPT[:, i, :].rearrange("p (t c) -> p t c", c=16) for i in range(6)]
            v.tensor_tensor(s2[0], ab[:, :, 0:16], bm(DTB, 2), ALU.add)
            settle()
            v.scalar_tensor_tensor(s2[1], s2[0], -1.0, s2[0], ALU.mult, ALU.min).then_inc(sem("decay_in"), 1)
            dve.wait_ge(sem("sq_done"), 16)
            v.tensor_scalar(RQK, RQK, 1e-6, None, ALU.add).then_inc(sem("gdn_ms"), 1)
            dve.wait_ge(sem("gdn_rs"), 1)
            for t in range(TT):
                ins = v.tensor_tensor(KN[:, :, t, :], KN[:, :, t, :], bc(RQV[:, t, 8:16], P), ALU.mult)
            ins.then_inc(sem("kn_ready"), 1)
            dve.wait_ge(sem("decay_out"), 1)
            v.scalar_tensor_tensor(s2[5], s2[0], 0.0, s2[3], ALU.max, ALU.add)
            v.tensor_scalar(s2[4], s2[4], 1.0, None, ALU.add)
            settle()
            v.reciprocal(BT, s2[4])
            v.scalar_tensor_tensor(GS, s2[5], -1.0, bm(ALOG, 2), ALU.mult, ALU.mult)
            settle()
            v.tensor_copy(TOT[:, 0, 0, 0:1], GS[:, 0, 0:1]).then_inc(sem("gs_ready"), 1)
            for u in range(2):
                for t in range(TT):
                    dve.wait_ge(sem("z_act"), 2 * u + t + 1)
                    z = Z[:, t, u * 512:(u + 1) * 512].rearrange("p (a b) -> p a b", b=P)
                    v.tensor_tensor(z, z, bm(NW, 4), ALU.mult).then_inc(sem("tok_out"), 1)
            dve.wait_ge(sem("cum_mm"), 1)
            flat = lambda a: a.rearrange("p a b c -> p (a b c)")
            v.tensor_copy(flat(GC), PS[:, 7, 0:32])
            settle()
            v.tensor_tensor(flat(KD_S), PS[:, 7, 32:64], flat(GC), ALU.subtract).then_inc(sem("decay_in"), 1)
            dve.wait_ge(sem("decay_out"), 1 + 1)

            masks = marks[:].rearrange("p (w s i) -> p w s i", w=2, s=7)
            for it in range(4):
                d, hg = it // 2, (it % 2) * 4
                fst, snd = (0, 1) if d == 0 else (1, 0)
                hs = slice(hg, hg + 4)
                for l in range(2):
                    dve.wait_ge(sem("core_setup"), 2 * it + l + 1)
                    for h in range(4):
                        ins = v.scalar_tensor_tensor(lanes[l]["DT"][:, h], pair(3 * l, P)[:, h], GC[:, d, l, hg + h:hg + h + 1],
                                                     NEGM[:, d, :], ALU.subtract, ALU.add)
                    ins.then_inc(sem("dt_in"), 1)
                    v.tensor_copy(lanes[l]["U"], bm(ident, 4))
                v.tensor_tensor(R1, V[:, hs, fst, :], bc(BT[:, fst, d * 8 + hg:d * 8 + hg + 4], P), ALU.mult).then_inc(sem("r1_ready"), 1)
                for l in range(2):
                    dve.wait_ge(sem("dt_out"), 2 * it + l + 1)
                    kd, dt = lanes[l]["KD"], lanes[l]["DT"]
                    for half, b in ((0, 3 * l + 2), (2, 6 + l)):
                        v.tensor_tensor(kd[:, half:half + 2], PS[:, b, :].rearrange("p (a b c) -> p a b c", a=2, b=2),
                                        dt[:, half:half + 2].unsqueeze(2).to_broadcast([P, 2, 2, P]), ALU.mult)
                    settle()
                    v.scalar_tensor_tensor(kd[:, :, 0], kd[:, :, 0], -1.0, pair(3 * l + 1, P), ALU.mult, ALU.mult)
                    settle()
                    v.copy_predicated(lanes[l]["U"], bm(masks[:, 1 - d, 0], 4), kd[:, :, 0]).then_inc(sem("u_init"), 1)
                for q in range(nlev_):
                    for l in range(2):
                        if q < nlev_ - 1:
                            dve.wait_ge(sem("q_mm"), (it * 5 + q) * 2 + l + 1)
                            v.copy_predicated(lanes[l]["Tm"], bm(masks[:, d, q + 1], 4), pair(3 * l + 1, P)).then_inc(sem("t_grown"), 1)
                        dve.wait_ge(sem("r_mm"), (it * nlev_ + q) * 2 + l + 1)
                        v.copy_predicated(lanes[l]["U"], bm(masks[:, 1 - d, q + 1], 4), pair(3 * l + 2, P)).then_inc(sem("u_grown"), 1)
                v.tensor_tensor(lanes[fst]["Tm"], KN[:, hs, fst, :], bc(KD_S[:, d, fst, hs], P), ALU.mult).then_inc(sem("kdec"), 1)
                dve.wait_ge(sem("o_mm"), 2 * it + 1)
                o = O_ACC[:, fst, hs]
                if d == 0:
                    v.tensor_copy(o, pair(2, P))
                else:
                    v.tensor_tensor(o, pair(2, P), o, ALU.add)
                dve.wait_ge(sem("ks_mm"), it + 1)
                eg = bc(EG[:, d, snd, hs], P)
                v.tensor_tensor(R1, pair(0, P), eg, ALU.mult)
                settle()
                v.tensor_tensor(R1, V[:, hs, snd, :], R1, ALU.subtract)
                settle()
                v.tensor_tensor(R1, R1, bc(BT[:, snd, d * 8 + hg:d * 8 + hg + 4], P), ALU.mult).then_inc(sem("r1_ready"), 1)
                qs = lanes[snd]["Tm"]
                v.tensor_tensor(qs, pair(1, P), eg, ALU.mult)
                settle()
                dve.wait_ge(sem("o_mm"), 2 * it + 2)
                o = O_ACC[:, snd, hs]
                if d == 0:
                    v.tensor_tensor(o, pair(7, P), qs, ALU.add).then_inc(sem("core_done"), 1)
                else:
                    v.tensor_tensor(qs, pair(7, P), qs, ALU.add)
                    settle()
                    v.tensor_tensor(o, o, qs, ALU.add).then_inc(sem("core_done"), 1)
            settle()
            oa = O_ACC.rearrange("p t h e -> p (t h e)")
            v.tensor_tensor(GJUNK, oa, oa, ALU.mult)
            settle()
            rq, so, pw, fac = s2[0].rearrange("p a b -> p (a b)"), s2[1].rearrange("p a b -> p (a b)"), SPT[:, 2, :], SPT[:, 3, :]
            v.tensor_reduce(so[:, 0:16], GJUNK.rearrange("p (a e) -> p a e", e=P), AX, ALU.add)
            v.tensor_scalar(rq[:, 0:16].rearrange("p (t h) -> p t h", h=8), RQV[:, :, 0:8], P ** -0.5, None, ALU.mult)
            settle()
            v.tensor_tensor(so[:, 0:16], so[:, 0:16], rq[:, 0:16], ALU.mult)
            settle()
            v.tensor_tensor(so[:, 0:16], so[:, 0:16], rq[:, 0:16], ALU.mult)
            settle()
            v.tensor_scalar(so[:, 0:16], so[:, 0:16], 1.0 / P, EPS, ALU.mult, ALU.add).then_inc(sem("gdn_ms"), 1)
            dve.wait_ge(sem("gdn_rs"), 1 + 1)
            v.tensor_tensor(fac[:, 0:16], pw[:, 0:16], rq[:, 0:16], ALU.mult)
            settle()
            for t in range(TT):
                y = XN[:, t, :].rearrange("p (h e) -> p h e", e=P)
                v.tensor_tensor(y, O_ACC[:, t], bc(fac[:, t * 8:(t + 1) * 8], P), ALU.mult)
                settle()
                v.tensor_tensor(XN[:, t, :], XN[:, t, :], Z[:, t, :], ALU.mult).then_inc(sem("y_ready"), 1)
            dve.wait_ge(sem("y_turned"), 1)
            for i in (2, 3):
                v.tensor_copy(HT[:, 2 * i:2 * i + 2, :], pair(3 + i, T)).then_inc(sem("y_back"), 1)
            spent(dve, U_GOUT + 1)
            residual()
            if stop == "gdn":
                return

            def mlp(l):
                n0 = U_MLP[l]
                with dve.Fori(0, 2) as i:
                    for j in range(3):
                        turns = i * MLP_TURNS
                        m = i * 3 + j
                        dve.wait_ge(sem("mod_mm"), m + 6 * l + 1)
                        for mi in range(2):
                            n = n0 + 3 + 4 * j + 2 + mi
                            full(dve, n, turns)
                            for k in range(KC):
                                w = W(n, 512)[:, k, :]
                                if k == 0:
                                    ins = v.tensor_scalar(MA[mi], w, CACT[:, 0:1], None, ALU.mult)
                                else:
                                    settle()
                                    ins = v.scalar_tensor_tensor(MA[mi], w, CACT[:, k:k + 1], MA[mi], ALU.mult, ALU.add)
                            ins.then_inc(w_free[n % RING], 1)
                        dve.wait_ge(sem("mod_mm"), m + 6 * l + 1 + 1)
                        v.tensor_tensor(MODC[:, l, bass.ds(m * 8, 8)], PS[:, 6, 0:8],
                                        COLS[:, bass.ds(m * 8 + (COL["b_mod_2"] + 48 * l), 8)], ALU.add).then_inc(sem("mod_out"), 1)
                spent(dve, n0 + 27)
                residual()

            dve.wait_ge(sem("cact"), 1)
            settle()
            norm(1, 1, lambda dc: colof("norm_mlp", dc))
            mlp(0)
            if stop == "mlp0":
                return

            settle()
            norm(2, 2, lambda dc: colof("norm_mix", 8 + dc))
            dve.wait_ge(sem("rel_mm"), 1)
            v.tensor_tensor(RV[0:SH, 0:NREL], PS[0:SH, 3, 0:NREL], RMK[0:SH, 0:NREL], ALU.add).then_inc(sem("rel_vec"), 1)
            for i, (n, w, at, b) in enumerate(((4, 256, 0, 4), (5, 512, 256, 6), (6, 384, 768, 4))):
                for t in range(TT):
                    if t == 0:
                        dve.wait_ge(sem("tok_mm"), i + 1 + 2)
                    else:
                        spent(dve, U_SIN + n)
                    v.tensor_copy(SV[:, t, at:at + w], bank(b + t, w)).then_inc(sem("tok_out"), 1)
            for h in range(SH + 2):
                if h < SH:
                    dve.wait_ge(sem("scores_mm"), h + 1)
                    dve.wait_ge(sem(f"tz_in{h % 2}"), 16 * (h // 2 + 1))
                    if h >= 2:
                        dve.wait_ge(sem("p_turned"), h - 1)
                    for t in range(TT):
                        v.tensor_tensor_reduce(out=SP_[:, (h % 2) * 2 + t, :], in0=pair(h % 2, T)[:, t],
                                               in1=TZ[:, h % 2, P * (1 - t):P * (1 - t) + T], scale=1.0, scalar=-3e38,
                                               op0=ALU.add, op1=ALU.max, accum_out=MX[:, t, h:h + 1]).then_inc(sem("s_biased"), 1)
                    settle()
                    v.tensor_scalar(NMX[:, :, h], MX[:, :, h], -1.0, None, ALU.mult).then_inc(sem("row_max"), 1)
                if h >= 2:
                    g = h - 2
                    dve.wait_ge(sem("s_pv"), g + 1)
                    v.tensor_copy(SO[:, :, g * SE:(g + 1) * SE], pair(4 + g % 2, SE)[:, 0:2]).then_inc(sem("s_o_out"), 1)
            dve.wait_ge(sem("exp_done"), 2 * SH)
            by_group = lambda a: a.rearrange("p t (g j) -> p t j g", g=3)
            v.tensor_reduce(MM, by_group(MX), AX, ALU.max)
            settle()
            for g in range(3):
                js = slice(g * SGRP, (g + 1) * SGRP)
                ins = v.tensor_tensor(SS[:, :, js], MX[:, :, js], MM, ALU.subtract)
            ins.then_inc(sem("angle_in"), 1)
            dve.wait_ge(sem("angle_out"), 1)
            v.tensor_tensor(SS, SM, SC, ALU.mult)
            settle()
            v.tensor_reduce(DEN, by_group(SS), AX, ALU.add)
            settle()
            v.reciprocal(DEN, DEN)
            settle()
            for g in range(3):
                js = slice(g * SGRP, (g + 1) * SGRP)
                v.tensor_tensor(SC[:, :, js], SC[:, :, js], DEN, ALU.mult)
            settle()
            for t in range(TT):
                o = SO[:, t, :].rearrange("p (h e) -> p h e", e=SE)
                v.tensor_tensor(o, o, bc(SC[:, t, :], SE), ALU.mult).then_inc(sem("y_ready"), 1)
            dve.wait_ge(sem("y_turned"), 1 + 1)
            for i in (1, 3):
                v.tensor_copy(SOT[:, 2 * i:2 * i + 2, :], pair(i, T)).then_inc(sem("y_back"), 1)
            spent(dve, U_SOUT + 2)
            residual()
            settle()
            norm(3, 3, lambda dc: colof("norm_mlp", 8 + dc))
            mlp(1)
            settle()
            mean_square(4)
            dve.wait_ge(sem("fgr_in"), 16)
            for t in range(TT):
                ins = v.scalar_tensor_tensor(X[:, t, :], X[:, t, :], rstd[:, t:t + 1], FGR, ALU.mult, ALU.mult)
            ins.then_inc(sem("x_ready"), 1)
            settle()
            if stop == "b1":
                return

            TWO_PI = 2.0 * math.pi
            c1 = 6.28125
            c2_ = 0.0019350051879882812
            c3 = TWO_PI - c1 - c2_
            BIG = 12582912.0
            v.tensor_copy(POSF, POSI[:])
            settle()
            for t in range(TT):
                v.tensor_scalar(ANG[:, t, :], freq, POSF[:, t:t + 1], None, ALU.mult)
            settle()
            v.tensor_scalar(KRD, ANG, 1.0 / TWO_PI, BIG, ALU.mult, ALU.add)
            settle()
            v.tensor_scalar(KRD, KRD, BIG, None, ALU.subtract)
            settle()
            for cst in (c1, c2_, c3):
                v.scalar_tensor_tensor(ANG, KRD, -cst, ANG, ALU.mult, ALU.add)
                settle()
            v.tensor_scalar(COS, ANG, math.pi / 2, None, ALU.add)
            settle()
            v.tensor_scalar(KRD, COS, math.pi, None, ALU.is_gt)
            settle()
            v.scalar_tensor_tensor(COS, KRD, -TWO_PI, COS, ALU.mult, ALU.add)
            settle()
            lim = 3.1415925
            v.tensor_scalar(COS, COS, lim, -lim, ALU.min, ALU.max)
            v.tensor_scalar(ANG, ANG, lim, -lim, ALU.min, ALU.max).then_inc(sem("angle_in"), 1)
            dve.wait_ge(sem("angle_out"), 1 + 1)

            def rotate(x1, x2, t, shape):
                cs, sn = COS[:, t, :], SIN[:, t, :]
                r = [RT[:, i, 0:16] if shape is None else RT[:, i, :].rearrange("p (h e) -> p h e", e=16) for i in range(4)]
                if shape is not None:
                    cs, sn = bm(cs, shape), bm(sn, shape)
                v.tensor_tensor(r[0], x1, cs, ALU.mult)
                v.tensor_tensor(r[1], x2, sn, ALU.mult)
                v.tensor_tensor(r[2], x1, sn, ALU.mult)
                v.tensor_tensor(r[3], x2, cs, ALU.mult)
                settle()
                v.tensor_tensor(x1, r[0], r[1], ALU.subtract)
                ins = v.tensor_tensor(x2, r[2], r[3], ALU.add)
                settle()
                return ins

            def gated_residual(n):
                dve.wait_ge(sem("gr_out"), n)
                for b in range(4):
                    t, h = b // 2, b % 2
                    xs = X[:, t, h * 512:(h + 1) * 512]
                    v.tensor_tensor(TMP, bank(b), GR[:, h * 512:(h + 1) * 512], ALU.mult)
                    settle()
                    ins = v.tensor_tensor(xs, xs, TMP, ALU.add)
                    if b < 3:
                        settle()
                ins.then_inc(sem("x_ready"), 1)
                settle()

            with dve.Fori(0, NL) as L:
                tu = L * SEC_TURNS
                u2 = U_SEC
                mc = lambda k: MODC[:].rearrange("p l c -> p (l c)")[:, bass.ds(L * 48 + k * 8, 8)]
                pc = lambda name, w: COLS[:, bass.ds(L * w + COL[name], w)]
                v.scalar_tensor_tensor(SCL, mc(1), 1.0, pc("norm1_g_2", 8), ALU.add, ALU.mult)
                v.tensor_copy(BIA, mc(0))
                v.tensor_copy(GCOL[:, 0:8], mc(2))
                v.tensor_copy(GCOL[:, 8:16], mc(5))
                v.tensor_copy(PSC, pc("pool_scale_2", 8))
                v.tensor_copy(BG, pc("b_gate_2", 24))
                v.tensor_copy(CW, pc("conv_w_2", 12))
                v.tensor_copy(QKG[:, 0:3], pc("q_norm_g_2", 3))
                v.tensor_copy(QKG[:, 3:5], pc("kv_norm_g_2", 2))
                settle()
                v.memset(CZ[:, :, 0:1], 0.0)
                v.memset(CZ[:, :, 257:258], 0.0).then_inc(sem("gcol"), 1)
                norm(L * 2 + 5, L * 2 + 4, lambda dc: SCL[:, dc:dc + 1], lambda dc: BIA[:, dc:dc + 1])
                for t in range(TT):
                    if t == 0:
                        dve.wait_ge(sem("cq_mm"), L + 1)
                    else:
                        spent(dve, u2 + V_CQ, tu)
                    v.tensor_copy(CQ[:, t, 0:QR], bank(t, QR)).then_inc(sem("cq_out"), 1)
                for t in range(TT):
                    if t == 0:
                        dve.wait_ge(sem("kv_mm"), L + 1)
                    else:
                        spent(dve, u2 + V_KV, tu)
                    v.tensor_copy(CQ[:, t, QR:QKW], bank(2 + t, KVR)).then_inc(sem("cq_out"), 1)
                    ins = v.tensor_copy(KR[:, t, :], PS[:, 2 + t, KVR:KVR + ROPE])
                ins.then_inc(sem("ckv_out"), 1)
                dve.wait_ge(sem("sq2"), L + 1)
                v.tensor_scalar(VAR2[:, 0:2], SS2[:, 0:2], 1.0 / QR, EPS, ALU.mult, ALU.add)
                v.tensor_scalar(VAR2[:, 2:4], SS2[:, 2:4], 1.0 / KVR, EPS, ALU.mult, ALU.add).then_inc(sem("var2"), 1)
                dve.wait_ge(sem("rs2"), L + 1)
                for t in range(TT):
                    v.tensor_scalar(CQ[:, t, 0:QR], CQ[:, t, 0:QR], RS2[:, t:t + 1], None, ALU.mult)
                    ins = v.tensor_scalar(CQ[:, t, QR:QKW], CQ[:, t, QR:QKW], RS2[:, 2 + t:3 + t], None, ALU.mult)
                ins.then_inc(sem("cqn_ready"), 1)
                for t in range(TT):
                    rotate(KR[:, t, 0:16], KR[:, t, 16:32], t, None)
                    v.tensor_copy(MK[:, t, :, NOPE:DQK], bm(KR[:, t, :], MH))
                dve.wait_ge(sem("cx_out"), L + 1)
                spent(dve, u2 + V_CC, tu)
                for b in range(2):
                    v.tensor_tensor(CZ[:, 2 * b:2 * b + 2, 1:257], pair(b, T), CX[:, 2 * b:2 * b + 2, :], ALU.mult)
                settle()
                for ch in range(4):
                    v.tensor_scalar(BCT[:, ch, :], CZ[:, ch, 0:T], CW[:, ch:ch + 1], None, ALU.mult)
                for k in (1, 2):
                    settle()
                    for ch in range(4):
                        v.scalar_tensor_tensor(BCT[:, ch, :], CZ[:, ch, k:k + T], CW[:, 4 * k + ch:4 * k + ch + 1], BCT[:, ch, :],
                                               ALU.mult, ALU.add)
                settle()
                spent(dve, u2 + V_CB, tu)
                for b in range(2):
                    ins = v.tensor_tensor(BCT[:, 2 * b:2 * b + 2, :], pair(2 + b, T), BCT[:, 2 * b:2 * b + 2, :], ALU.mult)
                ins.then_inc(sem("conv_y"), 1)
                dve.wait_ge(sem("mq_raw"), L + 1)
                for t in range(TT):
                    rotate(MQ[:, t, :, NOPE:NOPE + 16], MQ[:, t, :, NOPE + 16:DQK], t, MH)
                v.tensor_copy(RT[:, 0, 0:1], MQ[:, 0, 0, NOPE:NOPE + 1]).then_inc(sem("mq_ready"), 1)
                spent(dve, u2 + V_UKV, tu)
                for b in range(4):
                    t, h = b // 2, b % 2
                    v.tensor_copy(MK[:, t, 4 * h:4 * h + 4, 0:NOPE], pair(b, P)[:, :, 0:NOPE]).then_inc(sem("mk_ready"), 1)
                for g in range(8):
                    if g % 2 == 1:
                        dve.wait_ge(sem("mqk_mm"), L * 8 + g + 1)
                        dst, b = (QT, 4 + g) if g < 4 else (KT, g - 4)
                        gg = g % 4
                        v.tensor_copy(dst[0:DQK, 2 * gg:2 * gg + 2, :], pair(b, T)[0:DQK]).then_inc(sem("mqk_out"), 1)
                for h in range(MH + 1):
                    if h < MH:
                        dve.wait_ge(sem("scores_mm"), L * 8 + h + 1 + SH)
                        v.tensor_reduce(MNM[:, h, :], pair(h % 2, T), AX, ALU.max, negate=True).then_inc(sem("row_max"), 1)
                    if h >= 1:
                        g = h - 1
                        dve.wait_ge(sem("exp_done"), L * 16 + 2 * g + 2 + 2 * SH)
                        v.reciprocal(MSM[:, g, :], MSM[:, g, :])
                        settle()
                        for t in range(TT):
                            pt = (MP, MP2)[g % 2][:, t, :]
                            ins = v.tensor_scalar(pt, pt, MSM[:, g, t:t + 1], None, ALU.mult)
                        ins.then_inc(sem("m_p"), 1)
                dve.wait_ge(sem("m_pv"), L * 2 + 2)
                v.tensor_copy(OT[:, 2:4, :], pair(5, T)).then_inc(sem("ot_out"), 1)
                for q in range(24):
                    b, dc = q // 8, q % 8
                    dve.wait_ge(sem("gate_out"), L * 24 + q + 1)
                    if dc == 7 and b != 1:
                        spent(dve, u2 + (V_OA if b == 0 else V_OC), tu)
                    else:
                        dve.wait_ge(sem("branch_mm"), L * 22 + (0, 7, 15)[b] + dc + 1)
                    y, sg, mg, MTMP = bank(2 + q % 2, T), SG[:, q % 2, :], MG[:, dc, :], MT2[:, q % 2, :]
                    if b == 0:
                        v.tensor_tensor(mg, y, sg, ALU.mult).then_inc(sem("merge"), 1)
                    else:
                        if b == 1:
                            v.scalar_tensor_tensor(MTMP, y, PSC[:, dc:dc + 1], sg, ALU.mult, ALU.mult)
                        else:
                            v.tensor_tensor(MTMP, y, sg, ALU.mult)
                        settle()
                        v.tensor_tensor(mg, mg, MTMP, ALU.add).then_inc(sem("merge"), 1)
                spent(dve, u2 + V_OUT + 1, tu)
                gated_residual(L * 2 + 1)

                v.scalar_tensor_tensor(SCL, mc(4), 1.0, pc("norm2_g_2", 8), ALU.add, ALU.mult)
                v.tensor_copy(BIA, mc(3))
                settle()
                norm(L * 2 + 6, L * 2 + 5, lambda dc: SCL[:, dc:dc + 1], lambda dc: BIA[:, dc:dc + 1])
                dve.wait_ge(sem("router_mm"), L + 1)
                v.tensor_reduce(RM, PS[:, 4, 0:TT * NE].rearrange("p (t e) -> p t e", e=NE), AX, ALU.max, negate=True).then_inc(sem("rm"), 1)
                dve.wait_ge(sem("aff_exp"), L + 1)
                v.reciprocal(RIN, RSM)
                settle()
                for t in range(TT):
                    ins = v.tensor_scalar(AFF[:, t, :], AFF[:, t, :], RIN[:, t:t + 1], None, ALU.mult)
                ins.then_inc(sem("aff_ready"), 1)
                dve.wait_ge(sem("aff_turned"), L + 1)
                v.tensor_copy(AT[0:NE, :], PS[0:NE, 5, 0:T])
                cur, other = AT[0:NE, :], AT2[0:NE, :]
                for r in range(CAP // 8):
                    settle()
                    best = VALS[0:NE, 8 * r:8 * r + 8]
                    v.max(best, cur)
                    settle()
                    v.max_index(IDXU[:, 8 * r:8 * r + 8], best, cur)
                    v.match_replace(other, best, cur, -1.0)
                    cur, other = other, cur
                settle()
                v.tensor_copy(IDXF[0:NE, :], IDXU[:])
                settle()
                eye16 = ident[0:NE, 0:NE].unsqueeze(2).to_broadcast([NE, NE, CAP])
                for j, src in enumerate((IDXF, VALS)):
                    ins = v.tensor_tensor(BD[0:NE, j, :].rearrange("p (e s) -> p e s", s=CAP), bm(src[0:NE, :], NE), eye16, ALU.mult)
                ins.then_inc(sem("bd_ready"), 1)
                dve.wait_ge(sem("picks_mm"), L + 1)
                for t in range(TT):
                    ins = v.tensor_scalar(ST[:, t, :], bank(6), tokid[:, t:t + 1], None, ALU.is_equal)
                ins.then_inc(sem("st_ready"), 1)
                settle()
                for t in range(TT):
                    v.tensor_tensor(STV[:, t, :], bank(7), ST[:, t, :], ALU.mult)
                for dc in range(1, KC, 2):
                    dve.wait_ge(sem("xg_mm"), L * 8 + dc + 1)
                    v.tensor_scalar(XG[:, dc, :], bank(dc % 4), SCL[:, dc:dc + 1], BIA[:, dc:dc + 1],
                                    ALU.mult, ALU.add).then_inc(sem("xg_out1"), 1)
                settle()
                with dve.Fori(0, NE) as e:
                    te = tu + e
                    w = u2 + V_MOE
                    ev = L * NE + e
                    dve.wait_ge(w_free[(w + 3) % RING], te + (w + 3) // RING)
                    dve.wait_ge(sem("xg_out0"), L * 4 + 4)
                    v.tensor_copy(XGE, XG[:, :, bass.ds(e * CAP, CAP)]).then_inc(sem("xge_ready"), 1)
                    dve.wait_ge(sem("s4_mm"), ev + 1)
                    for t in range(TT):
                        ins = v.tensor_copy(SREP[:, t], STV[:, t, bass.ds(e * CAP, CAP)].unsqueeze(1).to_broadcast([P, 4, CAP]))
                    ins.then_inc(sem("srep_ready"), 1)
                    dve.wait_ge(sem("silg"), ev + 1)
                    spent(dve, w + 3, te)
                    v.tensor_tensor(HE, bank(5, T), SILG, ALU.mult).then_inc(sem("he_ready"), 1)
                    dve.wait_ge(sem("expert_done"), ev + 1)
                    for u in range(2):
                        spent(dve, w + 4 + u, te)
                        v.tensor_copy(YS[:, u, :], bank((7, 4)[u])).then_inc(sem("ys_out"), 1)
                dve.wait_ge(sem("expert_done"), L * NE + NE + 1)
                gated_residual(L * 2 + 2)
            mean_square(9)
            dve.wait_ge(sem("fgr_in"), 32)
            for t in range(TT):
                v.scalar_tensor_tensor(X[:, t, :], X[:, t, :], rstd[:, t:t + 1], FGR2, ALU.mult, ALU.mult).then_inc(sem("x_ready"), 1)

        @block.scalar
        def _(act):
            a = nc.scalar
            settle = a.drain

            def mean_square(r, x_count):
                if x_count is not None:
                    act.wait_ge(sem("x_ready"), x_count)
                a.activation(XN[:, 0, :], X[:, 0, :], ACT.Square, accum_out=ssq[:, 0:1])
                settle()
                a.copy(ajunk[:], ssq[:, 0:1]).then_inc(sem("ssq_act"), 1)

            def norm(r, j, x_count, scale, shift=None):
                mean_square(r, x_count)
                act.wait_ge(sem("rstd_ready"), r + 1)
                a.activation(XN[:, 0, :], X[:, 0, :], ACT.Copy, scale=rstd[:, 0:1]).then_inc(sem("xn0"), 1)
                act.wait_ge(sem("ht_psum"), j + 1)
                for dc in range(4):
                    src = pair(4 + dc // 2, T)[:, dc % 2]
                    a.activation(HT[:, dc, :], src, ACT.Identity, scale=scale(dc),
                                 bias=0.0 if shift is None else shift(dc)).then_inc(sem("ht_ready"), 1)

            act.wait_ge(sem("cols_psum"), 1)
            for n, group in enumerate(ROWS):
                cnt = sum(x for _, x in group)
                a.copy(COLS[:, n * P:n * P + cnt], PS[:, 3, n * P:n * P + cnt]).then_inc(sem("cols_ready"), 1)
            settle()
            a.activation(CACT[:], COLS[:, COL["c_2"]:COL["c_2"] + 8], ACT.Silu).then_inc(sem("cact"), 1)
            act.wait_ge(sem("x_in"), 16)
            norm(0, 0, None, lambda dc: colof("norm_mix", dc))

            def conv_in(ch):
                qkv_piece(act, ch)
                if ch >= 3:
                    act.wait_ge(sem("conv_out"), ch - 2)
                a.copy(CP[:, ch % 3, 2:2 + T], bank(ch % 4, T)).then_inc(sem("chunk_out"), 1)

            def silu(ch):
                act.wait_ge(sem("conv_out"), ch + 1)
                dst = KQT[:, ch, 1, :] if ch < GH else KQT[:, ch - GH, 0, :] if ch < 2 * GH else CV[:, ch % 3, :]
                a.activation(dst, CV[:, ch % 3, :], ACT.Silu).then_inc(sem("silu"), 1)

            def squares(ch):
                if ch < GH:
                    act.wait_ge(sem("turned"), ch + 1)
                else:
                    act.wait_ge(sem("tok_done"), ch - GH + 1)
                for t in range(TT):
                    src = pair(4 + ch % 2, P)[:, t] if ch < GH else KN[:, ch - GH, t, :]
                    a.activation(JUNK, src, ACT.Square, accum_out=RQK[:, t, ch:ch + 1])
                    settle()
                a.copy(ajunk[:], RQK[:, 1, ch:ch + 1]).then_inc(sem("sq_done"), 1)

            for ch in range(24):
                conv_in(ch)
                if ch >= 1:
                    silu(ch - 1)
                if ch >= 3 and ch - 3 < 16:
                    squares(ch - 3)
            silu(23)
            for u in range(2):
                for t in range(TT):
                    if t == 0:
                        act.wait_ge(sem("tok_mm"), u + 1)
                    else:
                        spent(act, U_Z + u)
                    a.activation(Z[:, t, u * 512:(u + 1) * 512], bank(2 * u + t), ACT.Silu).then_inc(sem("z_act"), 1)
            act.wait_ge(sem("decay_in"), 1)
            act.wait_ge(sem("gdn_in"), 16 * 8)
            s2 = [SPT[:, i, :].rearrange("p (t c) -> p t c", c=16) for i in range(6)]
            a.activation(s2[2], s2[1], ACT.Exp)
            a.activation(s2[4], PS[:, 6, 0:64].rearrange("p (t c) -> p t c", c=32)[:, :, 16:32], ACT.Exp, scale=-1.0)
            a.activation(ALOG, ALOG, ACT.Exp)
            settle()
            a.activation(s2[3], s2[2], ACT.Ln, bias=1.0).then_inc(sem("decay_out"), 1)
            for g in range(4):
                act.wait_ge(sem("knt_mm"), g + 1)
                a.copy(KQT[:, 2 * g:2 * g + 2, 0, :], pair(4 + g % 2, T)).then_inc(sem("knt_done"), 1)
            act.wait_ge(sem("decay_in"), 1 + 1)
            a.activation(EG, GC, ACT.Exp)
            a.activation(KD_S, KD_S, ACT.Exp).then_inc(sem("decay_out"), 1)
            for it in range(4):
                for l in range(2):
                    act.wait_ge(sem("dt_in"), 2 * it + l + 1)
                    a.activation(lanes[l]["DT"], lanes[l]["DT"], ACT.Exp).then_inc(sem("dt_out"), 1)
                for l in range(2):
                    act.wait_ge(sem("t_init"), 2 * it + l + 1)
                    a.copy(lanes[l]["Tm"], pair(3 * l, P)).then_inc(sem("t_ready"), 1)
                for q in range(nlev_):
                    for l in range(2):
                        act.wait_ge(sem("p_mm"), (it * nlev_ + q) * 2 + l + 1)
                        if q >= 1:
                            act.wait_ge(sem("r_mm"), (it * nlev_ + q - 1) * 2 + l + 1)
                        a.copy(lanes[l]["DT"], pair(3 * l, P)).then_inc(sem("p_out"), 1)
                for i in range(2):
                    act.wait_ge(sem("vn_mm"), 2 * it + i + 1)
                    if i == 1:
                        act.wait_ge(sem("o_mm"), 2 * it + 1)
                    a.copy(VN, pair(6, P)).then_inc(sem("vn_out"), 1)
                    if i == 0:
                        act.wait_ge(sem("s_mm"), it + 1)
                        a.copy(SST, pair(7, P)).then_inc(sem("s_out"), 1)
            act.wait_ge(sem("y_turned"), 1)
            for i in (0, 1):
                a.copy(HT[:, 2 * i:2 * i + 2, :], pair(3 + i, T)).then_inc(sem("y_back"), 1)
            if stop == "gdn":
                return

            def mlp(l):
                def relu(u, t, n, turns):
                    if t == 0:
                        act.wait_ge(sem("up_mm"), u + 1)
                    else:
                        spent(act, n, turns)
                    act.wait_ge(sem("rl_turned"), u)
                    a.activation(RL[:, t, :], bank(4 + t), ACT.Relu).then_inc(sem("relu"), 1)

                def square(u):
                    act.wait_ge(sem("rl_turned"), u + 1)
                    for i in range(2):
                        a.activation(MT[:, 2 * i:2 * i + 2, :], pair(6 + i, T), ACT.Square).then_inc(sem("mt_ready"), 1)

                n0 = U_MLP[l]
                for t in range(TT):
                    relu(8 * l, t, n0, 0)
                relu(8 * l + 1, 0, n0 + 1, 0)
                square(8 * l)
                relu(8 * l + 1, 1, n0 + 1, 0)
                with act.Fori(0, 2) as i:
                    for j in range(3):
                        u = i * 3 + (8 * l + 1 + j)
                        n = n0 + 3 + 4 * j
                        relu(u + 1, 0, n, i * MLP_TURNS)
                        square(u)
                        relu(u + 1, 1, n, i * MLP_TURNS)
                square(8 * l + 7)

            norm(1, 1, 1, lambda dc: colof("norm_mlp", dc))
            mlp(0)
            if stop == "mlp0":
                return
            norm(2, 2, 2, lambda dc: colof("norm_mix", 8 + dc))
            for ch in range(18):
                if ch % 4 == 3:
                    spent(act, U_SIN + ch // 4)
                else:
                    act.wait_ge(sem("chunk_mm"), 3 * (ch // 4) + ch % 4 + 1 + 18)
                src = bank(ch % 4, T)
                if ch < 9:
                    back = bass.AP(src.tensor, src.offset + P - 1, [list(src.ap[0]), [P, TT], [-1, P]])
                    ins = a.activation(SQKT[:, ch, :].rearrange("p (t q) -> p t q", q=P), back, ACT.Copy, scale=SE ** -0.5)
                else:
                    ins = a.copy(SQKT[:, ch, :], src)
                ins.then_inc(sem("chunk_out"), 1)
            for h in range(SH + 1):
                if h < SH:
                    act.wait_ge(sem("row_max"), h + 1)
                    for t in range(TT):
                        p = SP_[:, (h % 2) * 2 + t, :]
                        a.activation(p, p, ACT.Exp, bias=NMX[:, t, h:h + 1], accum_out=SM[:, t, h:h + 1]).then_inc(sem("exp_done"), 1)
                if h >= 1:
                    g = h - 1
                    act.wait_ge(sem("p_turned"), g + 1)
                    a.copy(SPT2[:, g % 2], pair(2 + g % 2, T)).then_inc(sem("pt_out"), 1)
            act.wait_ge(sem("angle_in"), 1)
            a.activation(SC, SS, ACT.Exp).then_inc(sem("angle_out"), 1)
            act.wait_ge(sem("y_turned"), 1 + 1)
            for i in (0, 2, 4):
                w = 2 if i < 4 else 1
                a.copy(SOT[:, 2 * i:2 * i + w, :], pair(i, T)[:, 0:w]).then_inc(sem("y_back"), 1)
            norm(3, 3, 3, lambda dc: colof("norm_mlp", 8 + dc))
            mlp(1)
            mean_square(4, 4)
            if stop == "b1":
                return
            act.wait_ge(sem("angle_in"), 1 + 1)
            a.activation(SIN, ANG, ACT.Sin)
            a.activation(COS, COS, ACT.Sin).then_inc(sem("angle_out"), 1)
            with act.Fori(0, NL) as L:
                tu = L * SEC_TURNS
                u2 = U_SEC
                norm(L * 2 + 5, L * 2 + 4, L * 2 + 5, lambda dc: SCL[:, dc:dc + 1], lambda dc: BIA[:, dc:dc + 1])
                for i, (b, w, name, n) in enumerate(((0, QR, "cq_mm", V_CQ), (2, KVR, "kv_mm", V_KV))):
                    for t in range(TT):
                        act.wait_ge(sem("cq_out"), L * 4 + 2 * i + t + 1)
                        a.activation(TMP[:, 0:w], CQ[:, t, b * (QR // 2):b * (QR // 2) + w], ACT.Square, accum_out=SS2[:, 2 * i + t:2 * i + t + 1])
                        settle()
                a.copy(ajunk[:], SS2[:, 3:4]).then_inc(sem("sq2"), 1)
                for t in range(TT):
                    if t == 0:
                        act.wait_ge(sem("pu_mm"), L + 1)
                    else:
                        spent(act, u2 + V_PU, tu)
                    ins = a.copy(PU[:, t, :], bank(4 + t))
                ins.then_inc(sem("pu_out"), 1)
                spent(act, u2 + V_CX, tu)
                for b in range(2):
                    ins = a.copy(CX[:, 2 * b:2 * b + 2, :], pair(6 + b, T))
                ins.then_inc(sem("cx_out"), 1)
                act.wait_ge(sem("cqt_mm"), L + 1)
                for cc in range(5):
                    a.activation(CQT[:, cc, :], pair(4 + cc // 2, T)[:, cc % 2], ACT.Copy, scale=QKG[:, cc:cc + 1]).then_inc(sem("cqt_out"), 1)
                for j in range(2):
                    act.wait_ge(sem("mix_mm"), L * 2 + j + 1)
                    a.copy(MIXT[:, 2 * j:2 * j + 2, :], pair(7, T)).then_inc(sem("mix_out"), 1)
                spent(act, u2 + V_UQ, tu)
                for b in range(4):
                    t, h = b // 2, b % 2
                    ins = a.activation(MQ[:, t, 4 * h:4 * h + 4, :].rearrange("p a b -> p (a b)"), bank(4 + b, 384), ACT.Copy, scale=DQK ** -0.5)
                ins.then_inc(sem("mq_raw"), 1)
                for b in range(4):
                    t, h = b // 2, b % 2
                    act.wait_ge(sem("mk_ready"), L * 4 + b + 1)
                    ins = a.copy(MV[:, t, 4 * h:4 * h + 4, :], pair(b, P)[:, :, NOPE:P])
                ins.then_inc(sem("mv_out"), 1)
                for g in range(0, 8, 2):
                    act.wait_ge(sem("mqk_mm"), L * 8 + g + 1)
                    dst, b = (QT, 4 + g) if g < 4 else (KT, g - 4)
                    gg = g % 4
                    a.copy(dst[0:DQK, 2 * gg:2 * gg + 2, :], pair(b, T)[0:DQK]).then_inc(sem("mqk_out"), 1)
                for h in range(MH + 1):
                    if h < MH:
                        act.wait_ge(sem("row_max"), L * 8 + h + 1 + SH)
                        if h >= 2:
                            act.wait_ge(sem("p_turned"), L * 8 + h - 1 + SH)
                        for t in range(TT):
                            a.activation((MP, MP2)[h % 2][:, t, :], pair(h % 2, T)[:, t], ACT.Exp, bias=MNM[:, h, t:t + 1],
                                         accum_out=MSM[:, h, t:t + 1]).then_inc(sem("exp_done"), 1)
                    if h >= 1:
                        g = h - 1
                        act.wait_ge(sem("p_turned"), L * 8 + g + 1 + SH)
                        a.copy(MPT[g % 2], pair(2 + g % 2, T)).then_inc(sem("pt_out"), 1)
                act.wait_ge(sem("m_pv"), L * 2 + 1)
                a.copy(OT[:, 0:2, :], pair(4, T)).then_inc(sem("ot_out"), 1)
                for q in range(24):
                    if q % 4 == 3:
                        spent(act, u2 + V_GL[q // 4], tu)
                    else:
                        act.wait_ge(sem("gate_mm"), L * 18 + 3 * (q // 4) + q % 4 + 1)
                    if q >= 2:
                        act.wait_ge(sem("merge"), L * 24 + q - 1)
                    a.activation(SG[:, q % 2, :], bank(q % 2, T), ACT.Sigmoid, bias=BG[:, q:q + 1]).then_inc(sem("gate_out"), 1)
                act.wait_ge(sem("spread"), L * 2 + 1)
                a.copy(GR, PS[:, 4:6, :].rearrange("p a b -> p (a b)")).then_inc(sem("gr_out"), 1)
                norm(L * 2 + 6, L * 2 + 5, L * 2 + 6, lambda dc: SCL[:, dc:dc + 1], lambda dc: BIA[:, dc:dc + 1])
                act.wait_ge(sem("rm"), L + 1)
                for t in range(TT):
                    a.activation(AFF[:, t, :], PS[:, 4, t * NE:(t + 1) * NE], ACT.Exp, bias=RM[:, t:t + 1], accum_out=RSM[:, t:t + 1])
                    settle()
                a.copy(ajunk[:], RSM[:, 1:2]).then_inc(sem("aff_exp"), 1)
                for dc in range(0, KC, 2):
                    act.wait_ge(sem("xg_mm"), L * 8 + dc + 1)
                    a.activation(XG[:, dc, :], bank(dc % 4), ACT.Identity, scale=SCL[:, dc:dc + 1], bias=BIA[:, dc:dc + 1]).then_inc(sem("xg_out0"), 1)
                with act.Fori(0, NE) as e:
                    te = tu + e
                    w = u2 + V_MOE
                    ev = L * NE + e
                    spent(act, w + 1, te)
                    act.wait_ge(sem("he_ready"), ev + 1)
                    a.activation(SILG, bank(4, T), ACT.Silu).then_inc(sem("silg"), 1)
                    act.wait_ge(sem("s4_mm"), ev + 1 + 1)
                    act.wait_ge(sem("expert_done"), ev + 1)
                    a.copy(S4, PS[:, 6, T:2 * T]).then_inc(sem("s4_out"), 1)
                    act.wait_ge(sem("hte_mm"), ev + 1)
                    a.copy(HTE, pair(6, P)[:, 0:2]).then_inc(sem("hte_out"), 1)
                act.wait_ge(sem("spread"), L * 2 + 2)
                a.copy(GR, PS[:, 6:8, :].rearrange("p a b -> p (a b)")).then_inc(sem("gr_out"), 1)
            mean_square(9, 9)

        @block.gpsimd
        def _(pool):
            g = nc.gpsimd
            for name in CREDITED:
                g.sem_inc(sem(name), 1)
            g.memset(zero1, 0.0)
            g.memset(CP[:, :, 0:2], 0.0)
            g.memset(CP[:, :, 258:260], 0.0).then_inc(sem("filled"), 1)
            g.memset(nhalf[:], -0.5)
            g.drain()

            def rsqrt(out, x, n):
                return g.tensor_tensor(out, x, nhalf[:, 0:n], ALU.pow)

            def norm(r):
                pool.wait_ge(sem("var_ready"), r + 1)
                rsqrt(rstd[:], var[:], 2).then_inc(sem("rstd_ready"), 1)

            norm(0)
            pool.wait_ge(sem("gdn_ms"), 1)
            rsqrt(RQV.rearrange("p a b -> p (a b)"), RQK.rearrange("p a b -> p (a b)"), 32).then_inc(sem("gdn_rs"), 1)
            pool.wait_ge(sem("gdn_ms"), 1 + 1)
            rsqrt(SPT[:, 2, 0:16], SPT[:, 1, 0:16], 16).then_inc(sem("gdn_rs"), 1)
            if stop == "gdn":
                return
            norm(1)
            if stop == "mlp0":
                return
            norm(2)
            norm(3)
            norm(4)
            if stop == "b1":
                return
            with pool.Fori(0, NL) as L:
                norm(L * 2 + 5)
                pool.wait_ge(sem("var2"), L + 1)
                rsqrt(RS2, VAR2, 4).then_inc(sem("rs2"), 1)
                norm(L * 2 + 6)
            norm(9)


NAMES = ("x norm_mix norm_mlp norm_final rel_bias gdn_w_in gdn_conv_w gdn_a_log gdn_dt_bias gdn_norm_w gdn_w_out "
         "dswa_w_in dswa_w_out mlp_w1 mlp_w2 c_2 positions_2 w_mod_2 b_mod_2 norm1_g_2 w_in_2 b_gate_2 q_norm_g_2 "
         "w_uq_2 kv_norm_g_2 w_ukv_2 w_oa_2 w_pool_2 pool_scale_2 conv_w_2 w_oc_2 w_out_2 norm2_g_2 w_router_2 "
         "w_gate_2 w_up_2 w_down_2 final_g_2").split()


def kernel(**inputs):
    import concourse.bacc as bacc
    from concourse.bass_utils import run_bass_kernel_spmd

    nc = bacc.Bacc("TRN2", target_bir_lowering=False, num_devices=1)
    arrays, aps = {}, {}
    for name, a in [(n, np.ascontiguousarray(inputs[n])) for n in NAMES] + list(constants().items()):
        arrays[f"in_{name}"] = a
        aps[name] = nc.dram_tensor(f"in_{name}", a.shape, mybir.dt.from_np(a.dtype), kind="ExternalInput").ap()
    out = nc.dram_tensor("out_x", (1, T, D), F32, kind="ExternalOutput").ap()
    program(nc, aps, out)
    r = run_bass_kernel_spmd(nc, [arrays], core_ids=[0])
    return r.results[0]["out_x"]
```

```python
from contextlib import ExitStack
import math

import numpy as np

import concourse.bass as bass
from concourse import mybir

ALU = mybir.AluOpType
ACT = mybir.ActivationFunctionType
F32 = mybir.dt.float32
F32R = mybir.dt.float32r
I32 = mybir.dt.int32
U32 = mybir.dt.uint32
U8 = mybir.dt.uint8
AX = mybir.AxisListType.X

P = 128
D = 1024
KC = D // P
T = 256
TT = T // P
EPS = 1e-6
GH = 8
LEVELS = (2, 4, 8, 16, 32, 64)
Q32 = 32
NSMALL = 4
NMASK = 2 * 7 * P + 2 * (NSMALL + 1) * Q32
SH, SE, SGRP, SHALF = 18, 64, 6, 64
SDIL = (1, 4, 16)
BUCKETS, MAX_DIST = 32, 1024
TZW = 3 * P
NL = 2
MH, NOPE, ROPE, VH, QR, KVR = 8, 64, 32, 64, 384, 256
DQK = NOPE + ROPE
QKW = QR + KVR
NE, CAP, FF = 16, 32, 1024
C_PU, C_CX, C_CB, C_CC, C_GL = 672, 1184, 1696, 2208, 2720
NEG = -1e30

ROWS = (
    (("norm_mix", 16), ("norm_mlp", 16), ("c_2", 8), ("norm1_g_2", 16), ("norm2_g_2", 16), ("b_gate_2", 48)),
    (("gdn_conv_w", 120),),
    (("b_mod_2", 96), ("pool_scale_2", 16), ("q_norm_g_2", 6), ("kv_norm_g_2", 4)),
    (("conv_w_2", 24),),
)
COL = {}
for _n, _rows in enumerate(ROWS):
    _at = 0
    for _name, _len in _rows:
        COL[_name] = _n * P + _at
        _at += _len

CREDITED = ("mod_mm", "mod_out", "s4_mm", "expert_done", "he_ready", "ys_out")

RING = 6
SLOT = 4096
U_QKV, U_Z, U_AB, U_GOUT = 0, 6, 8, 9
U_MLP = (11, 49)
MLP_TURNS = 2
U_SIN, U_SOUT = 39, 46
U_SEC = 77
SEC_UNITS = 18 + 6 * NE
SEC_TURNS = SEC_UNITS // RING
(V_CQ, V_KV, V_PU, V_CX, V_CC, V_CB, V_UQ, V_UKV, V_OA, V_GL, V_OC, V_OUT, V_MOE) = (
    0, 1, 2, 3, 4, 5, 6, 7, 8, (9, 10, 11, 12, 14, 15), 13, 16, 18)


def rel_buckets():
    rel = np.arange(-(T - 1), T)
    nb = BUCKETS // 2
    me = nb // 2
    n = np.abs(rel)
    nf = np.maximum(n, 1).astype(np.float32)
    large = me + (np.log(nf / np.float32(me)) / np.float32(math.log(MAX_DIST / me)) * np.float32(nb - me)).astype(np.int32)
    large = np.minimum(large, nb - 1)
    return np.where(rel > 0, nb, 0) + np.where(n < me, n, large)


NREL = 2 * T - 1


def constants():
    i = np.arange(P)
    eye = np.eye(P, dtype=np.float32)
    ones = np.ones((P, P), np.float32)
    cum = np.stack([(i[:, None] <= i[None]), (i[:, None] >= i[None])], 1).astype(np.float32)
    neg = np.where(cum > 0, 0.0, NEG).astype(np.float32)
    fr = (10000.0 ** (-np.arange(0, ROPE, 2, dtype=np.float32) / np.float32(ROPE))).astype(np.float32)
    tok = np.stack([i, i + P], 1).astype(np.float32)
    fconst = np.concatenate([eye, ones, np.tile(fr[None], (P, 1)), tok], 1)
    gconst = np.concatenate([cum.reshape(P, -1), neg.reshape(P, -1), np.tile(eye[:Q32, :Q32], (P // Q32, 1))], 1)
    low = []
    for s in (1,) + LEVELS:
        same = (i[:, None] // (2 * s)) == (i[None] // (2 * s))
        low.append(same & (i[:, None] % (2 * s) >= s) & (i[None] % (2 * s) < s))
    low = np.stack(low, 1)
    masks = np.stack([low, low.transpose(2, 1, 0)], 1).astype(np.float32)
    small = np.stack([np.tile(masks[:Q32, :, s, :Q32], (P // Q32, 1, 1)) for s in range(NSMALL + 1)], 2)
    t = np.arange(T)
    pm = np.zeros((4, T, T), np.float32)
    for g, w in enumerate((2, 4, 8, 16)):
        lo, hi = np.clip(t - w // 2, 0, T - 1), np.clip(t + w // 2 - 1, 0, T - 1)
        inside = (t[None] >= lo[:, None]) & (t[None] <= hi[:, None])
        pm[g] = inside / (hi - lo + 1).astype(np.float32)[:, None] - np.eye(T, dtype=np.float32)
    pool = pm.transpose(2, 0, 1).reshape(TT, P, 4, T).transpose(1, 0, 2, 3)
    rel = np.arange(-(T - 1), T)
    onehot = (rel_buckets()[None] == np.arange(BUCKETS)[:, None]).astype(np.float32)
    mask = np.zeros((SH, NREL), np.float32)
    for g, d in enumerate(SDIL):
        bad = (rel % d != 0) | (np.abs(rel) > SHALF * d)
        mask[g * SGRP:(g + 1) * SGRP, bad] = NEG
    return {
        "k_base": fconst, "k_gdn": gconst, "k_masks": np.concatenate([masks.reshape(P, -1), small.reshape(P, -1)], 1),
        "k_pool": np.ascontiguousarray(pool.reshape(P, -1)).astype(np.float32),
        "k_onehot": onehot, "k_reverse": np.ascontiguousarray(eye[::-1]), "k_winmask": mask,
    }


def program(nc, A, out, stop=None):
    with ExitStack() as ctx:
        sb = lambda n, s, d=F32: ctx.enter_context(nc.sbuf_tensor(n, s, d))
        sems = {}

        def sem(n):
            if n not in sems:
                sems[n] = ctx.enter_context(nc.semaphore(n))
            return sems[n]

        PS = ctx.enter_context(nc.psum_tensor("psum", [P, 8, 512], F32))

        def both(name, shape):
            with nc.sbuf_tensor(name, shape, F32) as plain:
                pass
            return plain, sb(name + "_r", shape, F32R)

        ring = sb("ring", [P, RING, SLOT])
        X = sb("x_resid", [P, TT, D])
        XN, XN_R = both("x_normed", [P, TT, D])
        HT, HT_R = both("h_featmajor", [P, KC, T])
        base = sb("base", [P, 2 * P + 18])
        COLS = sb("param_cols", [P, 4 * P])
        MODC = sb("mod_cols", [P, NL, 48])
        CACT = sb("c_act", [P, KC])
        ssq = sb("ssq", [P, 2]); var = sb("var", [P, 2]); rstd = sb("rstd", [P, 2])
        nhalf = sb("neg_half", [P, 64])
        ar, ar_r = both("arena", [P, 20480])
        MSUM = sb("mod_sums", [P, 8])[:]
        COS, SIN, ANG, KRD = (sb(n, [P, TT, 16])[:] for n in ("rotary_cos", "rotary_sin", "angles", "turns"))
        POSF = sb("pos_f", [P, TT])[:]
        marks = sb("block_masks", [P, NMASK], U8)
        rel_dram = nc.dram_tensor("rel_scratch", [SH, NREL], F32, kind="Internal").ap()

        ident, ones = base[:, 0:P], base[:, P:2 * P]
        freq, tokid = base[:, 2 * P:2 * P + 16], base[:, 2 * P + 16:2 * P + 18]

        class Carve:
            def __init__(self, at=0):
                self.at = at

            def __call__(self, *shape, parts=P):
                n = int(np.prod(shape))
                v = ar[0:parts, self.at:self.at + n]
                self.at += n
                assert self.at <= 20480, self.at
                if len(shape) == 2:
                    v = v.rearrange("p (a b) -> p a b", b=shape[1])
                if len(shape) == 3:
                    v = v.rearrange("p (a b c) -> p a b c", b=shape[1], c=shape[2])
                if len(shape) == 4:
                    v = v.rearrange("p (a b c d) -> p a b c d", b=shape[1], c=shape[2], d=shape[3])
                return v

        def bank(b, n=512):
            return PS[:, b, 0:n]

        def pair(b, w):
            return PS[:, b, :].rearrange("p (a w) -> p a w", w=w)

        c = Carve()
        KQT = c(GH, 2, T)
        KN = c(GH, TT, P)
        V = c(GH, TT, P)
        Z = c(TT, D)
        CUM = c(2, P)
        NEGM = c(2, P)
        EYE32 = c(Q32)
        NW = c(P)
        GS = c(2, 16)
        BT = c(2, 16)
        GC = c(2, 2, 8)
        EG = c(2, 2, 8)
        KD_S = c(2, 2, 8)
        TOT = c(2, 2, 8)
        RQK = c(TT, 16)
        RQV = c(TT, 16)
        DTB = c(16); ALOG = c(16)
        SPT = c(6, 32)
        top = c.at
        CP = c(3, 260)
        CV = c(3, T)
        OA = Carve(top)
        O_ACC = OA(TT, GH, P)
        GJ = OA.at
        lanes = []
        for _ in range(2):
            lanes.append(dict(DT=OA(4, P), KD=OA(4, 2, P), Tm=OA(4, P), U=OA(4, P)))
        SST = OA(4, P)
        VN = OA(4, P)
        R1 = OA(4, P)
        c = Carve(0)
        RL = c(TT, 512)
        MT = c(4, T)
        MT_R = ar_r[:, 1024:2048].rearrange("p (a b) -> p a b", b=T)
        c(4, T)
        MTH_R = ar_r[:, 2048:3072].rearrange("p (a b) -> p a b", b=T)
        MA = [c(512), c(512)]
        FGR = ar[:, 3072:4096]
        HALF = SLOT // 2
        split_at = c.at
        at = [split_at + 2 * HALF * place for place in (0, 3, 1, 2)]
        WH = [ar_r[:, x:x + HALF] for x in at]
        WL = [ar_r[:, x + HALF:x + 2 * HALF] for x in at]
        assert split_at + 8 * HALF <= 20480
        HTH_R = XN_R[:].rearrange("p t (a b) -> p (t a) b", b=T)
        c = Carve(0)
        SQKT = c(18, T)
        SV = c(TT, SH * SE)
        TZ = c(2, TZW)
        SP_ = c(4, T)
        SPT2 = c(2, 2, T)
        SO = c(TT, SH * SE)
        SOT = c(9, T)
        NMX = c(TT, SH); MX = c(TT, SH); SM = c(TT, SH); SC = c(TT, SH)
        MM = c(TT, SGRP); SS = c(TT, SH); DEN = c(TT, SGRP)
        RV = c(NREL + 1); RMK = c(NREL + 1); ROH = c(NREL + 1); RTB = c(SH)
        RJ = c(P)
        c = Carve(0)
        POOLM = c(TT, 4, T)
        WPOOL = c(4, T)
        WR = c(KC, NE)
        GR = c(D)
        TMP = c(512)
        sec_top = c.at
        CQ = c(TT, QKW)
        KR = c(TT, ROPE)
        KRR = c(TT, ROPE)
        CQT = c(5, T)
        MQ = c(TT, MH, DQK)
        MK = c(TT, MH, DQK)
        MV = c(TT, MH, VH)
        RT = c(4, P)
        PU = c(TT, 512)
        MIXT = c(4, T)
        BCT = c(4, T)
        OT = c(4, T)
        MSM = c(MH, 2); MNM = c(MH, 2); SS2 = c(4); VAR2 = c(4); RS2 = c(4)
        q_at = c.at
        QT = c(MH, T)
        KT = c(MH, T)
        c = Carve(sec_top)
        MP = c(2, T); MP2 = c(2, T)
        c2 = Carve(c.at)
        MPT = [CQT[:, 0:2, :], CQT[:, 2:4, :]]
        c = Carve(q_at)
        CX = c(4, T)
        CZ = c(4, 258)
        c = Carve(q_at)
        MG = c(KC, T)
        SG = c(2, T)
        MT2 = c(2, T)
        c = Carve(sec_top)
        XG = c(KC, NE * CAP)
        ST = c(TT, NE * CAP)
        STV = c(TT, NE * CAP)
        AFF = c(TT, NE)
        RM = c(TT); RSM = c(TT); RIN = c(TT)
        AT = c(T); AT2 = c(T)
        VALS = c(CAP); IDXF = c(CAP)
        BD = c(2, NE * CAP)
        XGE = c(KC, CAP)
        SREP = c(TT, 4, CAP)
        S4 = c(T)
        SILG = c(T)
        HE = c(T)
        HTE = c(2, P)
        YS = c(2, 512)
        zero1 = sb("zero", [P, 1])[:]
        GCOL = sb("gate_cols", [P, 16])[:]
        SCL = sb("norm_scale", [P, KC])[:]
        BIA = sb("norm_shift", [P, KC])[:]
        LC = sb("layer_cols", [P, 49])[:]
        PSC, BG, CW, QKG = LC[:, 0:8], LC[:, 8:32], LC[:, 32:44], LC[:, 44:49]
        IDXU = sb("topk_index", [16, CAP], U32)
        POSI = sb("pos_i", [P, TT], I32)
        rows = ring

        nlev_ = len(LEVELS)
        small_at = lambda l, i: XN[:, 0, (l * 4 + i) * P:(l * 4 + i + 1) * P].rearrange("p (h c) -> p h c", c=Q32)
        small = [dict(AN=small_at(l, 0), Tm=small_at(l, 1), U=small_at(l, 2), PP=small_at(l, 3)) for l in range(2)]
        quads = [slice(Q32 * b, Q32 * (b + 1)) for b in range(4)]
        ajunk = sb("act_junk", [P, 1])
        eps = sb("eps", [P, 1])
        JUNK = lanes[0]["DT"][:, 0]
        GJUNK = ar[:, GJ:GJ + 2048]
        MSTAGE = ar[:, GJ + 512:GJ + 512 + NMASK]
        w_full = [sem(f"w_full{i}") for i in range(RING)]
        w_free = [sem(f"w_free{i}") for i in range(RING)]

        def full(eng, n, turns=0):
            eng.wait_ge(w_full[n % RING], (turns + (n // RING + 1)) * 16)

        def colof(name, i):
            return COLS[:, COL[name] + i:COL[name] + i + 1]

        block = ctx.enter_context(nc.Block())

        FGR2 = GR

        @block.sync
        def _(sp):
            def load(n, src, turns=0, parts=P):
                if n >= RING:
                    sp.wait_ge(w_free[n % RING], turns + n // RING)
                a, b = src.shape[1], src.shape[2]
                dst = ring[0:parts, n % RING, 0:a * b].rearrange("p (a b) -> p a b", b=b)
                sp.dma_start(dst, src).then_inc(w_full[n % RING], 16)

            def dump(n):
                sp.wait_ge(sem("x_ready"), n)
                sp.dma_start(out[0].rearrange("(t p) d -> p t d", p=P), X[:]).then_inc(sem("out_stored"), 16)
                sp.wait_ge(sem("out_stored"), 16)

            def cols(w, a, b):
                return w.rearrange("(k p) n -> p k n", p=P)[:, :, a:b]

            sp.dma_start(base[:], A["k_base"]).then_inc(sem("params_in"), 16)
            for n, group in enumerate(ROWS):
                at = 0
                for name, cnt in group:
                    v = A[name]
                    nd = len(v.shape)
                    flat = v.rearrange({1: "a -> a", 2: "a b -> (a b)", 3: "a b c -> (a b c)", 4: "a b c d -> (a b c d)"}[nd])
                    sp.dma_start(XN[at:at + cnt, 1, n * P:(n + 1) * P],
                                 flat.rearrange("(r w) -> r w", w=P)).then_inc(sem("params_in"), 16)
                    at += cnt
            sp.dma_start(X[:], A["x"][0].rearrange("(t p) d -> p t d", p=P)).then_inc(sem("x_in"), 16)
            load(0, cols(A["gdn_w_in"][0], 0, 512))
            sp.dma_start(CUM, A["k_gdn"][:, 0:2 * P].rearrange("p (a b) -> p a b", b=P)).then_inc(sem("gdn_in"), 16)
            sp.dma_start(NEGM, A["k_gdn"][:, 2 * P:4 * P].rearrange("p (a b) -> p a b", b=P)).then_inc(sem("gdn_in"), 16)
            sp.dma_start(EYE32, A["k_gdn"][:, 4 * P:4 * P + Q32]).then_inc(sem("gdn_in"), 16)
            sp.dma_start(MSTAGE, A["k_masks"]).then_inc(sem("gdn_in"), 16)
            sp.dma_start(NW, A["gdn_norm_w"].partition_broadcast(P)[:, 0]).then_inc(sem("gdn_in"), 16)
            sp.dma_start(DTB, A["gdn_dt_bias"].rearrange("a b c -> a (b c)").partition_broadcast(P)[:, 0]).then_inc(sem("gdn_in"), 16)
            sp.dma_start(ALOG, A["gdn_a_log"].rearrange("a b c -> a (b c)").partition_broadcast(P)[:, 0]).then_inc(sem("gdn_in"), 16)
            for t in range(TT):
                sp.dma_start(POSI[:, t:t + 1], A["positions_2"][0, t * P:(t + 1) * P].rearrange("(p a) -> p a", a=1)).then_inc(sem("gdn_in"), 16)
            for u in range(1, 8):
                load(U_QKV + u, cols(A["gdn_w_in"][0], 512 * u, 512 * (u + 1)))
            load(U_AB, cols(A["gdn_w_in"][0], 4096, 4128))

            def halves(w, u):
                return w[u * 512:(u + 1) * 512, :].rearrange("(k p) n -> p k n", p=P)

            for u in range(2):
                load(U_GOUT + u, halves(A["gdn_w_out"][0], u))
            if stop == "gdn":
                return dump(1)

            def mlp(l):
                w1, w2, wm = A["mlp_w1"][l], A["mlp_w2"][l], A["w_mod_2"][l]
                w1c = w1.rearrange("(k p) n -> p k n", p=P)
                wmc = wm.rearrange("(k p) n -> p k n", p=P)
                w2r = w2.rearrange("(u k p) n -> u p k n", k=4, p=P)
                n0 = U_MLP[l]
                load(n0, w1c[:, :, 0:512])
                load(n0 + 1, w1c[:, :, 512:1024])
                load(n0 + 2, w2r[0])
                with sp.Fori(0, 2) as i:
                    for j in range(3):
                        n = n0 + 3 + 4 * j
                        turns = i * MLP_TURNS
                        load(n, w1c[:, :, bass.ds((i * 3 + j + 2) * 512, 512)], turns)
                        load(n + 1, w2r[bass.ds(i * 3 + j + 1, 1)][0], turns)
                        load(n + 2, wmc[:, :, bass.ds((i * 3 + j) * 1024, 512)], turns)
                        load(n + 3, wmc[:, :, bass.ds((i * 3 + j) * 1024 + 512, 512)], turns)
                load(n0 + 27, w2r[7])

            mlp(0)
            if stop == "mlp0":
                return dump(2)
            sp.wait_ge(sem("x_ready"), 2)
            sp.dma_start(ROH[0:BUCKETS, 0:NREL], A["k_onehot"]).then_inc(sem("tables_in"), 16)
            sp.dma_start(RMK[0:SH, 0:NREL], A["k_winmask"]).then_inc(sem("tables_in"), 16)
            sp.dma_start(RTB[0:BUCKETS, :], A["rel_bias"]).then_inc(sem("tables_in"), 16)
            sp.dma_start(RJ, A["k_reverse"]).then_inc(sem("tables_in"), 16)
            w = A["dswa_w_in"][0]
            for u in range(7):
                load(U_SIN + u, cols(w, 512 * u, min(512 * (u + 1), 3456)))
            sp.wait_ge(sem("rel_vec"), 1)
            sp.dma_start(rel_dram, RV[0:SH, 0:NREL]).then_inc(sem("rel_out"), 16)
            sp.wait_ge(sem("rel_out"), 16)
            tz = lambda h: bass.AP(rel_dram.tensor, rel_dram.offset + h * NREL, [[1, P], [1, TZW]])
            for h in range(SH):
                if h >= 2:
                    sp.wait_ge(sem("s_biased"), 2 * (h - 1))
                sp.dma_start(TZ[:, h % 2, :], tz(h)).then_inc(sem(f"tz_in{h % 2}"), 16)
            wo = A["dswa_w_out"][0]
            for u in range(2):
                load(U_SOUT + u, halves(wo, u))
            load(U_SOUT + 2, wo[1024:1152, :].rearrange("(k p) n -> p k n", p=P))
            mlp(1)
            sp.wait_ge(sem("mod_mm"), 12 + 1)
            sp.dma_start(FGR, A["norm_final"].rearrange("(a d) -> a d", a=1).partition_broadcast(P)[:, 0]).then_inc(sem("fgr_in"), 16)
            if stop == "b1":
                return dump(5)
            with sp.Fori(0, NL) as L:
                tu = L * SEC_TURNS
                ld = lambda n, src: load(U_SEC + n, src, tu)
                one = lambda ap: ap[bass.ds(L, 1)][0]
                wi = one(A["w_in_2"])
                for n, a, b in ((V_CQ, 0, QR), (V_KV, QR, C_PU), (V_PU, C_PU, C_CX), (V_CX, C_CX, C_CB),
                                (V_CC, C_CC, C_GL), (V_CB, C_CB, C_CC)):
                    ld(n, cols(wi, a, b))
                sp.wait_ge(sem("x_ready"), L * 2 + 5)
                sp.dma_start(WPOOL, one(A["w_pool_2"]).rearrange("g c n -> c g n")).then_inc(sem("side_in"), 16)
                sp.dma_start(WR, one(A["w_router_2"]).rearrange("(k p) n -> p k n", p=P)).then_inc(sem("side_in"), 16)
                sp.dma_start(POOLM.rearrange("p a b c -> p (a b c)"), A["k_pool"]).then_inc(sem("tables_in"), 16)
                ld(V_UQ, one(A["w_uq_2"]).rearrange("(k p) n -> p k n", p=P))
                ld(V_UKV, one(A["w_ukv_2"]).rearrange("(k p) n -> p k n", p=P))
                ld(V_OA, one(A["w_oa_2"]).rearrange("(k p) n -> p k n", p=P))
                for g in range(6):
                    if g == 4:
                        ld(V_OC, one(A["w_oc_2"]).rearrange("(k p) n -> p k n", p=P))
                    ld(V_GL[g], cols(wi, C_GL + 512 * g, C_GL + 512 * (g + 1)))
                for u in range(2):
                    ld(V_OUT + u, halves(one(A["w_out_2"]), u))
                with sp.Fori(0, NE) as e:
                    two = lambda ap: one(ap)[bass.ds(e, 1)][0]
                    for m, name in enumerate(("w_gate_2", "w_up_2")):
                        for u in range(2):
                            load(U_SEC + V_MOE + 2 * m + u, halves(two(A[name]), u), tu + e)
                    for u in range(2):
                        load(U_SEC + V_MOE + 4 + u, cols(two(A["w_down_2"]), 512 * u, 512 * (u + 1)), tu + e)
            sp.wait_ge(sem("x_ready"), 9)
            sp.dma_start(FGR2, A["final_g_2"].rearrange("(a d) -> a d", a=1).partition_broadcast(P)[:, 0]).then_inc(sem("fgr_in"), 16)
            for t in range(TT):
                sp.wait_ge(sem("x_ready"), t + 1 + 9)
                sp.dma_start(out[0, t * P:(t + 1) * P, :], X[:, t, :]).then_inc(sem("out_stored"), 16)
            sp.wait_ge(sem("out_stored"), 16 * TT)


        def spent(eng, n, turns=0):
            eng.wait_ge(w_free[n % RING], turns + (n // RING + 1))

        def W(n, b, parts=P):
            a = SLOT // b
            return ring[0:parts, n % RING, 0:a * b].rearrange("p (a b) -> p a b", b=b)

        def qkv_piece(eng, ch):
            if ch % 4 == 3:
                spent(eng, U_QKV + ch // 4)
            else:
                eng.wait_ge(sem("chunk_mm"), 3 * (ch // 4) + ch % 4 + 1)

        @block.tensor
        def _(pe):
            mm = nc.tensor.matmul

            def used(ins, n):
                ins.then_inc(w_free[n % RING], 1)

            def norm(k):
                pe.wait_ge(sem("xn0"), k + 1)
                for t in range(TT):
                    if t == 1:
                        pe.wait_ge(sem("xn1"), k + 1)
                    for dc in range(KC):
                        o = pair(4 + dc // 2, P)[:, (dc % 2) * 2 + t]
                        ins = nc.tensor.transpose(o, XN[:, t, dc * P:(dc + 1) * P], ident)
                ins.then_inc(sem("ht_psum"), 1)

            def normed(k):
                pe.wait_ge(sem("ht_ready"), k * 8 + 8)

            pe.wait_ge(sem("params_in"), 16 + 16 * sum(len(g) for g in ROWS))
            for n, group in enumerate(ROWS):
                cnt = sum(x for _, x in group)
                ins = nc.tensor.transpose(PS[:, 3, n * P:n * P + cnt], XN[0:cnt, 1, n * P:(n + 1) * P], ident[0:cnt, 0:cnt])
            ins.then_inc(sem("cols_psum"), 1)

            norm(0)
            normed(0)

            def qkv(ch):
                n = U_QKV + ch // 4
                if ch % 4 == 0:
                    full(pe, n)
                if ch >= 4:
                    pe.wait_ge(sem("chunk_out"), ch - 3)
                for k in range(KC):
                    ins = mm(bank(ch % 4, T), W(n, 512)[:, k, (ch % 4) * P:(ch % 4 + 1) * P], HT[:, k, :],
                             start=k == 0, stop=k == KC - 1)
                if ch % 4 == 3:
                    used(ins, n)
                else:
                    ins.then_inc(sem("chunk_mm"), 1)

            def turn(ch):
                pe.wait_ge(sem("silu"), ch + 1)
                if ch >= 2:
                    if ch - 2 < 16:
                        pe.wait_ge(sem("sq_done"), ch - 1)
                    if ch - 2 >= GH:
                        pe.wait_ge(sem("tok_done"), ch - 1 - GH)
                src = KQT[:, ch, 1, :] if ch < GH else KQT[:, ch - GH, 0, :] if ch < 2 * GH else CV[:, ch % 3, :]
                for t in range(TT):
                    ins = nc.tensor.transpose(PS[:, 4 + ch % 2, t * P:(t + 1) * P], src[:, t * P:(t + 1) * P], ident)
                ins.then_inc(sem("turned"), 1)

            for ch in range(24):
                qkv(ch)
                if ch >= 2:
                    turn(ch - 2)
            turn(22)
            turn(23)
            for u in range(2):
                full(pe, U_Z + u)
                for t in range(TT):
                    b = 2 * u + t
                    pe.wait_ge(sem("chunk_out"), 21 + b)
                    for k in range(KC):
                        ins = mm(bank(b), HT[:, k, t * P:(t + 1) * P], W(U_Z + u, 512)[:, k, :],
                                 start=k == 0, stop=k == KC - 1)
                    if t == 0:
                        ins.then_inc(sem("tok_mm"), 1)
                used(ins, U_Z + u)
            full(pe, U_AB)
            for t in range(TT):
                for k in range(KC):
                    ins = mm(PS[:, 6, t * 32:(t + 1) * 32], HT[:, k, t * P:(t + 1) * P],
                             ring[:, U_AB % RING, k * 32:(k + 1) * 32], start=k == 0, stop=k == KC - 1)
            used(ins, U_AB)
            pe.wait_ge(sem("kn_ready"), 1)
            for g in range(4):
                if g >= 2:
                    pe.wait_ge(sem("knt_done"), g - 1)
                for hh in range(2):
                    for t in range(TT):
                        ins = nc.tensor.transpose(pair(4 + g % 2, P)[:, hh * 2 + t], KN[:, 2 * g + hh, t, :], ident)
                ins.then_inc(sem("knt_mm"), 1)
            pe.wait_ge(sem("gs_ready"), 1)
            for d in range(2):
                rhs = GS[:, :, d * 8:(d + 1) * 8]
                mm(PS[:, 7, d * 16:(d + 1) * 16].rearrange("p (a b) -> p a b", b=8), CUM[:, d, :], rhs, start=True, stop=True)
                ins = mm(PS[:, 7, 32 + d * 16:48 + d * 16].rearrange("p (a b) -> p a b", b=8), ones, rhs, start=True, stop=True)
            ins.then_inc(sem("cum_mm"), 1)
            pe.wait_ge(sem("decay_out"), 1 + 1)
            pe.wait_ge(sem("knt_done"), 4)
            pe.wait_ge(sem("tok_out"), 4)

            nlev = len(LEVELS)
            for it in range(4):
                d, hg = it // 2, (it % 2) * 4
                fst, snd = (0, 1) if d == 0 else (1, 0)
                if it >= 1:
                    pe.wait_ge(sem("core_done"), it)
                for l in range(2):
                    for h in range(4):
                        g = d * 8 + hg + h
                        mm(pair(4 * l, P)[:, h], GS[:, l, g:g + 1].to_broadcast([P, P]), CUM[:, d, :], start=True, stop=True)
                    for h in range(4):
                        g = d * 8 + hg + h
                        mm(pair(4 * l + 1, P)[:, h], BT[:, l, g:g + 1].to_broadcast([P, P]), ident, start=True, stop=True)
                    for h in range(4):
                        ins = mm(pair(4 * l + 2 + h // 2, P)[:, (h % 2) * 2:(h % 2) * 2 + 2], KQT[:, hg + h, 0, l * P:(l + 1) * P],
                                 KQT[:, hg + h, :, l * P:(l + 1) * P], start=True, stop=True)
                    ins.then_inc(sem("core_setup"), 1)
                for q in range(NSMALL):
                    for l in range(2):
                        if q == 0:
                            pe.wait_ge(sem("t_ready"), 2 * it + l + 1)
                        else:
                            pe.wait_ge(sem("t_grown"), (it * 5 + q - 1) * 2 + l + 1)
                        for h in range(4):
                            for b in range(4):
                                r = quads[b]
                                ins = mm(PS[r, 4 * l, h * Q32:(h + 1) * Q32], small[l]["AN"][r, h], small[l]["Tm"][r, h],
                                         start=True, stop=True, tile_position=(Q32 * b, Q32 * b))
                        ins.then_inc(sem("p_mm"), 1)
                    for l in range(2):
                        pe.wait_ge(sem("p_out"), (it * nlev + q) * 2 + l + 1)
                        if q >= 1:
                            pe.wait_ge(sem("u_grown"), (it * nlev + q - 1) * 2 + l + 1)
                        for h in range(4):
                            for b in range(4):
                                r = quads[b]
                                ins = mm(PS[r, 4 * l + 1, h * Q32:(h + 1) * Q32], small[l]["U"][r, h], small[l]["PP"][r, h],
                                         start=True, stop=True, tile_position=(Q32 * b, Q32 * b))
                        ins.then_inc(sem("q_mm"), 1)
                for q in range(NSMALL, nlev):
                    for l in range(2):
                        if q == NSMALL:
                            pe.wait_ge(sem("expanded"), 2 * it + l + 1)
                        else:
                            pe.wait_ge(sem("t_grown"), (it * 5 + q - 1) * 2 + l + 1)
                        for h in range(4):
                            ins = mm(pair(4 * l, P)[:, h], lanes[l]["KD"][:, h, 0], lanes[l]["Tm"][:, h], start=True, stop=True)
                        ins.then_inc(sem("p_mm"), 1)
                    for l in range(2):
                        pe.wait_ge(sem("p_out"), (it * nlev + q) * 2 + l + 1)
                        if q < nlev - 1:
                            for h in range(4):
                                ins = mm(pair(4 * l + 1, P)[:, h], lanes[l]["U"][:, h], lanes[l]["DT"][:, h], start=True, stop=True)
                            ins.then_inc(sem("q_mm"), 1)
                        else:
                            pe.wait_ge(sem("u_grown"), (it * nlev + q - 1) * 2 + l + 1)
                            for h in range(4):
                                ins = mm(pair(4 * l + 2, P)[:, h], lanes[l]["DT"][:, h], lanes[l]["U"][:, h], start=True, stop=True)
                            ins.then_inc(sem("r_mm"), 1)
                    if q < nlev - 1:
                        for l in range(2):
                            pe.wait_ge(sem("t_grown"), (it * 5 + q) * 2 + l + 1)
                            for h in range(4):
                                ins = nc.tensor.transpose(pair(4 * l + 2, P)[:, h], lanes[l]["Tm"][:, h], ident)
                            ins.then_inc(sem("t_turned"), 1)
                pe.wait_ge(sem("u_grown"), (it + 1) * nlev * 2)
                pe.wait_ge(sem("r1_ready"), 2 * it + 1)
                for h in range(4):
                    ins = mm(pair(6, P)[:, h], lanes[fst]["U"][:, h], R1[:, h], start=True, stop=True)
                ins.then_inc(sem("vn_mm"), 1)
                pe.wait_ge(sem("vn_out"), 2 * it + 1)
                pe.wait_ge(sem("kdec"), it + 1)
                for h in range(4):
                    ins = mm(pair(7, P)[:, h], lanes[fst]["Tm"][:, h], VN[:, h], start=True, stop=True)
                ins.then_inc(sem("s_mm"), 1)
                for h in range(4):
                    ins = mm(pair(2, P)[:, h], lanes[fst]["KD"][:, h, 1], VN[:, h], start=True, stop=True)
                ins.then_inc(sem("o_mm"), 1)
                pe.wait_ge(sem("s_out"), it + 1)
                for h in range(4):
                    mm(pair(0, P)[:, h], KQT[:, hg + h, 0, snd * P:(snd + 1) * P], SST[:, h], start=True, stop=True)
                    ins = mm(pair(1, P)[:, h], KQT[:, hg + h, 1, snd * P:(snd + 1) * P], SST[:, h], start=True, stop=True)
                ins.then_inc(sem("ks_mm"), 1)
                pe.wait_ge(sem("r1_ready"), 2 * it + 2)
                for h in range(4):
                    ins = mm(pair(6, P)[:, h], lanes[snd]["U"][:, h], R1[:, h], start=True, stop=True)
                ins.then_inc(sem("vn_mm"), 1)
                pe.wait_ge(sem("vn_out"), 2 * it + 2)
                for h in range(4):
                    ins = mm(pair(7, P)[:, h], lanes[snd]["KD"][:, h, 1], VN[:, h], start=True, stop=True)
                ins.then_inc(sem("o_mm"), 1)

            for t in range(TT):
                pe.wait_ge(sem("y_ready"), t + 1)
                for dc in range(KC):
                    ins = nc.tensor.transpose(pair(3 + dc // 2, P)[:, (dc % 2) * 2 + t], XN[:, t, dc * P:(dc + 1) * P], ident)
            ins.then_inc(sem("y_turned"), 1)
            pe.wait_ge(sem("y_back"), 4)

            def rows_product(n, turns, lhs, first, last):
                full(pe, n, turns)
                cnt = lhs.shape[1]
                order = [(kk, b) for b in range(4) for kk in range(cnt)]
                for kk, b in order:
                    t, h = b // 2, b % 2
                    ins = mm(bank(b), lhs[:, kk, t * P:(t + 1) * P], W(n, D)[:, kk, h * 512:(h + 1) * 512],
                             start=first and kk == 0, stop=last and kk == cnt - 1, skip_group_check=True)
                    if last and (kk, b) == (cnt - 1, 1):
                        ins.then_inc(sem("half_mm"), 1)
                used(ins, n)

            for u in range(2):
                rows_product(U_GOUT + u, 0, HT[:, 4 * u:4 * u + 4, :], u == 0, u == 1)
            if stop == "gdn":
                return

            def mlp(l):
                n0 = U_MLP[l]

                def parts(kind, idx, n, turns, count):
                    if idx % 2 == 0:
                        pe.wait_ge(sem(f"{kind}_first_lo"), count)
                    else:
                        spent(pe, n, turns)
                    return WH[idx % 4], WL[idx % 4]

                def three(o, xh, xl, wh, wl, start, stop):
                    mm(o, xh, wh, start=start, stop=False, skip_group_check=True)
                    mm(o, xl, wh, start=False, stop=False, skip_group_check=True)
                    return mm(o, xh, wl, start=False, stop=stop, skip_group_check=True)

                def up(idx, n, turns, count, t, relus):
                    if relus is not None:
                        pe.wait_ge(sem("relu"), relus)
                    ts = slice(t * P, (t + 1) * P)
                    for hf in range(2):
                        wh, wl = parts("w1", idx + hf, n, turns, count)
                        for kk in range(4):
                            k = 4 * hf + kk
                            c = slice(kk * 512, (kk + 1) * 512)
                            ins = three(bank(4 + t), HTH_R[:, k, ts], HT_R[:, k, ts], wh[:, c], wl[:, c], k == 0, k == KC - 1)
                        if t == 1:
                            ins.then_inc(sem("half_used"), 1)
                    if t == 0:
                        ins.then_inc(sem("up_mm"), 1)

                def down(idx, n, turns, count, hf, first, last):
                    halves_ = ((hf, idx + hf),) if not last else ((0, idx), (1, idx + 1))
                    split = {f: parts("w2", i, n, turns, count) for f, i in halves_}
                    if last:
                        order = [(b, 2 * f + kk) for b in range(4) for f in range(2) for kk in range(2)]
                    else:
                        order = [(b, 2 * hf + kk) for kk in range(2) for b in range(4)]
                    for b, k in order:
                        t, h = b // 2, b % 2
                        wh, wl = split[k // 2]
                        c = slice((k % 2) * D + h * 512, (k % 2) * D + (h + 1) * 512)
                        ts = slice(t * P, (t + 1) * P)
                        ins = three(bank(b), MTH_R[:, k, ts], MT_R[:, k, ts], wh[:, c], wl[:, c], first and k == 0, last and k == 3)
                        if last and (b, k) == (1, 3):
                            ins.then_inc(sem("half_mm"), 1)
                        if last and (b, k) == (3, 1):
                            ins.then_inc(sem("half_used"), 1)
                    ins.then_inc(sem("half_used"), 1)

                def turn(u, mods):
                    pe.wait_ge(sem("relu"), u * 2 + 2)
                    pe.wait_ge(sem("mod_out"), mods + 1)
                    for t in range(TT):
                        for cc in range(4):
                            ins = nc.tensor.transpose(pair(6 + cc // 2, P)[:, (cc % 2) * 2 + t], RL[:, t, cc * P:(cc + 1) * P], ident)
                    ins.then_inc(sem("rl_turned"), 1)

                pe.wait_ge(sem("act_lo"), 9 * l + 1)
                for t in range(TT):
                    up(0, n0, 0, 8 * l + 1, t, None)
                up(2, n0 + 1, 0, 8 * l + 2, 0, 16 * l + 1)
                turn(8 * l, 6 * l)
                up(2, n0 + 1, 0, 8 * l + 2, 1, 16 * l + 2)
                pe.wait_ge(sem("act_lo"), 9 * l + 2)
                for hf in range(2):
                    down(4, n0 + 2, 0, 8 * l + 1, hf, hf == 0, False)
                with pe.Fori(0, 2) as i:
                    for j in range(3):
                        u = i * 3 + (8 * l + 1 + j)
                        idx, n, turns = 6 + 4 * j, n0 + 3 + 4 * j, i * MLP_TURNS
                        up(idx, n, turns, u + 2, 0, u * 2 + 1)
                        turn(u, i * 3 + (6 * l + j))
                        up(idx, n, turns, u + 2, 1, u * 2 + 2)
                        pe.wait_ge(sem("act_lo"), u + (l + 2))
                        down(idx + 2, n + 1, turns, u + 1, 0, False, False)
                        for mi in range(2):
                            spent(pe, n0 + 3 + 4 * j + 2 + mi, i * MLP_TURNS)
                        for cc in range(8):
                            ins = nc.tensor.transpose(pair(6 + cc // 4, P)[:, cc % 4], MA[cc // 4][:, (cc % 4) * P:(cc % 4 + 1) * P], ident)
                        ins.then_inc(sem("mod_mm"), 1)
                        down(idx + 2, n + 1, turns, u + 1, 1, False, False)
                turn(8 * l + 7, 6 * l + 6)
                pe.wait_ge(sem("act_lo"), 9 * l + 9)
                down(30, n0 + 27, 0, 8 * l + 8, 0, False, True)

            norm(1)
            normed(1)
            mlp(0)
            if stop == "mlp0":
                return

            norm(2)
            normed(2)
            pe.wait_ge(sem("tables_in"), 64)
            mm(PS[0:SH, 3, 0:NREL], RTB[0:BUCKETS, :], ROH[0:BUCKETS, 0:NREL], start=True, stop=True).then_inc(sem("rel_mm"), 1)
            for ch in range(18):
                n = U_SIN + ch // 4
                if ch % 4 == 0:
                    full(pe, n)
                if ch == 3:
                    pe.wait_ge(sem("rel_vec"), 1)
                if ch >= 4:
                    pe.wait_ge(sem("chunk_out"), ch - 3 + 24)
                for k in range(KC):
                    ins = mm(bank(ch % 4, T), W(n, 512)[:, k, (ch % 4) * P:(ch % 4 + 1) * P], HT[:, k, :],
                             start=k == 0, stop=k == KC - 1)
                if ch % 4 == 3:
                    used(ins, n)
                else:
                    ins.then_inc(sem("chunk_mm"), 1)
            for i, (n, a, w, tot, b) in enumerate(((4, 256, 256, 512, 4), (5, 0, 512, 512, 6), (6, 0, 384, 384, 4))):
                full(pe, U_SIN + n)
                for t in range(TT):
                    if i == 2:
                        pe.wait_ge(sem("tok_out"), t + 1 + 4)
                    for k in range(KC):
                        ins = mm(bank(b + t, w), HT[:, k, t * P:(t + 1) * P], W(U_SIN + n, tot)[:, k, a:a + w],
                                 start=k == 0, stop=k == KC - 1)
                    if t == 0:
                        ins.then_inc(sem("tok_mm"), 1)
                used(ins, U_SIN + n)
            pe.wait_ge(sem("chunk_out"), 18 + 24)
            pe.wait_ge(sem("tok_out"), 6 + 4)

            for h in range(SH + 2):
                if h < SH:
                    lo = 64 * (h % 2)
                    if h >= 2:
                        pe.wait_ge(sem("s_biased"), 2 * (h - 1))
                    for t in range(TT):
                        ins = mm(pair(h % 2, T)[:, t], SQKT[lo:lo + 64, h // 2, t * P:(t + 1) * P],
                                 SQKT[lo:lo + 64, 9 + h // 2, :], start=True, stop=True)
                    ins.then_inc(sem("scores_mm"), 1)
                if 1 <= h <= SH:
                    g = h - 1
                    pe.wait_ge(sem("exp_done"), 2 * (g + 1))
                    if g >= 2:
                        pe.wait_ge(sem("pt_out"), g - 1)
                    for t in range(TT):
                        for kt in range(TT):
                            ins = nc.tensor.transpose(pair(2 + g % 2, T)[:, kt, t * P:(t + 1) * P],
                                                      SP_[:, (g % 2) * 2 + t, kt * P:(kt + 1) * P], ident)
                    ins.then_inc(sem("p_turned"), 1)
                if h >= 2:
                    g = h - 2
                    pe.wait_ge(sem("pt_out"), g + 1)
                    if g >= 2:
                        pe.wait_ge(sem("s_o_out"), g - 1)
                    for t in range(TT):
                        for kt in range(TT):
                            ins = mm(PS[:, 4 + g % 2, t * SE:(t + 1) * SE], SPT2[:, g % 2, kt, t * P:(t + 1) * P],
                                     SV[:, kt, g * SE:(g + 1) * SE], start=kt == 0, stop=kt == 1)
                    ins.then_inc(sem("s_pv"), 1)
            pe.wait_ge(sem("y_ready"), 2 + 2)
            for cc in range(9):
                for t in range(TT):
                    ins = nc.tensor.transpose(pair(cc // 2, P)[:, (cc % 2) * 2 + t], SO[:, t, cc * P:(cc + 1) * P], RJ)
            ins.then_inc(sem("y_turned"), 1)
            pe.wait_ge(sem("y_back"), 5 + 4)
            for u in range(3):
                rows_product(U_SOUT + u, 0, SOT[:, 4 * u:min(4 * u + 4, 9), :], u == 0, u == 2)
            norm(3)
            normed(3)
            mlp(1)
            if stop == "b1":
                return

            with pe.Fori(0, NL) as L:
                tu = L * SEC_TURNS
                u2 = U_SEC
                norm(L * 2 + 4)
                normed(L * 2 + 4)

                def tok(n, w, b, name, a=0):
                    full(pe, u2 + n, tu)
                    for t in range(TT):
                        for k in range(KC):
                            ins = mm(bank(b + t, w), HT[:, k, t * P:(t + 1) * P], W(u2 + n, w)[:, k, :],
                                     start=k == 0, stop=k == KC - 1)
                        if t == 0:
                            ins.then_inc(sem(name), 1)
                    used(ins, u2 + n)

                def feat(n, b):
                    full(pe, u2 + n, tu)
                    for ch in range(4):
                        for k in range(KC):
                            ins = mm(pair(b + ch // 2, T)[:, ch % 2], W(u2 + n, 512)[:, k, ch * P:(ch + 1) * P], HT[:, k, :],
                                     start=k == 0, stop=k == KC - 1, skip_group_check=True)
                    used(ins, u2 + n)

                tok(V_CQ, QR, 0, "cq_mm")
                tok(V_KV, C_PU - QR, 2, "kv_mm")
                tok(V_PU, 512, 4, "pu_mm")
                feat(V_CX, 6)
                pe.wait_ge(sem("ckv_out"), L + 1)
                pe.wait_ge(sem("sq2"), L + 1)
                feat(V_CC, 0)
                feat(V_CB, 2)
                pe.wait_ge(sem("cqn_ready"), L + 1)
                pe.wait_ge(sem("pu_out"), L + 1)
                pe.wait_ge(sem("cx_out"), L + 1)
                for cc in range(5):
                    for t in range(TT):
                        ins = nc.tensor.transpose(pair(4 + cc // 2, P)[:, (cc % 2) * 2 + t], CQ[:, t, cc * P:(cc + 1) * P], ident)
                ins.then_inc(sem("cqt_mm"), 1)
                pe.wait_ge(sem("tables_in"), L * 16 + 80)
                for g in range(4):
                    if g == 2:
                        pe.wait_ge(sem("mix_out"), L * 2 + 1)
                    for tt in range(TT):
                        ins = mm(pair(7, T)[:, g % 2], PU[:, tt, g * P:(g + 1) * P], POOLM[:, tt, g, :],
                                 start=tt == 0, stop=tt == 1, skip_group_check=True)
                    if g % 2 == 1:
                        ins.then_inc(sem("mix_mm"), 1)
                pe.wait_ge(sem("cqt_out"), L * 5 + 5)
                pe.wait_ge(sem("mix_out"), L * 2 + 2)
                full(pe, u2 + V_UQ, tu)
                for t in range(TT):
                    for h in range(2):
                        for k in range(3):
                            ins = mm(bank(4 + 2 * t + h, 384), CQT[:, k, t * P:(t + 1) * P], W(u2 + V_UQ, 768)[:, k, h * 384:(h + 1) * 384],
                                     start=k == 0, stop=k == 2)
                used(ins, u2 + V_UQ)
                full(pe, u2 + V_UKV, tu)
                pe.wait_ge(sem("conv_y"), L + 1)
                for t in range(TT):
                    for h in range(2):
                        for k in range(2):
                            ins = mm(bank(2 * t + h), CQT[:, 3 + k, t * P:(t + 1) * P], W(u2 + V_UKV, D)[:, k, h * 512:(h + 1) * 512],
                                     start=k == 0, stop=k == 1)
                used(ins, u2 + V_UKV)
                for j, src in enumerate((MQ, MK)):
                    if j == 0:
                        pe.wait_ge(sem("mq_ready"), L + 1)
                    else:
                        pe.wait_ge(sem("mk_ready"), L * 4 + 4)
                    if j == 1:
                        pe.wait_ge(sem("mv_out"), L + 1)
                    for g in range(4):
                        b = (4 if j == 0 else 0) + g
                        for hh in range(2):
                            for t in range(TT):
                                ins = nc.tensor.transpose(pair(b, P)[0:DQK, hh * 2 + t], src[:, t, 2 * g + hh, :], ident)
                        ins.then_inc(sem("mqk_mm"), 1)
                pe.wait_ge(sem("mqk_out"), L * 8 + 8)
                for h in range(MH + 2):
                    if h < MH:
                        if h >= 2:
                            pe.wait_ge(sem("exp_done"), L * 16 + 2 * (h - 1) + 2 * SH)
                        for t in range(TT):
                            ins = mm(pair(h % 2, T)[:, t], QT[0:DQK, h, t * P:(t + 1) * P], KT[0:DQK, h, :], start=True, stop=True)
                        ins.then_inc(sem("scores_mm"), 1)
                    if 1 <= h <= MH:
                        g = h - 1
                        pe.wait_ge(sem("m_p"), L * 8 + g + 1)
                        if g >= 2:
                            pe.wait_ge(sem("pt_out"), L * 8 + g - 1 + SH)
                        for t in range(TT):
                            for kt in range(TT):
                                ins = nc.tensor.transpose(pair(2 + g % 2, T)[:, kt, t * P:(t + 1) * P],
                                                          (MP, MP2)[g % 2][:, t, kt * P:(kt + 1) * P], ident)
                        ins.then_inc(sem("p_turned"), 1)
                    if h >= 2:
                        g = h - 2
                        pe.wait_ge(sem("pt_out"), L * 8 + g + 1 + SH)
                        lo = 64 * (g % 2)
                        for kt in range(TT):
                            ins = mm(pair(4 + g // 4, T)[lo:lo + 64, (g // 2) % 2], MV[:, kt, g, :], MPT[g % 2][:, kt, :],
                                     start=kt == 0, stop=kt == 1, skip_group_check=True)
                        if g % 4 == 3:
                            ins.then_inc(sem("m_pv"), 1)
                pe.wait_ge(sem("ot_out"), L * 2 + 2)
                full(pe, u2 + V_OA, tu)
                for q in range(24):
                    b, dc = q // 8, q % 8
                    ng = u2 + V_GL[q // 4]
                    if q % 4 == 0:
                        full(pe, ng, tu)
                    if q == 16:
                        full(pe, u2 + V_OC, tu)
                    if q >= 2:
                        pe.wait_ge(sem("gate_out"), L * 24 + q - 1)
                        pe.wait_ge(sem("merge"), L * 24 + q - 1)
                    for k in range(KC):
                        ins = mm(bank(q % 2, T), W(ng, 512)[:, k, (dc % 4) * P:(dc % 4 + 1) * P], HT[:, k, :],
                                 start=k == 0, stop=k == KC - 1)
                    if q % 4 == 3:
                        used(ins, ng)
                    else:
                        ins.then_inc(sem("gate_mm"), 1)
                    o = bank(2 + q % 2, T)
                    if b == 1:
                        pe.wait_ge(sem("side_in"), L * 32 + 32)
                        mm(o, WPOOL[:, dc // 2, (dc % 2) * P:(dc % 2 + 1) * P], MIXT[:, dc // 2, :],
                           start=True, stop=True).then_inc(sem("branch_mm"), 1)
                    else:
                        wu = u2 + (V_OA if b == 0 else V_OC)
                        for k in range(4):
                            ins = mm(o, W(wu, D)[:, k, dc * P:(dc + 1) * P], (OT, BCT)[b // 2][:, k, :], start=k == 0, stop=k == 3)
                        if dc == 7:
                            used(ins, wu)
                        else:
                            ins.then_inc(sem("branch_mm"), 1)

                def spread(ins_col, b, name):
                    for dc in range(KC):
                        ins = mm(pair(b + dc // 4, P)[:, dc % 4], GCOL[:, ins_col + dc:ins_col + dc + 1].to_broadcast([P, P]), ident,
                                 start=True, stop=True, skip_group_check=True)
                    ins.then_inc(sem("spread"), 1)

                pe.wait_ge(sem("gcol"), L + 1)
                spread(0, 4, "g1")
                pe.wait_ge(sem("merge"), L * 24 + 24)
                for u in range(2):
                    rows_product(u2 + V_OUT + u, tu, MG[:, 4 * u:4 * u + 4, :], u == 0, u == 1)

                norm(L * 2 + 5)
                normed(L * 2 + 5)
                for t in range(TT):
                    for k in range(KC):
                        ins = mm(PS[:, 4, t * NE:(t + 1) * NE], HT[:, k, t * P:(t + 1) * P], WR[:, k, :], start=k == 0, stop=k == KC - 1)
                ins.then_inc(sem("router_mm"), 1)
                spread(8, 2, "g2")
                pe.wait_ge(sem("aff_ready"), L + 1)
                for t in range(TT):
                    ins = nc.tensor.transpose(PS[0:NE, 5, t * P:(t + 1) * P], AFF[:, t, :], ident)
                ins.then_inc(sem("aff_turned"), 1)
                pe.wait_ge(sem("bd_ready"), L + 1)
                for j in range(2):
                    ins = mm(bank(6 + j), ones[0:NE, :], BD[0:NE, j, :], start=True, stop=True)
                ins.then_inc(sem("picks_mm"), 1)
                pe.wait_ge(sem("st_ready"), L + 1)
                pe.wait_ge(sem("gr_out"), L * 2 + 2)
                for dc in range(KC):
                    if dc >= 4:
                        pe.wait_ge(sem(f"xg_out{dc % 2}"), L * 4 + (dc - 4) // 2 + 1)
                    for t in range(TT):
                        ins = mm(bank(dc % 4), XN[:, t, dc * P:(dc + 1) * P], ST[:, t, :], start=t == 0, stop=t == 1)
                    ins.then_inc(sem("xg_mm"), 1)
                pe.wait_ge(sem("xg_out0"), L * 4 + 4)
                pe.wait_ge(sem("xg_out1"), L * 4 + 4)
                pe.wait_ge(sem("filled"), 1)
                for b in range(4):
                    mm(bank(b), zero1.to_broadcast([P, P]), zero1.to_broadcast([P, 512]), start=True, stop=False, skip_group_check=True)
                with pe.Fori(0, NE) as e:
                    te = tu + e
                    v = u2 + V_MOE
                    ev = L * NE + e
                    pe.wait_ge(sem("xge_ready"), ev + 1)
                    pe.wait_ge(sem("ys_out"), ev * 2 + 1)
                    for m in range(2):
                        if m == 1:
                            pe.wait_ge(sem("he_ready"), ev + 1)
                        for u in range(2):
                            full(pe, v + 2 * m + u, te)
                            for kk in range(4):
                                for j in range(4):
                                    ins = mm(PS[32 * j:32 * j + 32, 4 + m, 0:T], XGE[:, 4 * u + kk, :],
                                             W(v + 2 * m + u, D)[:, kk, j * T:(j + 1) * T],
                                             start=u == 0 and kk == 0, stop=u == 1 and kk == 3, tile_position=(0, 32 * j),
                                             skip_group_check=True)
                            used(ins, v + 2 * m + u)
                    pe.wait_ge(sem("srep_ready"), ev + 1)
                    for t in range(TT):
                        ins = nc.tensor.transpose(PS[:, 6, T + t * P:T + (t + 1) * P], SREP[:, t].rearrange("p a b -> p (a b)"), ident)
                    ins.then_inc(sem("s4_mm"), 1)
                    pe.wait_ge(sem("s4_out"), ev + 1)
                    pe.wait_ge(sem("he_ready"), ev + 1 + 1)
                    for cc in range(2):
                        ins = nc.tensor.transpose(PS[:, 6, cc * P:(cc + 1) * P], HE[:, cc * P:(cc + 1) * P], ident)
                    ins.then_inc(sem("hte_mm"), 1)
                    pe.wait_ge(sem("hte_out"), ev + 1)
                    for u in range(2):
                        full(pe, v + 4 + u, te)
                        yb = (7, 4)[u]
                        for cc in range(2):
                            for j in range(4):
                                ins = mm(PS[32 * j:32 * j + 32, yb, :], HTE[:, cc, 32 * j:32 * j + 32], W(v + 4 + u, 512)[:, 2 * j + cc, :],
                                         start=cc == 0, stop=cc == 1, tile_position=(0, 32 * j), skip_group_check=True)
                        used(ins, v + 4 + u)
                    for u in range(2):
                        pe.wait_ge(sem("ys_out"), ev * 2 + u + 1 + 1)
                        for t in range(TT):
                            ins = mm(bank(2 * t + u), S4[:, t * P:(t + 1) * P], YS[:, u, :], start=False, stop=False, skip_group_check=True)
                    ins.then_inc(sem("expert_done"), 1)

        @block.vector
        def _(dve):
            v = nc.vector
            settle = v.drain

            def bc(ap, n):
                return ap.unsqueeze(2).to_broadcast([ap.shape[0], ap.shape[1], n])

            def bm(ap, n):
                return ap.unsqueeze(1).to_broadcast([ap.shape[0], n, ap.shape[1]])

            def mean_square(r, meanwhile=None):
                v.tensor_tensor_reduce(out=XN[:, 1, :], in0=X[:, 1, :], in1=X[:, 1, :], scale=1.0, scalar=0.0,
                                       op0=ALU.mult, op1=ALU.add, accum_out=ssq[:, 1:2])
                settle()
                v.tensor_scalar(var[:, 1:2], ssq[:, 1:2], 1.0 / D, EPS, ALU.mult, ALU.add).then_inc(sem("var1"), 1)
                if meanwhile:
                    meanwhile()
                dve.wait_ge(sem("rstd_ready"), r * 2 + 2)

            def norm(r, j, scale, shift=None, split=False, meanwhile=None):
                mean_square(r, meanwhile)
                v.tensor_scalar(XN[:, 1, :], X[:, 1, :], rstd[:, 1:2], None, ALU.mult).then_inc(sem("xn1"), 1)
                dve.wait_ge(sem("ht_psum"), j + 1)
                for dc in range(4, KC):
                    src = pair(4 + dc // 2, T)[:, dc % 2]
                    if shift is None:
                        ins = v.tensor_scalar(HT[:, dc, :], src, scale(dc), None, ALU.mult)
                    else:
                        ins = v.tensor_scalar(HT[:, dc, :], src, scale(dc), shift(dc), ALU.mult, ALU.add)
                    ins.then_inc(sem("ht_ready"), 1)
                if split:
                    settle()
                    v.tensor_copy(HTH_R[:, 4:KC, :], HT[:, 4:KC, :])

            def residual(n, complete):
                dve.wait_ge(sem("half_mm"), n)
                for b in range(4):
                    t, h = b // 2, b % 2
                    if b == 2:
                        ins.then_inc(sem("x_half"), 1)
                        complete()
                    xs = X[:, t, h * 512:(h + 1) * 512]
                    ins = v.tensor_tensor(xs, bank(b), xs, ALU.add)
                ins.then_inc(sem("x_ready"), 1)

            def low(n, idx, done):
                for hf in range(2):
                    dve.wait_ge(sem("hi"), done + hf + 1)
                    b = (idx + hf) % 4
                    ins = v.tensor_tensor(WL[b], W(n, SLOT)[:, 0, hf * HALF:(hf + 1) * HALF], WH[b].bitcast(F32), ALU.subtract)
                    ins.then_inc(sem("w1_first_lo") if hf == 0 else w_free[n % RING], 1)

            dve.wait_ge(sem("x_in"), 16)
            dve.wait_ge(sem("cols_psum"), 1)
            dve.wait_ge(sem("cols_ready"), 4)
            norm(0, 0, lambda dc: colof("norm_mix", dc))
            dve.wait_ge(sem("filled"), 1)

            def conv(ch):
                dve.wait_ge(sem("chunk_out"), ch + 1)
                if ch >= 3:
                    dve.wait_ge(sem("silu"), ch - 2)
                if ch - 3 >= 16:
                    dve.wait_ge(sem("turned"), ch - 2)
                x, y = CP[:, ch % 3, :], CV[:, ch % 3, :]
                tap = lambda k: colof("gdn_conv_w", 24 * k + ch)
                v.tensor_scalar(y, x[:, 0:T], tap(0), None, ALU.mult)
                for k in range(1, 5):
                    settle()
                    ins = v.scalar_tensor_tensor(y, x[:, k:k + T], tap(k), y, ALU.mult, ALU.add)
                ins.then_inc(sem("conv_out"), 1)

            def to_tokens(ch):
                dve.wait_ge(sem("turned"), ch + 1)
                dst = KN[:, ch - GH] if ch < 2 * GH else V[:, ch - 2 * GH]
                v.tensor_copy(dst, pair(4 + ch % 2, P)[:, 0:2]).then_inc(sem("tok_done"), 1)

            for ch in range(24):
                conv(ch)
                if ch - 3 >= GH:
                    to_tokens(ch - 3)
            for ch in (21, 22, 23):
                to_tokens(ch)
            dve.wait_ge(sem("gdn_in"), 16 * 9)
            v.tensor_copy(marks[:], MSTAGE)
            TWO_PI = 2.0 * math.pi
            c1 = 6.28125
            c2_ = 0.0019350051879882812
            c3 = TWO_PI - c1 - c2_
            BIG = 12582912.0
            v.tensor_copy(POSF, POSI[:])
            settle()
            for t in range(TT):
                v.tensor_scalar(ANG[:, t, :], freq, POSF[:, t:t + 1], None, ALU.mult)
            settle()
            v.tensor_scalar(KRD, ANG, 1.0 / TWO_PI, BIG, ALU.mult, ALU.add)
            settle()
            v.tensor_scalar(KRD, KRD, BIG, None, ALU.subtract)
            settle()
            for cst in (c1, c2_, c3):
                v.scalar_tensor_tensor(ANG, KRD, -cst, ANG, ALU.mult, ALU.add)
                settle()
            v.tensor_scalar(COS, ANG, math.pi / 2, None, ALU.add)
            settle()
            v.tensor_scalar(KRD, COS, math.pi, None, ALU.is_gt)
            settle()
            v.scalar_tensor_tensor(COS, KRD, -TWO_PI, COS, ALU.mult, ALU.add)
            settle()
            lim = 3.1415925
            v.tensor_scalar(COS, COS, lim, -lim, ALU.min, ALU.max)
            v.tensor_scalar(ANG, ANG, lim, -lim, ALU.min, ALU.max).then_inc(sem("angle_in"), 1)
            spent(dve, U_AB)
            ab = PS[:, 6, 0:64].rearrange("p (t c) -> p t c", c=32)
            s2 = [SPT[:, i, :].rearrange("p (t c) -> p t c", c=16) for i in range(6)]
            v.tensor_tensor(s2[0], ab[:, :, 0:16], bm(DTB, 2), ALU.add)
            settle()
            v.scalar_tensor_tensor(s2[1], s2[0], -1.0, s2[0], ALU.mult, ALU.min).then_inc(sem("decay_in"), 1)
            dve.wait_ge(sem("sq_done"), 16)
            v.tensor_scalar(RQK, RQK, 1e-6, None, ALU.add).then_inc(sem("gdn_ms"), 1)
            dve.wait_ge(sem("gdn_rs"), 1)
            for t in range(TT):
                ins = v.tensor_tensor(KN[:, :, t, :], KN[:, :, t, :], bc(RQV[:, t, 8:16], P), ALU.mult)
            ins.then_inc(sem("kn_ready"), 1)
            dve.wait_ge(sem("decay_out"), 1)
            v.scalar_tensor_tensor(s2[5], s2[0], 0.0, s2[3], ALU.max, ALU.add)
            v.tensor_scalar(s2[4], s2[4], 1.0, None, ALU.add)
            settle()
            v.reciprocal(BT, s2[4])
            v.scalar_tensor_tensor(GS, s2[5], -1.0, bm(ALOG, 2), ALU.mult, ALU.mult)
            settle()
            v.tensor_copy(TOT[:, 0, 0, 0:1], GS[:, 0, 0:1]).then_inc(sem("gs_ready"), 1)
            for u in range(2):
                for t in range(TT):
                    dve.wait_ge(sem("z_act"), 2 * u + t + 1)
                    z = Z[:, t, u * 512:(u + 1) * 512].rearrange("p (a b) -> p a b", b=P)
                    v.tensor_tensor(z, z, bm(NW, 4), ALU.mult).then_inc(sem("tok_out"), 1)
            dve.wait_ge(sem("cum_mm"), 1)
            flat = lambda a: a.rearrange("p a b c -> p (a b c)")
            v.tensor_copy(flat(GC), PS[:, 7, 0:32])
            settle()
            v.tensor_tensor(flat(KD_S), PS[:, 7, 32:64], flat(GC), ALU.subtract).then_inc(sem("decay_in"), 1)
            dve.wait_ge(sem("decay_out"), 1 + 1)

            masks = marks[:, 0:2 * 7 * P].rearrange("p (w s i) -> p w s i", w=2, s=7)
            masks32 = marks[:, 2 * 7 * P:NMASK].rearrange("p (w s i) -> p w s i", w=2, s=NSMALL + 1)
            for it in range(4):
                d, hg = it // 2, (it % 2) * 4
                fst, snd = (0, 1) if d == 0 else (1, 0)
                hs = slice(hg, hg + 4)
                for l in range(2):
                    dve.wait_ge(sem("core_setup"), 2 * it + l + 1)
                    for h in range(4):
                        ins = v.scalar_tensor_tensor(lanes[l]["DT"][:, h], pair(4 * l, P)[:, h], GC[:, d, l, hg + h:hg + h + 1],
                                                     NEGM[:, d, :], ALU.subtract, ALU.add)
                    ins.then_inc(sem("dt_in"), 1)
                for l in range(2):
                    v.tensor_copy(small[l]["U"], bm(EYE32, 4))
                for l in range(2):
                    dve.wait_ge(sem("dt_out"), 2 * it + l + 1)
                    kd, dt = lanes[l]["KD"], lanes[l]["DT"]
                    for half in (0, 2):
                        v.tensor_tensor(kd[:, half:half + 2], PS[:, 4 * l + 2 + half // 2, :].rearrange("p (a b c) -> p a b c", a=2, b=2),
                                        dt[:, half:half + 2].unsqueeze(2).to_broadcast([P, 2, 2, P]), ALU.mult)
                    settle()
                    v.scalar_tensor_tensor(kd[:, :, 0], kd[:, :, 0], -1.0, pair(4 * l + 1, P), ALU.mult, ALU.mult)
                    settle()
                    sm = small[l]
                    for r in quads:
                        v.tensor_copy(sm["AN"][r], kd[r, :, 0, r])
                    settle()
                    v.copy_predicated(sm["U"], bm(masks32[:, 1 - d, 0], 4), sm["AN"])
                    settle()
                    v.transpose(sm["Tm"].rearrange("p h c -> p (h c)"), sm["U"].rearrange("p h c -> p (h c)")).then_inc(sem("t_ready"), 1)
                v.tensor_tensor(R1, V[:, hs, fst, :], bc(BT[:, fst, d * 8 + hg:d * 8 + hg + 4], P), ALU.mult).then_inc(sem("r1_ready"), 1)
                for q in range(NSMALL):
                    for l in range(2):
                        sm = small[l]
                        dve.wait_ge(sem("q_mm"), (it * 5 + q) * 2 + l + 1)
                        v.copy_predicated(sm["Tm"], bm(masks32[:, d, q + 1], 4),
                                          PS[:, 4 * l + 1, 0:P].rearrange("p (h c) -> p h c", c=Q32)).then_inc(sem("t_grown"), 1)
                        settle()
                        v.transpose(sm["U"].rearrange("p h c -> p (h c)"), sm["Tm"].rearrange("p h c -> p (h c)")).then_inc(sem("u_grown"), 1)
                settle()
                dve.wait_ge(sem("cleared"), it + 1)
                for l in range(2):
                    for r in quads:
                        ins = v.tensor_copy(lanes[l]["Tm"][r, :, r], small[l]["Tm"][r])
                    ins.then_inc(sem("expanded"), 1)
                settle()
                for l in range(2):
                    dve.wait_ge(sem("q_mm"), (it * 5 + NSMALL) * 2 + l + 1)
                    v.copy_predicated(lanes[l]["Tm"], bm(masks[:, d, NSMALL + 1], 4), pair(4 * l + 1, P)).then_inc(sem("t_grown"), 1)
                for l in range(2):
                    dve.wait_ge(sem("r_mm"), it * 2 + l + 1)
                    v.copy_predicated(lanes[l]["U"], bm(masks[:, 1 - d, nlev_], 4), pair(4 * l + 2, P)).then_inc(sem("u_grown"), 1)
                v.tensor_tensor(lanes[fst]["Tm"], KN[:, hs, fst, :], bc(KD_S[:, d, fst, hs], P), ALU.mult).then_inc(sem("kdec"), 1)
                dve.wait_ge(sem("o_mm"), 2 * it + 1)
                o = O_ACC[:, fst, hs]
                if d == 0:
                    v.tensor_copy(o, pair(2, P))
                else:
                    v.tensor_tensor(o, pair(2, P), o, ALU.add)
                dve.wait_ge(sem("ks_mm"), it + 1)
                eg = bc(EG[:, d, snd, hs], P)
                v.tensor_tensor(R1, pair(0, P), eg, ALU.mult)
                settle()
                v.tensor_tensor(R1, V[:, hs, snd, :], R1, ALU.subtract)
                settle()
                v.tensor_tensor(R1, R1, bc(BT[:, snd, d * 8 + hg:d * 8 + hg + 4], P), ALU.mult).then_inc(sem("r1_ready"), 1)
                qs = lanes[snd]["Tm"]
                v.tensor_tensor(qs, pair(1, P), eg, ALU.mult)
                settle()
                dve.wait_ge(sem("o_mm"), 2 * it + 2)
                o = O_ACC[:, snd, hs]
                if d == 0:
                    v.tensor_tensor(o, pair(7, P), qs, ALU.add).then_inc(sem("core_done"), 1)
                else:
                    v.tensor_tensor(qs, pair(7, P), qs, ALU.add)
                    settle()
                    v.tensor_tensor(o, o, qs, ALU.add).then_inc(sem("core_done"), 1)
            settle()
            oa = O_ACC.rearrange("p t h e -> p (t h e)")
            v.tensor_tensor(GJUNK, oa, oa, ALU.mult)
            settle()
            rq, so, pw, fac = s2[0].rearrange("p a b -> p (a b)"), s2[1].rearrange("p a b -> p (a b)"), SPT[:, 2, :], SPT[:, 3, :]
            v.tensor_reduce(so[:, 0:16], GJUNK.rearrange("p (a e) -> p a e", e=P), AX, ALU.add)
            v.tensor_scalar(rq[:, 0:16].rearrange("p (t h) -> p t h", h=8), RQV[:, :, 0:8], P ** -0.5, None, ALU.mult)
            settle()
            v.tensor_tensor(so[:, 0:16], so[:, 0:16], rq[:, 0:16], ALU.mult)
            settle()
            v.tensor_tensor(so[:, 0:16], so[:, 0:16], rq[:, 0:16], ALU.mult)
            settle()
            v.tensor_scalar(so[:, 0:16], so[:, 0:16], 1.0 / P, EPS, ALU.mult, ALU.add).then_inc(sem("gdn_ms"), 1)
            dve.wait_ge(sem("gdn_rs"), 1 + 1)
            v.tensor_tensor(fac[:, 0:16], pw[:, 0:16], rq[:, 0:16], ALU.mult)
            settle()
            for t in range(TT):
                y = XN[:, t, :].rearrange("p (h e) -> p h e", e=P)
                v.tensor_tensor(y, O_ACC[:, t], bc(fac[:, t * 8:(t + 1) * 8], P), ALU.mult)
                settle()
                v.tensor_tensor(XN[:, t, :], XN[:, t, :], Z[:, t, :], ALU.mult).then_inc(sem("y_ready"), 1)
            dve.wait_ge(sem("y_turned"), 1)
            for i in (2, 3):
                v.tensor_copy(HT[:, 2 * i:2 * i + 2, :], pair(3 + i, T)).then_inc(sem("y_back"), 1)
            low(U_MLP[0], 0, 0)
            residual(1, lambda: spent(dve, U_GOUT + 1))
            if stop == "gdn":
                return

            def mlp(l):
                n0 = U_MLP[l]
                s0 = 32 * l

                def hidden_low(u):
                    dve.wait_ge(sem("act_hi"), u + (l + 2))
                    v.tensor_tensor(MT_R, MT, MTH_R.bitcast(F32), ALU.subtract).then_inc(sem("act_lo"), 1)

                def mod_unit(mi, n, turns):
                    full(dve, n, turns)
                    for k in range(KC):
                        w = W(n, 512)[:, k, :]
                        if k == 0:
                            ins = v.tensor_scalar(MA[mi], w, CACT[:, 0:1], None, ALU.mult)
                        else:
                            settle()
                            ins = v.scalar_tensor_tensor(MA[mi], w, CACT[:, k:k + 1], MA[mi], ALU.mult, ALU.add)
                    ins.then_inc(w_free[n % RING], 1)

                settle()
                dve.wait_ge(sem("act_hi"), 9 * l + 1)
                v.tensor_tensor(HT_R[:], HT[:], HTH_R.bitcast(F32), ALU.subtract).then_inc(sem("act_lo"), 1)
                low(n0 + 1, 2, s0 + 2)
                hidden_low(8 * l)
                with dve.Fori(0, 2) as i:
                    for j in range(3):
                        turns = i * MLP_TURNS
                        m = i * 3 + j
                        n = n0 + 3 + 4 * j
                        low(n, 6 + 4 * j, i * 12 + (s0 + 6 + 4 * j))
                        dve.wait_ge(sem("mod_mm"), m + 6 * l + 1)
                        mod_unit(0, n + 2, turns)
                        hidden_low(i * 3 + (8 * l + 1 + j))
                        mod_unit(1, n + 3, turns)
                        dve.wait_ge(sem("mod_mm"), m + 6 * l + 1 + 1)
                        for mi in range(2):
                            v.tensor_reduce(MSUM[:, mi * 4:mi * 4 + 4], pair(6 + mi, P), AX, ALU.add)
                        settle()
                        v.tensor_tensor(MODC[:, l, bass.ds(m * 8, 8)], MSUM,
                                        COLS[:, bass.ds(m * 8 + (COL["b_mod_2"] + 48 * l), 8)], ALU.add).then_inc(sem("mod_out"), 1)
                hidden_low(8 * l + 7)
                residual(2 + 2 * l, lambda: dve.wait_ge(sem("half_used"), 32 * (l + 1)))

            dve.wait_ge(sem("cact"), 1)
            settle()
            norm(1, 1, lambda dc: colof("norm_mlp", dc), split=True)
            mlp(0)
            if stop == "mlp0":
                return

            settle()
            norm(2, 2, lambda dc: colof("norm_mix", 8 + dc))
            dve.wait_ge(sem("rel_mm"), 1)
            v.tensor_tensor(RV[0:SH, 0:NREL], PS[0:SH, 3, 0:NREL], RMK[0:SH, 0:NREL], ALU.add).then_inc(sem("rel_vec"), 1)
            for i, (n, w, at, b) in enumerate(((4, 256, 0, 4), (5, 512, 256, 6), (6, 384, 768, 4))):
                for t in range(TT):
                    if t == 0:
                        dve.wait_ge(sem("tok_mm"), i + 1 + 2)
                    else:
                        spent(dve, U_SIN + n)
                    v.tensor_copy(SV[:, t, at:at + w], bank(b + t, w)).then_inc(sem("tok_out"), 1)
            for h in range(SH + 2):
                if h < SH:
                    dve.wait_ge(sem("scores_mm"), h + 1)
                    dve.wait_ge(sem(f"tz_in{h % 2}"), 16 * (h // 2 + 1))
                    if h >= 2:
                        dve.wait_ge(sem("p_turned"), h - 1)
                    for t in range(TT):
                        v.tensor_tensor_reduce(out=SP_[:, (h % 2) * 2 + t, :], in0=pair(h % 2, T)[:, t],
                                               in1=TZ[:, h % 2, P * (1 - t):P * (1 - t) + T], scale=1.0, scalar=-3e38,
                                               op0=ALU.add, op1=ALU.max, accum_out=MX[:, t, h:h + 1]).then_inc(sem("s_biased"), 1)
                    settle()
                    v.tensor_scalar(NMX[:, :, h], MX[:, :, h], -1.0, None, ALU.mult).then_inc(sem("row_max"), 1)
                if h >= 2:
                    g = h - 2
                    dve.wait_ge(sem("s_pv"), g + 1)
                    v.tensor_copy(SO[:, :, g * SE:(g + 1) * SE], pair(4 + g % 2, SE)[:, 0:2]).then_inc(sem("s_o_out"), 1)
            dve.wait_ge(sem("exp_done"), 2 * SH)
            by_group = lambda a: a.rearrange("p t (g j) -> p t j g", g=3)
            v.tensor_reduce(MM, by_group(MX), AX, ALU.max)
            settle()
            for g in range(3):
                js = slice(g * SGRP, (g + 1) * SGRP)
                ins = v.tensor_tensor(SS[:, :, js], MX[:, :, js], MM, ALU.subtract)
            ins.then_inc(sem("angle_in"), 1)
            dve.wait_ge(sem("angle_out"), 1 + 1)
            v.tensor_tensor(SS, SM, SC, ALU.mult)
            settle()
            v.tensor_reduce(DEN, by_group(SS), AX, ALU.add)
            settle()
            v.reciprocal(DEN, DEN)
            settle()
            for g in range(3):
                js = slice(g * SGRP, (g + 1) * SGRP)
                v.tensor_tensor(SC[:, :, js], SC[:, :, js], DEN, ALU.mult)
            settle()
            for t in range(TT):
                o = SO[:, t, :].rearrange("p (h e) -> p h e", e=SE)
                v.tensor_tensor(o, o, bc(SC[:, t, :], SE), ALU.mult).then_inc(sem("y_ready"), 1)
            dve.wait_ge(sem("y_turned"), 1 + 1)
            for i in (1, 3):
                v.tensor_copy(SOT[:, 2 * i:2 * i + 2, :], pair(i, T)).then_inc(sem("y_back"), 1)
            low(U_MLP[1], 0, 32)
            residual(3, lambda: spent(dve, U_SOUT + 2))
            settle()
            norm(3, 3, lambda dc: colof("norm_mlp", 8 + dc), split=True)
            mlp(1)
            settle()
            mean_square(4)
            dve.wait_ge(sem("fgr_in"), 16)
            for t in range(TT):
                v.scalar_tensor_tensor(X[:, t, :], X[:, t, :], rstd[:, t:t + 1], FGR, ALU.mult, ALU.mult).then_inc(
                    sem(("x_half", "x_ready")[t]), 1)
            settle()
            if stop == "b1":
                return

            dve.wait_ge(sem("angle_out"), 1)

            def rotate(x1, x2, t, shape):
                cs, sn = COS[:, t, :], SIN[:, t, :]
                r = [RT[:, i, 0:16] if shape is None else RT[:, i, :].rearrange("p (h e) -> p h e", e=16) for i in range(4)]
                if shape is not None:
                    cs, sn = bm(cs, shape), bm(sn, shape)
                v.tensor_tensor(r[0], x1, cs, ALU.mult)
                v.tensor_tensor(r[1], x2, sn, ALU.mult)
                v.tensor_tensor(r[2], x1, sn, ALU.mult)
                v.tensor_tensor(r[3], x2, cs, ALU.mult)
                settle()
                v.tensor_tensor(x1, r[0], r[1], ALU.subtract)
                ins = v.tensor_tensor(x2, r[2], r[3], ALU.add)
                settle()
                return ins

            def gated_residual(n, tile1_ready):
                dve.wait_ge(sem("gr_out"), n)
                for b in range(4):
                    t, h = b // 2, b % 2
                    xs = X[:, t, h * 512:(h + 1) * 512]
                    v.tensor_tensor(TMP, bank(b), GR[:, h * 512:(h + 1) * 512], ALU.mult)
                    settle()
                    ins = v.tensor_tensor(xs, xs, TMP, ALU.add)
                    if b == 1:
                        ins.then_inc(sem("x_half"), 1)
                        tile1_ready()
                    elif b < 3:
                        settle()
                ins.then_inc(sem("x_ready"), 1)
                settle()

            with dve.Fori(0, NL) as L:
                tu = L * SEC_TURNS
                u2 = U_SEC
                mc = lambda k: MODC[:].rearrange("p l c -> p (l c)")[:, bass.ds(L * 48 + k * 8, 8)]
                pc = lambda name, w: COLS[:, bass.ds(L * w + COL[name], w)]
                def columns():
                    v.scalar_tensor_tensor(SCL, mc(1), 1.0, pc("norm1_g_2", 8), ALU.add, ALU.mult)
                    v.tensor_copy(BIA, mc(0))
                    v.tensor_copy(GCOL[:, 0:8], mc(2))
                    v.tensor_copy(GCOL[:, 8:16], mc(5))
                    v.tensor_copy(PSC, pc("pool_scale_2", 8))
                    v.tensor_copy(BG, pc("b_gate_2", 24))
                    v.tensor_copy(CW, pc("conv_w_2", 12))
                    v.tensor_copy(QKG[:, 0:3], pc("q_norm_g_2", 3))
                    v.tensor_copy(QKG[:, 3:5], pc("kv_norm_g_2", 2))
                    settle()
                    v.memset(CZ[:, :, 0:1], 0.0)
                    v.memset(CZ[:, :, 257:258], 0.0).then_inc(sem("gcol"), 1)

                norm(L * 2 + 5, L * 2 + 4, lambda dc: SCL[:, dc:dc + 1], lambda dc: BIA[:, dc:dc + 1], meanwhile=columns)
                for t in range(TT):
                    if t == 0:
                        dve.wait_ge(sem("cq_mm"), L + 1)
                    else:
                        spent(dve, u2 + V_CQ, tu)
                    v.tensor_copy(CQ[:, t, 0:QR], bank(t, QR)).then_inc(sem("cq_out"), 1)
                for t in range(TT):
                    if t == 0:
                        dve.wait_ge(sem("kv_mm"), L + 1)
                    else:
                        spent(dve, u2 + V_KV, tu)
                    v.tensor_copy(CQ[:, t, QR:QKW], bank(2 + t, KVR)).then_inc(sem("cq_out"), 1)
                    ins = v.tensor_copy(KR[:, t, :], PS[:, 2 + t, KVR:KVR + ROPE])
                ins.then_inc(sem("ckv_out"), 1)
                dve.wait_ge(sem("sq2"), L + 1)
                v.tensor_scalar(VAR2[:, 0:2], SS2[:, 0:2], 1.0 / QR, EPS, ALU.mult, ALU.add)
                v.tensor_scalar(VAR2[:, 2:4], SS2[:, 2:4], 1.0 / KVR, EPS, ALU.mult, ALU.add).then_inc(sem("var2"), 1)
                dve.wait_ge(sem("rs2"), L + 1)
                for t in range(TT):
                    v.tensor_scalar(CQ[:, t, 0:QR], CQ[:, t, 0:QR], RS2[:, t:t + 1], None, ALU.mult)
                    ins = v.tensor_scalar(CQ[:, t, QR:QKW], CQ[:, t, QR:QKW], RS2[:, 2 + t:3 + t], None, ALU.mult)
                ins.then_inc(sem("cqn_ready"), 1)
                for t in range(TT):
                    rotate(KR[:, t, 0:16], KR[:, t, 16:32], t, None)
                    v.tensor_copy(MK[:, t, :, NOPE:DQK], bm(KR[:, t, :], MH))
                dve.wait_ge(sem("cx_out"), L + 1)
                spent(dve, u2 + V_CC, tu)
                for b in range(2):
                    v.tensor_tensor(CZ[:, 2 * b:2 * b + 2, 1:257], pair(b, T), CX[:, 2 * b:2 * b + 2, :], ALU.mult)
                settle()
                for ch in range(4):
                    v.tensor_scalar(BCT[:, ch, :], CZ[:, ch, 0:T], CW[:, ch:ch + 1], None, ALU.mult)
                for k in (1, 2):
                    settle()
                    for ch in range(4):
                        v.scalar_tensor_tensor(BCT[:, ch, :], CZ[:, ch, k:k + T], CW[:, 4 * k + ch:4 * k + ch + 1], BCT[:, ch, :],
                                               ALU.mult, ALU.add)
                settle()
                spent(dve, u2 + V_CB, tu)
                for b in range(2):
                    ins = v.tensor_tensor(BCT[:, 2 * b:2 * b + 2, :], pair(2 + b, T), BCT[:, 2 * b:2 * b + 2, :], ALU.mult)
                ins.then_inc(sem("conv_y"), 1)
                dve.wait_ge(sem("mq_raw"), L + 1)
                for t in range(TT):
                    rotate(MQ[:, t, :, NOPE:NOPE + 16], MQ[:, t, :, NOPE + 16:DQK], t, MH)
                v.tensor_copy(RT[:, 0, 0:1], MQ[:, 0, 0, NOPE:NOPE + 1]).then_inc(sem("mq_ready"), 1)
                spent(dve, u2 + V_UKV, tu)
                for b in range(4):
                    t, h = b // 2, b % 2
                    v.tensor_copy(MK[:, t, 4 * h:4 * h + 4, 0:NOPE], pair(b, P)[:, :, 0:NOPE]).then_inc(sem("mk_ready"), 1)
                for g in range(8):
                    if g % 2 == 1:
                        dve.wait_ge(sem("mqk_mm"), L * 8 + g + 1)
                        dst, b = (QT, 4 + g) if g < 4 else (KT, g - 4)
                        gg = g % 4
                        v.tensor_copy(dst[0:DQK, 2 * gg:2 * gg + 2, :], pair(b, T)[0:DQK]).then_inc(sem("mqk_out"), 1)
                for h in range(MH + 1):
                    if h < MH:
                        dve.wait_ge(sem("scores_mm"), L * 8 + h + 1 + SH)
                        v.tensor_reduce(MNM[:, h, :], pair(h % 2, T), AX, ALU.max, negate=True).then_inc(sem("row_max"), 1)
                    if h >= 1:
                        g = h - 1
                        dve.wait_ge(sem("exp_done"), L * 16 + 2 * g + 2 + 2 * SH)
                        v.reciprocal(MSM[:, g, :], MSM[:, g, :])
                        settle()
                        for t in range(TT):
                            pt = (MP, MP2)[g % 2][:, t, :]
                            ins = v.tensor_scalar(pt, pt, MSM[:, g, t:t + 1], None, ALU.mult)
                        ins.then_inc(sem("m_p"), 1)
                dve.wait_ge(sem("m_pv"), L * 2 + 2)
                v.tensor_copy(OT[:, 2:4, :], pair(5, T)).then_inc(sem("ot_out"), 1)
                for q in range(24):
                    b, dc = q // 8, q % 8
                    dve.wait_ge(sem("gate_out"), L * 24 + q + 1)
                    if dc == 7 and b != 1:
                        spent(dve, u2 + (V_OA if b == 0 else V_OC), tu)
                    else:
                        dve.wait_ge(sem("branch_mm"), L * 22 + (0, 7, 15)[b] + dc + 1)
                    y, sg, mg, MTMP = bank(2 + q % 2, T), SG[:, q % 2, :], MG[:, dc, :], MT2[:, q % 2, :]
                    if b == 0:
                        v.tensor_tensor(mg, y, sg, ALU.mult).then_inc(sem("merge"), 1)
                    else:
                        if b == 1:
                            v.scalar_tensor_tensor(MTMP, y, PSC[:, dc:dc + 1], sg, ALU.mult, ALU.mult)
                        else:
                            v.tensor_tensor(MTMP, y, sg, ALU.mult)
                        settle()
                        v.tensor_tensor(mg, mg, MTMP, ALU.add).then_inc(sem("merge"), 1)
                dve.wait_ge(sem("half_mm"), L + 5)
                gated_residual(L * 2 + 1, lambda: (settle(), spent(dve, u2 + V_OUT + 1, tu)))

                v.scalar_tensor_tensor(SCL, mc(4), 1.0, pc("norm2_g_2", 8), ALU.add, ALU.mult)
                v.tensor_copy(BIA, mc(3))
                settle()
                norm(L * 2 + 6, L * 2 + 5, lambda dc: SCL[:, dc:dc + 1], lambda dc: BIA[:, dc:dc + 1])
                dve.wait_ge(sem("router_mm"), L + 1)
                v.tensor_reduce(RM, PS[:, 4, 0:TT * NE].rearrange("p (t e) -> p t e", e=NE), AX, ALU.max, negate=True).then_inc(sem("rm"), 1)
                dve.wait_ge(sem("aff_exp"), L + 1)
                v.reciprocal(RIN, RSM)
                settle()
                for t in range(TT):
                    ins = v.tensor_scalar(AFF[:, t, :], AFF[:, t, :], RIN[:, t:t + 1], None, ALU.mult)
                ins.then_inc(sem("aff_ready"), 1)
                dve.wait_ge(sem("aff_turned"), L + 1)
                v.tensor_copy(AT[0:NE, :], PS[0:NE, 5, 0:T])
                cur, other = AT[0:NE, :], AT2[0:NE, :]
                for r in range(CAP // 8):
                    settle()
                    best = VALS[0:NE, 8 * r:8 * r + 8]
                    v.max(best, cur)
                    settle()
                    v.max_index(IDXU[:, 8 * r:8 * r + 8], best, cur)
                    v.match_replace(other, best, cur, -1.0)
                    cur, other = other, cur
                settle()
                v.tensor_copy(IDXF[0:NE, :], IDXU[:])
                settle()
                eye16 = ident[0:NE, 0:NE].unsqueeze(2).to_broadcast([NE, NE, CAP])
                for j, src in enumerate((IDXF, VALS)):
                    ins = v.tensor_tensor(BD[0:NE, j, :].rearrange("p (e s) -> p e s", s=CAP), bm(src[0:NE, :], NE), eye16, ALU.mult)
                ins.then_inc(sem("bd_ready"), 1)
                dve.wait_ge(sem("picks_mm"), L + 1)
                for t in range(TT):
                    ins = v.tensor_scalar(ST[:, t, :], bank(6), tokid[:, t:t + 1], None, ALU.is_equal)
                ins.then_inc(sem("st_ready"), 1)
                settle()
                for t in range(TT):
                    v.tensor_tensor(STV[:, t, :], bank(7), ST[:, t, :], ALU.mult)
                for dc in range(1, KC, 2):
                    dve.wait_ge(sem("xg_mm"), L * 8 + dc + 1)
                    v.tensor_scalar(XG[:, dc, :], bank(dc % 4), SCL[:, dc:dc + 1], BIA[:, dc:dc + 1],
                                    ALU.mult, ALU.add).then_inc(sem("xg_out1"), 1)
                settle()
                with dve.Fori(0, NE) as e:
                    te = tu + e
                    w = u2 + V_MOE
                    ev = L * NE + e
                    dve.wait_ge(w_free[(w + 3) % RING], te + (w + 3) // RING)
                    dve.wait_ge(sem("xg_out0"), L * 4 + 4)
                    v.tensor_copy(XGE, XG[:, :, bass.ds(e * CAP, CAP)]).then_inc(sem("xge_ready"), 1)
                    dve.wait_ge(sem("s4_mm"), ev + 1)
                    for t in range(TT):
                        ins = v.tensor_copy(SREP[:, t], STV[:, t, bass.ds(e * CAP, CAP)].unsqueeze(1).to_broadcast([P, 4, CAP]))
                    ins.then_inc(sem("srep_ready"), 1)
                    dve.wait_ge(sem("silg"), ev + 1)
                    spent(dve, w + 3, te)
                    v.tensor_tensor(HE, bank(5, T), SILG, ALU.mult).then_inc(sem("he_ready"), 1)
                    dve.wait_ge(sem("expert_done"), ev + 1)
                    for u in range(2):
                        spent(dve, w + 4 + u, te)
                        v.tensor_copy(YS[:, u, :], bank((7, 4)[u])).then_inc(sem("ys_out"), 1)
                dve.wait_ge(sem("expert_done"), L * NE + NE + 1)
                gated_residual(L * 2 + 2, settle)
            mean_square(9)
            dve.wait_ge(sem("fgr_in"), 32)
            for t in range(TT):
                v.scalar_tensor_tensor(X[:, t, :], X[:, t, :], rstd[:, t:t + 1], FGR2, ALU.mult, ALU.mult).then_inc(sem("x_ready"), 1)

        @block.scalar
        def _(act):
            a = nc.scalar
            settle = a.drain

            def mean_square(r, x_count):
                if x_count is not None:
                    act.wait_ge(sem("x_half"), x_count)
                a.activation(XN[:, 0, :], X[:, 0, :], ACT.Square, accum_out=ssq[:, 0:1])
                settle()
                a.activation(var[:, 0:1], ssq[:, 0:1], ACT.Identity, scale=1.0 / D, bias=eps[:]).then_inc(sem("var0"), 1)

            def norm(r, j, x_count, scale, shift=None, split=False):
                mean_square(r, x_count)
                act.wait_ge(sem("rstd_ready"), r * 2 + 1)
                a.activation(XN[:, 0, :], X[:, 0, :], ACT.Copy, scale=rstd[:, 0:1]).then_inc(sem("xn0"), 1)
                act.wait_ge(sem("ht_psum"), j + 1)
                for dc in range(4):
                    src = pair(4 + dc // 2, T)[:, dc % 2]
                    a.activation(HT[:, dc, :], src, ACT.Identity, scale=scale(dc),
                                 bias=0.0 if shift is None else shift(dc)).then_inc(sem("ht_ready"), 1)
                if split:
                    settle()
                    a.copy(HTH_R[:, 0:4, :], HT[:, 0:4, :]).then_inc(sem("act_hi"), 1)

            def high(n, turns, idx, base, s0=0):
                full(act, n, turns)
                for hf in range(2):
                    b = (idx + hf) % 4
                    if idx >= 4:
                        act.wait_ge(sem("half_used"), base * 12 + (s0 + idx + hf - 3))
                    a.copy(WH[b], W(n, SLOT)[:, 0, hf * HALF:(hf + 1) * HALF]).then_inc(sem("hi"), 1)

            act.wait_ge(sem("cols_psum"), 1)
            for n, group in enumerate(ROWS):
                cnt = sum(x for _, x in group)
                a.copy(COLS[:, n * P:n * P + cnt], PS[:, 3, n * P:n * P + cnt]).then_inc(sem("cols_ready"), 1)
            settle()
            a.activation(CACT[:], COLS[:, COL["c_2"]:COL["c_2"] + 8], ACT.Silu).then_inc(sem("cact"), 1)
            act.wait_ge(sem("x_in"), 16)
            act.wait_ge(sem("filled"), 1)
            norm(0, 0, None, lambda dc: colof("norm_mix", dc))

            def conv_in(ch):
                qkv_piece(act, ch)
                if ch >= 3:
                    act.wait_ge(sem("conv_out"), ch - 2)
                a.copy(CP[:, ch % 3, 2:2 + T], bank(ch % 4, T)).then_inc(sem("chunk_out"), 1)

            def silu(ch):
                act.wait_ge(sem("conv_out"), ch + 1)
                dst = KQT[:, ch, 1, :] if ch < GH else KQT[:, ch - GH, 0, :] if ch < 2 * GH else CV[:, ch % 3, :]
                a.activation(dst, CV[:, ch % 3, :], ACT.Silu).then_inc(sem("silu"), 1)

            def squares(ch):
                if ch < GH:
                    act.wait_ge(sem("turned"), ch + 1)
                else:
                    act.wait_ge(sem("tok_done"), ch - GH + 1)
                for t in range(TT):
                    src = pair(4 + ch % 2, P)[:, t] if ch < GH else KN[:, ch - GH, t, :]
                    a.activation(JUNK, src, ACT.Square, accum_out=RQK[:, t, ch:ch + 1])
                    settle()
                a.copy(ajunk[:], RQK[:, 1, ch:ch + 1]).then_inc(sem("sq_done"), 1)

            for ch in range(24):
                conv_in(ch)
                if ch >= 1:
                    silu(ch - 1)
                if ch >= 3 and ch - 3 < 16:
                    squares(ch - 3)
            silu(23)
            for u in range(2):
                for t in range(TT):
                    if t == 0:
                        act.wait_ge(sem("tok_mm"), u + 1)
                    else:
                        spent(act, U_Z + u)
                    a.activation(Z[:, t, u * 512:(u + 1) * 512], bank(2 * u + t), ACT.Silu).then_inc(sem("z_act"), 1)
            act.wait_ge(sem("decay_in"), 1)
            act.wait_ge(sem("gdn_in"), 16 * 9)
            s2 = [SPT[:, i, :].rearrange("p (t c) -> p t c", c=16) for i in range(6)]
            a.activation(s2[2], s2[1], ACT.Exp)
            a.activation(s2[4], PS[:, 6, 0:64].rearrange("p (t c) -> p t c", c=32)[:, :, 16:32], ACT.Exp, scale=-1.0)
            a.activation(ALOG, ALOG, ACT.Exp)
            settle()
            a.activation(s2[3], s2[2], ACT.Ln, bias=1.0).then_inc(sem("decay_out"), 1)
            for g in range(4):
                act.wait_ge(sem("knt_mm"), g + 1)
                a.copy(KQT[:, 2 * g:2 * g + 2, 0, :], pair(4 + g % 2, T)).then_inc(sem("knt_done"), 1)
            act.wait_ge(sem("decay_in"), 1 + 1)
            a.activation(EG, GC, ACT.Exp)
            a.activation(KD_S, KD_S, ACT.Exp).then_inc(sem("decay_out"), 1)
            for it in range(4):
                for l in range(2):
                    act.wait_ge(sem("dt_in"), 2 * it + l + 1)
                    a.activation(lanes[l]["DT"], lanes[l]["DT"], ACT.Exp).then_inc(sem("dt_out"), 1)
                for q in range(NSMALL):
                    for l in range(2):
                        act.wait_ge(sem("p_mm"), (it * nlev_ + q) * 2 + l + 1)
                        a.copy(small[l]["PP"].rearrange("p h c -> p (h c)"), PS[:, 4 * l, 0:P]).then_inc(sem("p_out"), 1)
                act.wait_ge(sem("cleared"), it + 1)
                for l in range(2):
                    act.wait_ge(sem("u_grown"), (it * nlev_ + NSMALL - 1) * 2 + l + 1)
                    for r in quads:
                        a.copy(lanes[l]["U"][r, :, r], small[l]["U"][r])
                for l in range(2):
                    act.wait_ge(sem("p_mm"), (it * nlev_ + NSMALL) * 2 + l + 1)
                    a.copy(lanes[l]["DT"], pair(4 * l, P)).then_inc(sem("p_out"), 1)
                for l in range(2):
                    act.wait_ge(sem("t_turned"), 2 * it + l + 1)
                    a.copy(lanes[l]["U"], pair(4 * l + 2, P)).then_inc(sem("u_grown"), 1)
                for l in range(2):
                    act.wait_ge(sem("p_mm"), (it * nlev_ + NSMALL + 1) * 2 + l + 1)
                    a.copy(lanes[l]["DT"], pair(4 * l, P)).then_inc(sem("p_out"), 1)
                for i in range(2):
                    act.wait_ge(sem("vn_mm"), 2 * it + i + 1)
                    if i == 1:
                        act.wait_ge(sem("o_mm"), 2 * it + 1)
                    a.copy(VN, pair(6, P)).then_inc(sem("vn_out"), 1)
                    if i == 0:
                        act.wait_ge(sem("s_mm"), it + 1)
                        a.copy(SST, pair(7, P)).then_inc(sem("s_out"), 1)
            act.wait_ge(sem("angle_in"), 1)
            a.activation(SIN, ANG, ACT.Sin)
            a.activation(COS, COS, ACT.Sin).then_inc(sem("angle_out"), 1)
            act.wait_ge(sem("y_turned"), 1)
            for i in (0, 1):
                a.copy(HT[:, 2 * i:2 * i + 2, :], pair(3 + i, T)).then_inc(sem("y_back"), 1)
            high(U_MLP[0], 0, 0, 0)
            if stop == "gdn":
                return

            def mlp(l):
                s0 = 32 * l

                def relu(u, t, used_halves):
                    if t == 0:
                        act.wait_ge(sem("up_mm"), u + 1)
                    else:
                        act.wait_ge(sem("half_used"), used_halves)
                    act.wait_ge(sem("rl_turned"), u)
                    a.activation(RL[:, t, :], bank(4 + t), ACT.Relu).then_inc(sem("relu"), 1)

                def square(u):
                    act.wait_ge(sem("rl_turned"), u + 1)
                    for i in range(2):
                        a.activation(MT[:, 2 * i:2 * i + 2, :], pair(6 + i, T), ACT.Square)
                    settle()
                    a.copy(MTH_R, MT).then_inc(sem("act_hi"), 1)

                n0 = U_MLP[l]
                high(n0 + 1, 0, 2, 0, s0)
                for t in range(TT):
                    relu(8 * l, t, s0 + 2)
                high(n0 + 2, 0, 4, 0, s0)
                relu(8 * l + 1, 0, None)
                square(8 * l)
                relu(8 * l + 1, 1, s0 + 4)
                with act.Fori(0, 2) as i:
                    for j in range(3):
                        u = i * 3 + (8 * l + 1 + j)
                        n = n0 + 3 + 4 * j
                        idx = 6 + 4 * j
                        high(n, i * MLP_TURNS, idx, i, s0)
                        high(n + 1, i * MLP_TURNS, idx + 2, i, s0)
                        relu(u + 1, 0, None)
                        square(u)
                        relu(u + 1, 1, i * 12 + (s0 + idx + 2))
                high(n0 + 27, 0, 30, 0, s0)
                square(8 * l + 7)

            norm(1, 1, 1, lambda dc: colof("norm_mlp", dc), split=True)
            mlp(0)
            if stop == "mlp0":
                return
            norm(2, 2, 2, lambda dc: colof("norm_mix", 8 + dc))
            for ch in range(18):
                if ch % 4 == 3:
                    spent(act, U_SIN + ch // 4)
                else:
                    act.wait_ge(sem("chunk_mm"), 3 * (ch // 4) + ch % 4 + 1 + 18)
                src = bank(ch % 4, T)
                if ch < 9:
                    back = bass.AP(src.tensor, src.offset + P - 1, [list(src.ap[0]), [P, TT], [-1, P]])
                    ins = a.activation(SQKT[:, ch, :].rearrange("p (t q) -> p t q", q=P), back, ACT.Copy, scale=SE ** -0.5)
                else:
                    ins = a.copy(SQKT[:, ch, :], src)
                ins.then_inc(sem("chunk_out"), 1)
            for h in range(SH + 1):
                if h < SH:
                    act.wait_ge(sem("row_max"), h + 1)
                    for t in range(TT):
                        p = SP_[:, (h % 2) * 2 + t, :]
                        a.activation(p, p, ACT.Exp, bias=NMX[:, t, h:h + 1], accum_out=SM[:, t, h:h + 1]).then_inc(sem("exp_done"), 1)
                if h >= 1:
                    g = h - 1
                    act.wait_ge(sem("p_turned"), g + 1)
                    a.copy(SPT2[:, g % 2], pair(2 + g % 2, T)).then_inc(sem("pt_out"), 1)
            act.wait_ge(sem("angle_in"), 1 + 1)
            a.activation(SC, SS, ACT.Exp).then_inc(sem("angle_out"), 1)
            act.wait_ge(sem("y_turned"), 1 + 1)
            for i in (0, 2, 4):
                w = 2 if i < 4 else 1
                a.copy(SOT[:, 2 * i:2 * i + w, :], pair(i, T)[:, 0:w]).then_inc(sem("y_back"), 1)
            high(U_MLP[1], 0, 0, 0)
            norm(3, 3, 3, lambda dc: colof("norm_mlp", 8 + dc), split=True)
            mlp(1)
            mean_square(4, 4)
            if stop == "b1":
                return
            with act.Fori(0, NL) as L:
                tu = L * SEC_TURNS
                u2 = U_SEC
                norm(L * 2 + 5, L * 2 + 4, L * 2 + 5, lambda dc: SCL[:, dc:dc + 1], lambda dc: BIA[:, dc:dc + 1])
                for i, (b, w, name, n) in enumerate(((0, QR, "cq_mm", V_CQ), (2, KVR, "kv_mm", V_KV))):
                    for t in range(TT):
                        act.wait_ge(sem("cq_out"), L * 4 + 2 * i + t + 1)
                        a.activation(TMP[:, 0:w], CQ[:, t, b * (QR // 2):b * (QR // 2) + w], ACT.Square, accum_out=SS2[:, 2 * i + t:2 * i + t + 1])
                        settle()
                a.copy(ajunk[:], SS2[:, 3:4]).then_inc(sem("sq2"), 1)
                for t in range(TT):
                    if t == 0:
                        act.wait_ge(sem("pu_mm"), L + 1)
                    else:
                        spent(act, u2 + V_PU, tu)
                    ins = a.copy(PU[:, t, :], bank(4 + t))
                ins.then_inc(sem("pu_out"), 1)
                spent(act, u2 + V_CX, tu)
                for b in range(2):
                    ins = a.copy(CX[:, 2 * b:2 * b + 2, :], pair(6 + b, T))
                ins.then_inc(sem("cx_out"), 1)
                act.wait_ge(sem("cqt_mm"), L + 1)
                for cc in range(5):
                    a.activation(CQT[:, cc, :], pair(4 + cc // 2, T)[:, cc % 2], ACT.Copy, scale=QKG[:, cc:cc + 1]).then_inc(sem("cqt_out"), 1)
                for j in range(2):
                    act.wait_ge(sem("mix_mm"), L * 2 + j + 1)
                    a.copy(MIXT[:, 2 * j:2 * j + 2, :], pair(7, T)).then_inc(sem("mix_out"), 1)
                spent(act, u2 + V_UQ, tu)
                for b in range(4):
                    t, h = b // 2, b % 2
                    ins = a.activation(MQ[:, t, 4 * h:4 * h + 4, :].rearrange("p a b -> p (a b)"), bank(4 + b, 384), ACT.Copy, scale=DQK ** -0.5)
                ins.then_inc(sem("mq_raw"), 1)
                for b in range(4):
                    t, h = b // 2, b % 2
                    act.wait_ge(sem("mk_ready"), L * 4 + b + 1)
                    ins = a.copy(MV[:, t, 4 * h:4 * h + 4, :], pair(b, P)[:, :, NOPE:P])
                ins.then_inc(sem("mv_out"), 1)
                for g in range(0, 8, 2):
                    act.wait_ge(sem("mqk_mm"), L * 8 + g + 1)
                    dst, b = (QT, 4 + g) if g < 4 else (KT, g - 4)
                    gg = g % 4
                    a.copy(dst[0:DQK, 2 * gg:2 * gg + 2, :], pair(b, T)[0:DQK]).then_inc(sem("mqk_out"), 1)
                for h in range(MH + 1):
                    if h < MH:
                        act.wait_ge(sem("row_max"), L * 8 + h + 1 + SH)
                        if h >= 2:
                            act.wait_ge(sem("p_turned"), L * 8 + h - 1 + SH)
                        for t in range(TT):
                            a.activation((MP, MP2)[h % 2][:, t, :], pair(h % 2, T)[:, t], ACT.Exp, bias=MNM[:, h, t:t + 1],
                                         accum_out=MSM[:, h, t:t + 1]).then_inc(sem("exp_done"), 1)
                    if h >= 1:
                        g = h - 1
                        act.wait_ge(sem("p_turned"), L * 8 + g + 1 + SH)
                        a.copy(MPT[g % 2], pair(2 + g % 2, T)).then_inc(sem("pt_out"), 1)
                act.wait_ge(sem("m_pv"), L * 2 + 1)
                a.copy(OT[:, 0:2, :], pair(4, T)).then_inc(sem("ot_out"), 1)
                for q in range(24):
                    if q % 4 == 3:
                        spent(act, u2 + V_GL[q // 4], tu)
                    else:
                        act.wait_ge(sem("gate_mm"), L * 18 + 3 * (q // 4) + q % 4 + 1)
                    if q >= 2:
                        act.wait_ge(sem("merge"), L * 24 + q - 1)
                    a.activation(SG[:, q % 2, :], bank(q % 2, T), ACT.Sigmoid, bias=BG[:, q:q + 1]).then_inc(sem("gate_out"), 1)
                act.wait_ge(sem("spread"), L * 2 + 1)
                a.copy(GR, PS[:, 4:6, :].rearrange("p a b -> p (a b)")).then_inc(sem("gr_out"), 1)
                norm(L * 2 + 6, L * 2 + 5, L * 2 + 6, lambda dc: SCL[:, dc:dc + 1], lambda dc: BIA[:, dc:dc + 1])
                act.wait_ge(sem("rm"), L + 1)
                for t in range(TT):
                    a.activation(AFF[:, t, :], PS[:, 4, t * NE:(t + 1) * NE], ACT.Exp, bias=RM[:, t:t + 1], accum_out=RSM[:, t:t + 1])
                    settle()
                a.copy(ajunk[:], RSM[:, 1:2]).then_inc(sem("aff_exp"), 1)
                act.wait_ge(sem("spread"), L * 2 + 2)
                a.copy(GR, PS[:, 2:4, :].rearrange("p a b -> p (a b)")).then_inc(sem("gr_out"), 1)
                for dc in range(0, KC, 2):
                    act.wait_ge(sem("xg_mm"), L * 8 + dc + 1)
                    a.activation(XG[:, dc, :], bank(dc % 4), ACT.Identity, scale=SCL[:, dc:dc + 1], bias=BIA[:, dc:dc + 1]).then_inc(sem("xg_out0"), 1)
                with act.Fori(0, NE) as e:
                    te = tu + e
                    w = u2 + V_MOE
                    ev = L * NE + e
                    spent(act, w + 1, te)
                    act.wait_ge(sem("he_ready"), ev + 1)
                    a.activation(SILG, bank(4, T), ACT.Silu).then_inc(sem("silg"), 1)
                    act.wait_ge(sem("s4_mm"), ev + 1 + 1)
                    act.wait_ge(sem("expert_done"), ev + 1)
                    a.copy(S4, PS[:, 6, T:2 * T]).then_inc(sem("s4_out"), 1)
                    act.wait_ge(sem("hte_mm"), ev + 1)
                    a.copy(HTE, pair(6, P)[:, 0:2]).then_inc(sem("hte_out"), 1)
            mean_square(9, 9)

        @block.gpsimd
        def _(pool):
            g = nc.gpsimd
            for name in CREDITED:
                g.sem_inc(sem(name), 1)
            g.memset(zero1, 0.0)
            g.memset(CP[:, :, 0:2], 0.0)
            g.memset(nhalf[:], -0.5)
            g.memset(eps[:], EPS)
            g.memset(CP[:, :, 258:260], 0.0).then_inc(sem("filled"), 1)
            g.drain()

            def rsqrt(out, x, n):
                return g.tensor_tensor(out, x, nhalf[:, 0:n], ALU.pow)

            def norm(r):
                for t in range(TT):
                    pool.wait_ge(sem(f"var{t}"), r + 1)
                    rsqrt(rstd[:, t:t + 1], var[:, t:t + 1], 1).then_inc(sem("rstd_ready"), 1)

            norm(0)
            pool.wait_ge(sem("gdn_ms"), 1)
            rsqrt(RQV.rearrange("p a b -> p (a b)"), RQK.rearrange("p a b -> p (a b)"), 32).then_inc(sem("gdn_rs"), 1)
            for it in range(4):
                if it == 0:
                    pool.wait_ge(sem("decay_in"), 1 + 1)
                else:
                    pool.wait_ge(sem("core_done"), it)
                for l in range(2):
                    g.memset(lanes[l]["Tm"], 0.0)
                    ins = g.memset(lanes[l]["U"], 0.0)
                ins.then_inc(sem("cleared"), 1)
            pool.wait_ge(sem("gdn_ms"), 1 + 1)
            rsqrt(SPT[:, 2, 0:16], SPT[:, 1, 0:16], 16).then_inc(sem("gdn_rs"), 1)
            if stop == "gdn":
                return

            def mlp(l):
                s0, n0 = 32 * l, U_MLP[l]

                def low(n, idx, done):
                    for hf in range(2):
                        pool.wait_ge(sem("hi"), done + hf + 1)
                        b = (idx + hf) % 4
                        ins = g.tensor_tensor(WL[b], W(n, SLOT)[:, 0, hf * HALF:(hf + 1) * HALF], WH[b].bitcast(F32), ALU.subtract)
                        ins.then_inc(sem("w2_first_lo") if hf == 0 else w_free[n % RING], 1)

                low(n0 + 2, 4, s0 + 4)
                with pool.Fori(0, 2) as i:
                    for j in range(3):
                        low(n0 + 4 + 4 * j, 8 + 4 * j, i * 12 + (s0 + 8 + 4 * j))
                low(n0 + 27, 30, s0 + 30)

            norm(1)
            mlp(0)
            if stop == "mlp0":
                return
            norm(2)
            norm(3)
            mlp(1)
            norm(4)
            if stop == "b1":
                return
            with pool.Fori(0, NL) as L:
                norm(L * 2 + 5)
                pool.wait_ge(sem("var2"), L + 1)
                rsqrt(RS2, VAR2, 4).then_inc(sem("rs2"), 1)
                norm(L * 2 + 6)
            norm(9)


NAMES = ("x norm_mix norm_mlp norm_final rel_bias gdn_w_in gdn_conv_w gdn_a_log gdn_dt_bias gdn_norm_w gdn_w_out "
         "dswa_w_in dswa_w_out mlp_w1 mlp_w2 c_2 positions_2 w_mod_2 b_mod_2 norm1_g_2 w_in_2 b_gate_2 q_norm_g_2 "
         "w_uq_2 kv_norm_g_2 w_ukv_2 w_oa_2 w_pool_2 pool_scale_2 conv_w_2 w_oc_2 w_out_2 norm2_g_2 w_router_2 "
         "w_gate_2 w_up_2 w_down_2 final_g_2").split()


def kernel(**inputs):
    import concourse.bacc as bacc
    from concourse.bass_utils import run_bass_kernel_spmd

    nc = bacc.Bacc("TRN2", target_bir_lowering=False, num_devices=1)
    arrays, aps = {}, {}
    for name, a in [(n, np.ascontiguousarray(inputs[n])) for n in NAMES] + list(constants().items()):
        arrays[f"in_{name}"] = a
        aps[name] = nc.dram_tensor(f"in_{name}", a.shape, mybir.dt.from_np(a.dtype), kind="ExternalInput").ap()
    out = nc.dram_tensor("out_x", (1, T, D), F32, kind="ExternalOutput").ap()
    program(nc, aps, out)
    r = run_bass_kernel_spmd(nc, [arrays], core_ids=[0])
    return r.results[0]["out_x"]
```
